# Optimizing a Trainium2 kernel written in Bass

```python
import math
import jax, jax.numpy as jnp
from jax import lax
import numpy as np

D_MODEL = 1024
BATCH = 1
SEQ = 128
DEPTH = 2
DEC_BATCH = 1
DEC_SEQ = 512
PAST_LEN = 128

GRID_W = 64
N_EVEN = (DEPTH + 1) // 2
N_ODD = DEPTH // 2
NORM_EPS = 1e-6
GDN_HEADS = 4
GDN_DK = 128
GDN_DV = 128
GDN_CONV_W = 5
GDN_CHUNK = 64
HY_CH = 512
HY_ORDER = 2
HY_CONV_W = 3
HY_EMB = 33
HY_BANDS = (HY_EMB - 1) // 2
HY_FILTER_HIDDEN = 64
HY_DECAY_TARGET = 1e-2
HY_SHORT_DECAY_PCT = 0.3
HY_LONG_DECAY_PCT = 1.5
GQA_HEADS = 4
GQA_KV_HEADS = 2
GQA_HEAD_DIM = 128
MLA_HEADS = 4
MLA_Q_RANK = 256
MLA_KV_RANK = 128
MLA_NOPE_DIM = 128
MLA_ROPE_DIM = 64
MLA_V_DIM = 128
ROPE_THETA = 10000.0
Q_BLOCK = 128

GDN_QK_W = GDN_HEADS * GDN_DK
GDN_W = GDN_HEADS * GDN_DV
EVEN_SPLITS = (GDN_QK_W, GDN_QK_W, GDN_W, 2 * GDN_HEADS, 2 * GDN_HEADS, GDN_W, HY_CH, HY_CH, HY_CH, HY_CH)
EVEN_IN = sum(EVEN_SPLITS)
EVEN_MIX = GDN_W + HY_CH
GQA_W = GQA_HEADS * GQA_HEAD_DIM
GQA_KV_W = GQA_KV_HEADS * GQA_HEAD_DIM
MLA_W = MLA_HEADS * MLA_V_DIM
ODD_SPLITS = (GQA_W, GQA_KV_W, GQA_KV_W, GQA_W, MLA_Q_RANK, MLA_KV_RANK, MLA_ROPE_DIM, MLA_W)
ODD_IN = sum(ODD_SPLITS)
ODD_MIX = GQA_W + MLA_W

kernel_name = 'hybrid_gdn_hyena_gqa_mla_diffusion_step'

def split_cols(z, sizes):
    idx = np.cumsum(np.array(sizes))[:-1].tolist()
    return jnp.split(z, idx, axis=-1)

def rms_norm(x, g):
    xf = x.astype(jnp.float32)
    y = xf * lax.rsqrt(jnp.mean(xf * xf, axis=-1, keepdims=True) + NORM_EPS)
    return (y * g.astype(jnp.float32)).astype(x.dtype)

def l2_normalize(x):
    return x * lax.rsqrt(jnp.sum(x * x, axis=-1, keepdims=True) + NORM_EPS)

def adaln(cond, w, b):
    m = jax.nn.silu(cond) @ w + b
    return jnp.split(m[:, None, :], 3, axis=-1)

def depthwise_conv(x, w):
    width = w.shape[0]
    return lax.conv_general_dilated(x, w[:, None, :].astype(x.dtype), window_strides=(1,),
                                    padding=[(width // 2, width // 2)],
                                    dimension_numbers=('NWC', 'WIO', 'NWC'),
                                    feature_group_count=x.shape[-1])

def grid_positions(n_tokens):
    rows = n_tokens // GRID_W
    row = jnp.broadcast_to(jnp.arange(rows)[:, None], (rows, GRID_W)).reshape(-1)
    col = jnp.broadcast_to(jnp.arange(GRID_W)[None, :], (rows, GRID_W)).reshape(-1)
    return row.astype(jnp.float32), col.astype(jnp.float32)

def rope_1d(x, pos):
    d = x.shape[-1]
    half = d // 2
    inv = ROPE_THETA ** (-jnp.arange(half, dtype=jnp.float32) * 2.0 / d)
    ang = pos[:, None] * inv[None, :]
    cos = jnp.cos(ang)[:, None, :]
    sin = jnp.sin(ang)[:, None, :]
    xf = x.astype(jnp.float32)
    x1, x2 = xf[..., :half], xf[..., half:]
    return jnp.concatenate([x1 * cos - x2 * sin, x1 * sin + x2 * cos], axis=-1).astype(x.dtype)

def axial_rope(x):
    row, col = grid_positions(x.shape[1])
    r = x.shape[-1] // 2
    return jnp.concatenate([rope_1d(x[..., :r], row), rope_1d(x[..., r:], col)], axis=-1)

def block_attention(q, k, v, scale):
    B, Lq, Hkv, G, Dq = q.shape
    nb = Lq // Q_BLOCK
    kf = k.astype(jnp.float32)
    vf = v.astype(jnp.float32)
    qb = q.astype(jnp.float32).reshape(B, nb, Q_BLOCK, Hkv, G, Dq).swapaxes(0, 1)

    def one_block(qblk):
        s = jnp.einsum('bqhgd,bkhd->bhgqk', qblk, kf) * scale
        p = jax.nn.softmax(s, axis=-1)
        return jnp.einsum('bhgqk,bkhe->bqhge', p, vf)

    o = lax.map(one_block, qb)
    return o.swapaxes(0, 1).reshape(B, Lq, -1).astype(v.dtype)

def gdn_chunked(q, k, v, g, beta, s0):
    B, L, H, K = q.shape
    V = v.shape[-1]
    C = GDN_CHUNK
    n = L // C

    def chunks(t):
        return t.reshape((B, n, C, H) + t.shape[3:]).swapaxes(2, 3)

    q = chunks(q * (K ** -0.5))
    k = chunks(k)
    v = chunks(v)
    beta = chunks(beta)
    g = jnp.cumsum(chunks(g), axis=-1)
    kb = k * beta[..., None]
    vb = v * beta[..., None]
    tril = jnp.tril(jnp.ones((C, C), dtype=bool))
    strict = jnp.tril(jnp.ones((C, C), dtype=bool), -1)
    diff = g[..., :, None] - g[..., None, :]
    decay = jnp.where(tril, jnp.exp(jnp.where(tril, diff, 0.0)), 0.0)
    lmat = jnp.where(strict, jnp.einsum('bnhcd,bnhed->bnhce', kb, k) * decay, 0.0)
    a = lmat + jnp.eye(C, dtype=jnp.float32)
    rhs = jnp.concatenate([vb, kb * jnp.exp(g)[..., None]], axis=-1)
    sol = lax.linalg.triangular_solve(a, rhs, left_side=True, lower=True, unit_diagonal=True)
    u, w = sol[..., :V], sol[..., V:]
    intra = jnp.einsum('bnhcd,bnhed->bnhce', q, k) * decay
    qg = q * jnp.exp(g)[..., None]
    kdec = k * jnp.exp(g[..., -1:] - g)[..., None]
    glast = jnp.exp(g[..., -1])
    xs = tuple(t.swapaxes(0, 1) for t in (qg, kdec, u, w, intra, glast))

    def step(S, inp):
        qg_i, kd_i, u_i, w_i, in_i, gl_i = inp
        v_new = u_i - jnp.einsum('bhck,bhkv->bhcv', w_i, S)
        o = jnp.einsum('bhck,bhkv->bhcv', qg_i, S) + jnp.einsum('bhce,bhev->bhcv', in_i, v_new)
        S = S * gl_i[..., None, None] + jnp.einsum('bhck,bhcv->bhkv', kd_i, v_new)
        return S, o

    S, o = lax.scan(step, s0, xs)
    return o.transpose(1, 0, 3, 2, 4).reshape(B, L, H, V), S

def gdn_branch(zq, zk, zv, za, zb, zg, conv_w, a_log, dt_bias, norm_g, s0_f, s0_b):
    B, L, _ = zq.shape
    qkv = jax.nn.silu(depthwise_conv(jnp.concatenate([zq, zk, zv], axis=-1), conv_w).astype(jnp.float32))
    q, k, v = split_cols(qkv, (GDN_QK_W, GDN_QK_W, GDN_W))
    q = l2_normalize(q.reshape(B, L, GDN_HEADS, GDN_DK))
    k = l2_normalize(k.reshape(B, L, GDN_HEADS, GDN_DK))
    v = v.reshape(B, L, GDN_HEADS, GDN_DV)
    g = -jnp.exp(a_log.astype(jnp.float32)) * jax.nn.softplus(
        za.astype(jnp.float32).reshape(B, L, 2, GDN_HEADS) + dt_bias.astype(jnp.float32))
    beta = jax.nn.sigmoid(zb.astype(jnp.float32).reshape(B, L, 2, GDN_HEADS))
    o_f, s_f = gdn_chunked(q, k, v, g[:, :, 0], beta[:, :, 0], s0_f.astype(jnp.float32))
    flip = lambda t: jnp.flip(t, axis=1)
    o_b, s_b = gdn_chunked(flip(q), flip(k), flip(v), flip(g[:, :, 1]), flip(beta[:, :, 1]), s0_b.astype(jnp.float32))
    o = o_f + flip(o_b)
    o = rms_norm(o, norm_g) * jax.nn.silu(zg.astype(jnp.float32).reshape(B, L, GDN_HEADS, GDN_DV))
    return o.reshape(B, L, GDN_W).astype(zq.dtype), s_f, s_b

def hyena_filters(L, w1, b1, w2, b2, w3, sin_freq):
    f32 = jnp.float32
    t = jnp.linspace(0.0, 1.0, L, dtype=f32)[:, None]
    wpos = 2.0 * math.pi * jnp.arange(L, dtype=f32)[:, None] / L
    f = jnp.linspace(1e-4, HY_BANDS - 1, HY_BANDS, dtype=f32)[None, :]
    z = jnp.concatenate([t, jnp.cos(f * wpos), -jnp.sin(f * wpos)], axis=-1)
    sf = sin_freq.astype(f32)
    h = jnp.sin(sf[0] * (z @ w1.astype(f32) + b1.astype(f32)))
    h = jnp.sin(sf[1] * (h @ w2.astype(f32) + b2.astype(f32)))
    h = (h @ w3.astype(f32)).reshape(L, HY_ORDER, 2, HY_CH)
    deltas = jnp.abs(jnp.linspace(math.log(HY_DECAY_TARGET) / HY_LONG_DECAY_PCT,
                                  math.log(HY_DECAY_TARGET) / HY_SHORT_DECAY_PCT, HY_CH, dtype=f32))
    window = jnp.exp(-t * deltas[None, :])
    return h * window[:, None, None, :]

def two_sided_filter(h_fwd, h_bwd):
    zero = jnp.zeros((1, h_fwd.shape[1]), h_fwd.dtype)
    return jnp.concatenate([h_fwd, zero, h_bwd[1:][::-1]], axis=0)

def fft_long_conv(u, filt):
    L = u.shape[1]
    U = jnp.fft.rfft(u, n=2 * L, axis=1)
    Hf = jnp.fft.rfft(filt, n=2 * L, axis=0)
    return jnp.fft.irfft(U * Hf[None], n=2 * L, axis=1)[:, :L]

def hyena_branch(zv, z1, z2, zg, conv_w, conv_b, w1, b1, w2, b2, w3, sin_freq, skip):
    u = depthwise_conv(jnp.concatenate([zv, z1, z2], axis=-1), conv_w) + conv_b
    v, x1, x2 = split_cols(u.astype(jnp.float32), (HY_CH, HY_CH, HY_CH))
    filt = hyena_filters(u.shape[1], w1, b1, w2, b2, w3, sin_freq)
    z = v
    for o, xo in enumerate((x1, x2)):
        fo = two_sided_filter(filt[:, o, 0], filt[:, o, 1])
        z = xo * (fft_long_conv(z, fo) + z * skip[o].astype(jnp.float32))
    return (z * jax.nn.silu(zg.astype(jnp.float32))).astype(zv.dtype)

def even_mixer(h, p, s0_f, s0_b):
    z = h @ p['in_w']
    zq, zk, zv, za, zb, zg, hv, h1, h2, hg = split_cols(z, EVEN_SPLITS)
    oa, s_f, s_b = gdn_branch(zq, zk, zv, za, zb, zg, p['gdn_conv_w'], p['gdn_a_log'], p['gdn_dt_bias'],
                              p['gdn_norm_g'], s0_f, s0_b)
    ob = hyena_branch(hv, h1, h2, hg, p['hy_conv_w'], p['hy_conv_b'], p['hy_w1'], p['hy_b1'], p['hy_w2'],
                      p['hy_b2'], p['hy_w3'], p['hy_freq'], p['hy_skip'])
    y = jnp.concatenate([oa, ob], axis=-1) @ p['out_w']
    return y, s_f, s_b

def mla_expand(ckv, kpe, kv_up):
    B, L, _ = ckv.shape
    kv = (ckv @ kv_up).reshape(B, L, MLA_HEADS, MLA_NOPE_DIM + MLA_V_DIM)
    k_nope, vals = kv[..., :MLA_NOPE_DIM], kv[..., MLA_NOPE_DIM:]
    k_pe = jnp.broadcast_to(kpe[:, :, None, :].astype(k_nope.dtype), (B, L, MLA_HEADS, MLA_ROPE_DIM))
    return jnp.concatenate([k_nope, k_pe], axis=-1), vals

def odd_mixer(h, p, cache):
    B, L, _ = h.shape
    z = h @ p['in_w']
    gq, gk, gv, gg, mq, mkv, mpe, mg = split_cols(z, ODD_SPLITS)
    q = rms_norm(gq.reshape(B, L, GQA_HEADS, GQA_HEAD_DIM), p['q_norm_g'])
    k = rms_norm(gk.reshape(B, L, GQA_KV_HEADS, GQA_HEAD_DIM), p['k_norm_g'])
    v = gv.reshape(B, L, GQA_KV_HEADS, GQA_HEAD_DIM)
    qm = (rms_norm(mq, p['mq_norm_g']) @ p['mq_up']).reshape(B, L, MLA_HEADS, MLA_NOPE_DIM + MLA_ROPE_DIM)
    ckv = rms_norm(mkv, p['mkv_norm_g'])
    qm_nope, qm_pe = qm[..., :MLA_NOPE_DIM], qm[..., MLA_NOPE_DIM:]
    if cache is None:
        q_g, keys_g, vals_g = q, k, v
        km, vm = mla_expand(ckv, mpe, p['mkv_up'])
        new = (k, v, ckv, mpe)
    else:
        ck, cv, cckv, ckpe = cache
        q_g = axial_rope(q)
        keys_g = jnp.concatenate([axial_rope(k), ck.astype(k.dtype)], axis=1)
        vals_g = jnp.concatenate([v, cv.astype(v.dtype)], axis=1)
        qm_pe = axial_rope(qm_pe)
        kl, vl = mla_expand(ckv, axial_rope(mpe[:, :, None, :])[:, :, 0], p['mkv_up'])
        kc, vc = mla_expand(cckv.astype(ckv.dtype), ckpe, p['mkv_up'])
        km = jnp.concatenate([kl, kc], axis=1)
        vm = jnp.concatenate([vl, vc], axis=1)
        new = ()
    group = GQA_HEADS // GQA_KV_HEADS
    o_g = block_attention(q_g.reshape(B, L, GQA_KV_HEADS, group, GQA_HEAD_DIM), keys_g, vals_g,
                          GQA_HEAD_DIM ** -0.5) * jax.nn.silu(gg)
    qm_full = jnp.concatenate([qm_nope, qm_pe.astype(qm_nope.dtype)], axis=-1)[:, :, :, None, :]
    o_m = block_attention(qm_full, km, vm, (MLA_NOPE_DIM + MLA_ROPE_DIM) ** -0.5) * jax.nn.silu(mg)
    y = jnp.concatenate([o_g, o_m], axis=-1) @ p['out_w']
    return y, new

def setup_inputs(seed: int = 0) -> dict:
    key = jax.random.key(seed)
    ks = iter(jax.random.split(key, 48))
    f32 = jnp.float32

    def nrm(shape, s):
        return jax.random.normal(next(ks), shape, f32) * s

    x_prompt = nrm((BATCH, SEQ, D_MODEL), 1.0)
    x_sample = nrm((DEC_BATCH, DEC_SEQ, D_MODEL), 1.0)
    state_gdn_fwd = nrm((DEC_BATCH, N_EVEN, GDN_HEADS, GDN_DK, GDN_DV), 0.5)
    state_gdn_bwd = nrm((DEC_BATCH, N_EVEN, GDN_HEADS, GDN_DK, GDN_DV), 0.5)
    cache_gqa_k = nrm((DEC_BATCH, N_ODD, PAST_LEN, GQA_KV_HEADS, GQA_HEAD_DIM), 1.0)
    cache_gqa_v = nrm((DEC_BATCH, N_ODD, PAST_LEN, GQA_KV_HEADS, GQA_HEAD_DIM), 1.0)
    cache_mla_ckv = nrm((DEC_BATCH, N_ODD, PAST_LEN, MLA_KV_RANK), 1.0)
    cache_mla_kpe = nrm((DEC_BATCH, N_ODD, PAST_LEN, MLA_ROPE_DIM), 1.0)
    c = nrm((DEC_BATCH, D_MODEL), 1.0)
    c_ctx = nrm((D_MODEL,), 1.0)
    mod_w = nrm((DEPTH, D_MODEL, 3 * D_MODEL), D_MODEL ** -0.5)
    mod_b = nrm((DEPTH, 3 * D_MODEL), 0.02)
    pre_norm_g = 1.0 + nrm((DEPTH, D_MODEL), 0.02)
    post_norm_g = 1.0 + nrm((DEPTH, D_MODEL), 0.02)
    even_in_w = nrm((N_EVEN, D_MODEL, EVEN_IN), D_MODEL ** -0.5)
    gdn_conv_w = nrm((N_EVEN, GDN_CONV_W, 2 * GDN_QK_W + GDN_W), GDN_CONV_W ** -0.5)
    gdn_a_log = jnp.log(jax.random.uniform(next(ks), (N_EVEN, 2, GDN_HEADS), f32, 1.0, 16.0))
    dt = jnp.exp(jax.random.uniform(next(ks), (N_EVEN, 2, GDN_HEADS), f32, math.log(1e-3), math.log(1e-1)))
    gdn_dt_bias = dt + jnp.log(-jnp.expm1(-dt))
    gdn_norm_g = 1.0 + nrm((N_EVEN, GDN_DV), 0.02)
    hyena_conv_w = nrm((N_EVEN, HY_CONV_W, 3 * HY_CH), HY_CONV_W ** -0.5)
    hyena_conv_b = nrm((N_EVEN, 3 * HY_CH), 0.02)
    hyena_ffn_w1 = nrm((N_EVEN, HY_EMB, HY_FILTER_HIDDEN), HY_EMB ** -0.5)
    hyena_ffn_b1 = nrm((N_EVEN, HY_FILTER_HIDDEN), 0.02)
    hyena_ffn_w2 = nrm((N_EVEN, HY_FILTER_HIDDEN, HY_FILTER_HIDDEN), HY_FILTER_HIDDEN ** -0.5)
    hyena_ffn_b2 = nrm((N_EVEN, HY_FILTER_HIDDEN), 0.02)
    hyena_ffn_w3 = nrm((N_EVEN, HY_FILTER_HIDDEN, HY_ORDER * 2 * HY_CH), 0.1 * HY_FILTER_HIDDEN ** -0.5)
    hyena_sin_freq = 1.0 + nrm((N_EVEN, 2, HY_FILTER_HIDDEN), 0.02)
    hyena_bias = nrm((N_EVEN, HY_ORDER, HY_CH), 0.5)
    even_out_w = nrm((N_EVEN, EVEN_MIX, D_MODEL), EVEN_MIX ** -0.5)
    odd_in_w = nrm((N_ODD, D_MODEL, ODD_IN), D_MODEL ** -0.5)
    gqa_q_norm_g = 1.0 + nrm((N_ODD, GQA_HEAD_DIM), 0.02)
    gqa_k_norm_g = 1.0 + nrm((N_ODD, GQA_HEAD_DIM), 0.02)
    mla_q_norm_g = 1.0 + nrm((N_ODD, MLA_Q_RANK), 0.02)
    mla_q_up = nrm((N_ODD, MLA_Q_RANK, MLA_HEADS * (MLA_NOPE_DIM + MLA_ROPE_DIM)), MLA_Q_RANK ** -0.5)
    mla_kv_norm_g = 1.0 + nrm((N_ODD, MLA_KV_RANK), 0.02)
    mla_kv_up = nrm((N_ODD, MLA_KV_RANK, MLA_HEADS * (MLA_NOPE_DIM + MLA_V_DIM)), MLA_KV_RANK ** -0.5)
    odd_out_w = nrm((N_ODD, ODD_MIX, D_MODEL), ODD_MIX ** -0.5)
    return {'x_prompt': x_prompt, 'x_sample': x_sample,
            'state_gdn_fwd': state_gdn_fwd, 'state_gdn_bwd': state_gdn_bwd,
            'cache_gqa_k': cache_gqa_k, 'cache_gqa_v': cache_gqa_v,
            'cache_mla_ckv': cache_mla_ckv, 'cache_mla_kpe': cache_mla_kpe,
            'c': c, 'c_ctx': c_ctx, 'mod_w': mod_w, 'mod_b': mod_b,
            'pre_norm_g': pre_norm_g, 'post_norm_g': post_norm_g,
            'even_in_w': even_in_w, 'gdn_conv_w': gdn_conv_w, 'gdn_a_log': gdn_a_log,
            'gdn_dt_bias': gdn_dt_bias, 'gdn_norm_g': gdn_norm_g,
            'hyena_conv_w': hyena_conv_w, 'hyena_conv_b': hyena_conv_b,
            'hyena_ffn_w1': hyena_ffn_w1, 'hyena_ffn_b1': hyena_ffn_b1,
            'hyena_ffn_w2': hyena_ffn_w2, 'hyena_ffn_b2': hyena_ffn_b2,
            'hyena_ffn_w3': hyena_ffn_w3, 'hyena_sin_freq': hyena_sin_freq, 'hyena_bias': hyena_bias,
            'even_out_w': even_out_w, 'odd_in_w': odd_in_w,
            'gqa_q_norm_g': gqa_q_norm_g, 'gqa_k_norm_g': gqa_k_norm_g,
            'mla_q_norm_g': mla_q_norm_g, 'mla_q_up': mla_q_up,
            'mla_kv_norm_g': mla_kv_norm_g, 'mla_kv_up': mla_kv_up, 'odd_out_w': odd_out_w}

def reference(x_prompt, x_sample, state_gdn_fwd, state_gdn_bwd, cache_gqa_k, cache_gqa_v, cache_mla_ckv,
              cache_mla_kpe, c, c_ctx, mod_w, mod_b, pre_norm_g, post_norm_g, even_in_w, gdn_conv_w, gdn_a_log,
              gdn_dt_bias, gdn_norm_g, hyena_conv_w, hyena_conv_b, hyena_ffn_w1, hyena_ffn_b1, hyena_ffn_w2,
              hyena_ffn_b2, hyena_ffn_w3, hyena_sin_freq, hyena_bias, even_out_w, odd_in_w, gqa_q_norm_g,
              gqa_k_norm_g, mla_q_norm_g, mla_q_up, mla_kv_norm_g, mla_kv_up, odd_out_w):
    xp, xs = x_prompt, x_sample
    zero_state = jnp.zeros((x_prompt.shape[0], GDN_HEADS, GDN_DK, GDN_DV), jnp.float32)
    new_f, new_b, new_gk, new_gv, new_ckv, new_kpe = [], [], [], [], [], []
    for i in range(DEPTH):
        j = i // 2
        sh_p, sc_p, gt_p = adaln(c_ctx[None, :], mod_w[i], mod_b[i])
        sh_s, sc_s, gt_s = adaln(c, mod_w[i], mod_b[i])
        hp = rms_norm(xp, pre_norm_g[i]) * (1.0 + sc_p) + sh_p
        hs = rms_norm(xs, pre_norm_g[i]) * (1.0 + sc_s) + sh_s
        if i % 2 == 0:
            p = {'in_w': even_in_w[j], 'gdn_conv_w': gdn_conv_w[j], 'gdn_a_log': gdn_a_log[j],
                 'gdn_dt_bias': gdn_dt_bias[j], 'gdn_norm_g': gdn_norm_g[j],
                 'hy_conv_w': hyena_conv_w[j], 'hy_conv_b': hyena_conv_b[j],
                 'hy_w1': hyena_ffn_w1[j], 'hy_b1': hyena_ffn_b1[j], 'hy_w2': hyena_ffn_w2[j],
                 'hy_b2': hyena_ffn_b2[j], 'hy_w3': hyena_ffn_w3[j], 'hy_freq': hyena_sin_freq[j],
                 'hy_skip': hyena_bias[j], 'out_w': even_out_w[j]}
            yp, sf, sb = even_mixer(hp, p, zero_state, zero_state)
            ys, _, _ = even_mixer(hs, p, state_gdn_fwd[:, j], state_gdn_bwd[:, j])
            new_f.append(sf.astype(x_prompt.dtype))
            new_b.append(sb.astype(x_prompt.dtype))
        else:
            p = {'in_w': odd_in_w[j], 'q_norm_g': gqa_q_norm_g[j], 'k_norm_g': gqa_k_norm_g[j],
                 'mq_norm_g': mla_q_norm_g[j], 'mq_up': mla_q_up[j], 'mkv_norm_g': mla_kv_norm_g[j],
                 'mkv_up': mla_kv_up[j], 'out_w': odd_out_w[j]}
            yp, ctx = odd_mixer(hp, p, None)
            ys, _ = odd_mixer(hs, p, (cache_gqa_k[:, j], cache_gqa_v[:, j], cache_mla_ckv[:, j], cache_mla_kpe[:, j]))
            new_gk.append(ctx[0])
            new_gv.append(ctx[1])
            new_ckv.append(ctx[2])
            new_kpe.append(ctx[3])
        xp = xp + gt_p * rms_norm(yp, post_norm_g[i])
        xs = xs + gt_s * rms_norm(ys, post_norm_g[i])
    new_gdn_fwd = jnp.stack(new_f, axis=1)
    new_gdn_bwd = jnp.stack(new_b, axis=1)
    new_gqa_k = jnp.stack(new_gk, axis=1)
    new_gqa_v = jnp.stack(new_gv, axis=1)
    new_mla_ckv = jnp.stack(new_ckv, axis=1)
    new_mla_kpe = jnp.stack(new_kpe, axis=1)
    return (xp, xs, new_gdn_fwd, new_gdn_bwd, new_gqa_k, new_gqa_v, new_mla_ckv, new_mla_kpe)


_drawn_inputs = setup_inputs


def setup_inputs(seed=0):
    import zlib

    import numpy as np

    out = dict(_drawn_inputs(seed))
    spreads = {}
    factors = {'cache_gqa_k': 2.974,
     'cache_mla_kpe': 4.569,
     'post_norm_g': 3.904,
     'gdn_norm_g': 6.921,
     'hyena_sin_freq': 5.669,
     'gqa_q_norm_g': 8.0,
     'gqa_k_norm_g': 2.775,
     'mla_q_norm_g': 8.0,
     'mla_kv_norm_g': 3.072,
     'hyena_conv_b': 4.13}
    for name, (base, spread) in spreads.items():
        noise = np.random.default_rng([zlib.crc32(name.encode()), seed]).standard_normal(out[name].shape)
        drawn = base * np.exp(spread * noise) if base else spread * noise
        out[name] = __import__('jax').numpy.asarray(drawn.astype(out[name].dtype))
    for name, factor in factors.items():
        out[name] = (out[name] * factor).astype(out[name].dtype)
    return out
```

```python
import math
from contextlib import ExitStack

import numpy as np

import concourse.bass as bass
from concourse import mybir

F32 = mybir.dt.float32
I32 = mybir.dt.int32
ALU = mybir.AluOpType
ACT = mybir.ActivationFunctionType
AXX = mybir.AxisListType.X

P = 128
D = 1024
KD = D // P
LS, LP = 512, 128
NT = (LS + LP) // P
TS = LS // P
TP = TS
TOK = LS + LP
H = 4
CH = 512
EPS = 1e-6
BANKS = 8

Q0, K0, V0, AB0, ZG0, HV0, HX10, HX20, HG0 = 0, 512, 1024, 1536, 1552, 2064, 2576, 3088, 3600
GQ0, GK0, GG0, MQ0, MG0 = 0, 512, 1024, 1536, 1984
RQ, RKV, ROPE = 256, 128, 64
WC = 256
WSLOTS = 3

ZPAD = TOK + 8
CMW = TOK + 4
CMP = LS + 4

INV = 42
MODS = [0, 3, 6, 8, 10, 12]
LEVELS = [2, 4, 8, 16, 32, 64]

FILLS = [("vectors", 2), ("film", 4), ("filt0", 2 * NT), ("filt1", 2 * NT), ("spec0", 12), ("spec1", 12),
         ("mod0", 12), ("hT0", 2 * NT), ("in_hy", 24), ("tr_hy", 2 * NT), ("fft0", 15), ("fft1", 15),
         ("ab", 1), ("in_gd", 24), ("tr_q", NT), ("tr_k", NT), ("tr_v", NT), ("cumsum", 1),
         ("back", 2 * NT), ("inv", NT * INV + 12), ("scan", 10 * NT), ("tr_o", NT),
         ("gate0", 4), ("out0", 4 * NT),
         ("hT1", 2 * NT), ("in_tm", 6 * NT), ("in_g", 12), ("tr_att", 3 * NT + 1),
         ("q_nope", 5), ("q_pe", NT), ("k_nope", 6), ("v_up", NT + 1), ("tr_qpe", NT),
         ("att", 8 * 11 + 2 * 3), ("gate1", 4), ("out1", 4 * NT)]

UNITS = [("sample", 0), ("sample", 1), ("sample", 2), ("sample", 3), ("prompt", 0),
         ("sample", 4), ("sample", 5), ("sample", 6), ("sample", 7), ("prompt", 4)]


def fill_starts(fills):
    start, at = {}, 0
    for name, n in fills:
        start[name] = at
        at += n
    return start


def unit_fills(at):
    table = [None] * len(UNITS)
    order = [("s", 0)]
    for u in range(len(UNITS)):
        order += ([("s", u + 1)] if u + 1 < len(UNITS) else []) + [("t", u), ("p", u)]
    for kind, u in order:
        n = {"s": 5, "t": 5, "p": 1}[kind] if UNITS[u][0] == "sample" else 1
        table[u] = dict(table[u] or {}, **{kind: at})
        at += n
    return table, at


def constants():
    f32 = np.float32
    out = {}
    out["k_ident"] = np.eye(P, dtype=f32)
    e, c = np.arange(P)[:, None], np.arange(P)[None, :]
    out["k_masks"] = np.concatenate([e <= c, e < c, e >= c, e > c], axis=1).astype(f32)
    lvl = []
    for d in range(2):
        first, second = (e, c) if d == 0 else (c, e)
        lvl.append(((first // 2 == second // 2) & (first % 2 == 0) & (second % 2 == 1)).astype(f32))
    for d in range(2):
        for b in LEVELS:
            cols = np.arange(P).reshape(-1, 2, b)[:, d, :].reshape(1, -1)
            rows = np.arange(P)[:, None]
            lvl.append(((rows // (2 * b) == cols // (2 * b)) & ((rows // b) % 2 == 1 - d)).astype(f32))
    out["k_levels"] = np.concatenate(lvl, axis=1)
    for name, n in (("", LS), ("_p", LP)):
        k, t = np.arange(n), np.arange(n)
        ang = 2 * np.pi * ((t[:, None] * k[None, :]) % (2 * n)) / (2 * n)
        alt = 1.0 - 2.0 * (t % 2)
        fc, fs = np.cos(ang), np.sin(ang)
        fs[:, 0] = alt
        out["k_dft" + name] = np.concatenate([fc, fs], axis=1).astype(f32)
        wgt = np.full((n, 1), 2.0 / (2 * n))
        wgt[0] = 1.0 / (2 * n)
        out["k_idft" + name] = np.concatenate([fc.T * wgt, fs.T * wgt], axis=0).astype(f32)
        tt = np.linspace(0.0, 1.0, n, dtype=f32)[:, None]
        wpos = (f32(2.0 * math.pi) * np.arange(n, dtype=f32)[:, None] / f32(n)).astype(f32)
        f = np.linspace(1e-4, 15, 16, dtype=f32)[None, :]
        out["k_pos" + name] = np.ascontiguousarray(
            np.concatenate([tt, np.cos(f * wpos), -np.sin(f * wpos)], axis=-1).astype(f32).T)
        deltas = np.abs(np.linspace(math.log(1e-2) / 1.5, math.log(1e-2) / 0.3, CH, dtype=f32))
        out["k_window" + name] = np.exp(-tt * deltas[None, :]).astype(f32)
    out["k_alt"] = (1.0 - 2.0 * (np.arange(P) % 2)).astype(f32)[:, None]
    pos = np.arange(LS)
    parts = []
    for width in (128, ROPE):
        r = width // 2
        half = r // 2
        inv = (10000.0 ** (-np.arange(half, dtype=f32) * 2.0 / r)).astype(f32)
        cs, sn = [], []
        for where in (pos // 64, pos % 64):
            a = (where.astype(f32)[:, None] * inv[None, :]).astype(f32)
            cs += [np.cos(a), np.cos(a)]
            sn += [-np.sin(a), np.sin(a)]
        parts += cs + sn
    out["k_rope"] = np.concatenate(parts, axis=1).astype(f32)
    return out


def program(nc, a, out, consts):
    start = fill_starts(FILLS)
    ctx = ExitStack()
    with ctx:
        def sb(name, shape, dt=F32):
            return ctx.enter_context(nc.sbuf_tensor(name, shape, dt))

        def sem(name):
            return ctx.enter_context(nc.semaphore(name))

        ps = ctx.enter_context(nc.psum_tensor("ps", [P, BANKS, 512], F32))
        ctx.enter_context(nc.allow_non_contiguous_dma("small parameter vectors"))

        hT = sb("hT", [P, KD, TOK])
        mix = sb("mix", [P, 8, TOK])
        wring = sb("wring", [P, WSLOTS, KD, WC])
        xreg = sb("xreg", [P, 2 * 4 * CMW])
        pad = sb("pad", [P, 2, ZPAD])
        ident = sb("ident", [P, P])
        ones = sb("ones", [P, P])
        masks = sb("masks", [P, 4 * P])
        vec1 = sb("vec1", [P, 99])
        vec2 = sb("vec2", [P, 108])
        modc_l = [sb(f"modc{n}", [P, 24, 2]) for n in range(2)]
        acol_l = [sb(f"acol{n}", [P, KD, 2]) for n in range(2)]
        gcol_l = [sb(f"gcol{n}", [P, KD, 2]) for n in range(2)]
        scond = sb("scond", [P, KD, 2])
        stat = sb("stat", [P, 2, 4 * NT])
        yst = sb("yst", [P, 2, NT])
        ostat = sb("ostat", [P, 2, NT, 8])
        smax = sb("smax", [P, 2, 2, 4])
        ssum = sb("ssum", [P, 2, 2, 4])
        nmax = sb("nmax", [P, 2, 4])
        rsum = sb("rsum", [P, 2, 4])
        phase = sb("phase", [P, 28704])

        def view(at, *shape):
            n = int(np.prod(shape))
            v = phase[:, at:at + n]
            if len(shape) == 1:
                return v
            names = "abcd"[:len(shape)]
            return v.rearrange(f"p ({' '.join(names)}) -> p {' '.join(names)}",
                               **{k: s for k, s in zip(names, shape)})

        x = xreg[:, 0:NT * D].rearrange("p (t d) -> p t d", t=NT)
        cm = xreg[:, :].rearrange("p (s m c) -> p s m c", s=2, m=4)

        dft, idft = view(0, 4, 1024), view(4096, 8, 512)
        dft_p, idft_p = view(8192, 256), view(8448, 2, 128)
        specP = [view(8704 + 6144 * o, NT, 512) for o in range(2)]
        specQ = [view(8704 + 6144 * o + 2560, NT, 512) for o in range(2)]
        specX = [view(8704 + 6144 * o + 5120, 2, 512) for o in range(2)]
        hy_v, hy_x1, hy_x2 = view(20992, NT, 512), view(23552, NT, 512), view(26112, 4, CMW)
        plus = [view(20992, NT, 512), hT[:, 0:4, :].rearrange("p k n -> p (k n)").rearrange("p (t n) -> p t n", t=NT)]
        minus = [view(23552, NT, 512), hT[:, 4:8, :].rearrange("p k n -> p (k n)").rearrange("p (t n) -> p t n", t=NT)]
        mflat = mix[:, :, :].rearrange("p k n -> p (k n)")
        window = mflat[:, 0:NT * 512].rearrange("p (t n) -> p t n", t=NT)
        w3 = mflat[0:64, 2560:2560 + 2048]
        wflat = wring[:, WSLOTS - 1, :, :].rearrange("p k c -> p (k c)")
        rows = view(26120, 256)
        film_w = view(26400, 512)
        h2, turns, turns_f = view(26640, TOK), view(27280, TOK), view(27920, TOK)
        YP = xreg[:, 0:NT * 512].rearrange("p (t n) -> p t n", t=NT)
        YQ = xreg[:, NT * 512:2 * NT * 512].rearrange("p (t n) -> p t n", t=NT)
        pflat = pad[:, :, :].rearrange("p s n -> p (s n)")

        q_tm, k_tm, v_tm = view(0, NT, 512), view(2560, NT, 512), view(5120, NT, 512)
        qT, kT = view(7680, H, TOK), view(10240, H, TOK)
        v_cm = view(12800, 4, CMW)
        Uinv = view(12800, 2 * NT, 512)
        intraT = view(17920, 2 * NT, 512)
        o_acc = view(23040, NT, 512)
        levels = view(25600, 1024)
        abw = view(26624, KD, 16)
        ab = view(26752, NT, 16)
        gsm = view(26832, 14, NT, 8)
        dtb, alog = view(27392, 8), view(27400, 8)
        kd = view(27408, 2, 512)
        xs = xreg[:, :]
        Tinv = xs[:, 0:1024].rearrange("p (d n) -> p d n", d=2)
        LT = xs[:, 1024:2048].rearrange("p (d n) -> p d n", d=2)
        dec = xs[:, 2048:3072].rearrange("p (d n) -> p d n", d=2)
        Xl = xs[:, 3072:3584].rearrange("p (d n) -> p d n", d=2)
        gm = xs[:, 3584:4608].rearrange("p (d n) -> p d n", d=2)
        rr, vn = Tinv, LT
        S = dec
        Sp = gm
        y = view(0, NT, D)
        gb = view(12800, 2, D)
        ys = view(17920, 2, D)

        xn = view(23040, 2, D)
        ztm, v_all = view(0, NT, 5, WC), view(6400, NT + 1, WC)
        rope, g_rows = view(7936, TS, 384), view(9472, 3, P)
        q_up, kv_up = view(9856, 2, 768), view(11392, 1024)
        c_k, c_ckv, c_kpe = view(12416, 2 * P), view(12672, P), view(12800, ROPE)
        oq, ok = view(13056, H, TOK), view(15616, 2, TOK + P)
        mqT, ckvT = view(17152, 2, TOK), view(18432, TOK + P)
        qnT, qpT = view(19200, H, TOK), view(21760, H, TOK)
        qpe, knT = view(24320, NT, WC), view(25600, H, TOK + P)
        hflat = hT[:, :, :].rearrange("p k n -> p (k n)")
        vm, kpT = hflat[:, 0:3072].rearrange("p (t n) -> p t n", t=NT + 1), hflat[:, 3072:3072 + TOK + P]
        prob = [view(0, H, 640), view(2560, H, 640)]
        probT = [view(7936, NT, 512), view(10496, NT, 512)]
        GA, GE, GS, BE, CS, EG, NEG, TOT, KDF, GL, T0, T1, T2, T3 = range(14)

        bank_full = [sem(f"bank_full{b}") for b in range(BANKS)]
        bank_free = [sem(f"bank_free{b}") for b in range(BANKS)]
        w_landed = [sem(f"w_landed{s}") for s in range(WSLOTS)]
        dve_step, act_step, pool_step = sem("dve_step"), sem("act_step"), sem("pool_step")
        rows_in, film_in, dft_in, idft_in, x_in, xback_in, gdn_in, state_in = (sem(n) for n in (
            "rows_in", "film_in", "dft_in", "idft_in", "x_in", "xback_in", "gdn_in", "state_in"))
        const_ok = sem("const_ok")
        vec_ready, arg_ready, sin_ready, scond_ready = (sem(n) for n in (
            "vec_ready", "arg_ready", "sin_ready", "scond_ready"))
        film_ready, taps_ready, skip_in, spec_ready = (sem(n) for n in (
            "film_ready", "taps_ready", "skip_in", "spec_ready"))
        prestat_ready, pad_zero, acol_ready, sq_ready, rstd_ready, xn_ready, hT_ready = (sem(n) for n in (
            "prestat_ready", "pad_zero", "acol_ready", "sq_ready", "rstd_ready", "xn_ready", "hT_ready"))
        gates_ready, pad_ready, conv_ready, cm_ready, tm_ready = (sem(n) for n in (
            "gates_ready", "pad_ready", "conv_ready", "cm_ready", "tm_ready"))
        Y_ready, z1_ready, hy_done = (sem(n) for n in ("Y_ready", "z1_ready", "hy_done"))
        ab_copied, g_chain, g_act, g_ready, gmask_ready, scal_ready = (sem(n) for n in (
            "ab_copied", "g_chain", "g_act", "g_ready", "gmask_ready", "scal_ready"))
        sq2_ready, ss_ready, rinv_ready, normed, back_ready = (sem(n) for n in (
            "sq2_ready", "ss_ready", "rinv_ready", "normed", "back_ready"))
        diff_ready, expd, masked, LT_ready, intra_ready, U1_ready, T_ready, U_ready, X_ready = (sem(n) for n in (
            "diff_ready", "expd", "masked", "LT_ready", "intra_ready", "U1_ready", "T_ready", "U_ready", "X_ready"))
        kd_ready, r_ready, vn_ready, S_ready, o_ready = (sem(n) for n in (
            "kd_ready", "r_ready", "vn_ready", "S_ready", "o_ready"))
        osq_ready, oss_ready, orstd_ready, on_ready, mix_ready = (sem(n) for n in (
            "osq_ready", "oss_ready", "orstd_ready", "on_ready", "mix_ready"))
        odd_in, z_ready, osum_ready, oinv_ready, onorm_ready, qpe_ready, cache_out, max_ready, exp_ready, prob_ready = (
            sem(n) for n in ("odd_in", "z_ready", "osum_ready", "oinv_ready", "onorm_ready", "qpe_ready", "cache_out",
                             "max_ready", "exp_ready", "prob_ready"))
        diag_ready, gb_ready, y_ready, yss_ready, yrstd_ready, ys_ready, x_ready = (sem(n) for n in (
            "diag_ready", "gb_ready", "y_ready", "yss_ready", "yrstd_ready", "ys_ready", "x_ready"))
        stored = sem("stored")

        def inv0(t):
            return start["inv"] + INV * t + MODS[t]

        def mod1(j):
            t = [n for n in range(NT) if MODS[n] <= j < MODS[n + 1]][0]
            return inv0(t) + INV + j - MODS[t]

        def bank(f):
            return ps[:, f % BANKS, :]

        def wait_full(eng, f):
            eng.wait_ge(bank_full[f % BANKS], f // BANKS + 1)

        def wait_free(eng, f):
            if f >= BANKS:
                eng.wait_ge(bank_free[f % BANKS], f // BANKS)

        def wait_drained(eng, f):
            eng.wait_ge(bank_free[f % BANKS], f // BANKS + 1)

        def full(f):
            return bank_full[f % BANKS]

        def free(f):
            return bank_free[f % BANKS]

        def wchunk(i):
            return wring[:, i % WSLOTS, :, :]

        def wait_chunk(eng, i):
            eng.wait_ge(w_landed[i % WSLOTS], 16 * (i // WSLOTS + 1))

        def toks(t):
            return slice(t * P, t * P + P)

        def cols(t):
            return slice(t * P, t * P + P) if t < TS else slice(CMP, CMP + P)

        def halves(ap, b):
            return ap.rearrange("p (h n two b) -> p h n two b", h=H, two=2, b=b)

        def chunk_list():
            lst = []
            mod = a["mod_w"]
            even, odd = a["even_in_w"][0], a["odd_in_w"][0]
            for j in range(12):
                lst.append((mod[0], WC * j, WC, start["mod0"] + j))
            for n, c0 in enumerate((HG0, HV0, HX10, HX20)):
                for j in range(2):
                    lst.append((even, c0 + WC * j, WC, start["in_hy"] + 3 * (2 * n + j) + 2))
            for n, c0 in enumerate((ZG0, Q0, K0, V0)):
                for j in range(2):
                    lst.append((even, c0 + WC * j, WC, start["in_gd"] + 3 * (2 * n + j) + 2))
            for j in range(12):
                lst.append((mod[1], WC * j, WC, mod1(j)))
            for j in range(4):
                lst.append((a["even_out_w"][0], WC * j, WC, start["out0"] + NT * j + NT - 1))
            for n, c0 in enumerate((GQ0, GQ0 + WC, GK0, GK0 + WC, MQ0, MQ0 + WC)):
                lst.append((odd, c0, WC if n < 5 else RKV + ROPE, start["in_tm"] + NT * n + NT - 1))
            for j, c0 in enumerate((GG0, GG0 + WC, MG0, MG0 + WC)):
                lst.append((odd, c0, WC, start["in_g"] + 3 * j + 2))
            for j in range(4):
                lst.append((a["odd_out_w"][0], WC * j, WC, start["out1"] + NT * j + NT - 1))
            return lst

        chunks = chunk_list()
        chunk_of = {}
        for i, ch in enumerate(chunks):
            chunk_of[ch[3]] = i

        units, _ = unit_fills(start["att"])

        block = ctx.enter_context(nc.Block())

        @block.sync
        def _(sp):
            sp.dma_start(ident[:, :], consts["k_ident"]).then_inc(rows_in, 16)
            mb = a["mod_b"].rearrange("l (r c) -> (l r) c", c=P)
            r1, r2 = rows[:, 0:128], rows[:, 128:256]
            sp.dma_start(r1[0:48, :], mb).then_inc(rows_in, 16)
            sp.dma_start(r1[48:64, :], a["pre_norm_g"].rearrange("l (r c) -> (l r) c", c=P)).then_inc(rows_in, 16)
            sp.dma_start(r1[64:80, :], a["post_norm_g"].rearrange("l (r c) -> (l r) c", c=P)).then_inc(rows_in, 16)
            sp.dma_start(r1[80:88, :], a["c"].rearrange("l (r c) -> (l r) c", c=P)).then_inc(rows_in, 16)
            sp.dma_start(r1[88:96, :], a["c_ctx"].rearrange("(r c) -> r c", c=P)).then_inc(rows_in, 16)
            sp.dma_start(r1[96:97, :], a["gdn_norm_g"]).then_inc(rows_in, 16)
            sp.dma_start(r1[97:99, :], a["mla_q_norm_g"].rearrange("l (r c) -> (l r) c", c=P)).then_inc(rows_in, 16)
            sp.dma_start(r2[0:60, :], a["gdn_conv_w"].rearrange("l j (r c) -> (l j r) c", c=P)).then_inc(rows_in, 16)
            sp.dma_start(r2[60:96, :], a["hyena_conv_w"].rearrange("l j (r c) -> (l j r) c", c=P))\
              .then_inc(rows_in, 16)
            sp.dma_start(r2[96:108, :], a["hyena_conv_b"].rearrange("l (r c) -> (l r) c", c=P)).then_inc(rows_in, 16)
            sp.dma_start(film_w[0:33, 0:64], a["hyena_ffn_w1"][0]).then_inc(film_in, 16)
            sp.dma_start(film_w[0:64, 64:128], a["hyena_ffn_w2"][0]).then_inc(film_in, 16)
            for n, v in enumerate((a["hyena_ffn_b1"][0], a["hyena_ffn_b2"][0], a["hyena_sin_freq"][0, 0],
                                   a["hyena_sin_freq"][0, 1])):
                sp.dma_start(film_w[0:64, 128 + n:129 + n], v.rearrange("(c o) -> c o", o=1)).then_inc(film_in, 16)
            sp.dma_start(film_w[:, 132:133], consts["k_alt"]).then_inc(film_in, 16)
            sp.dma_start(wflat[0:33, 0:LS], consts["k_pos"]).then_inc(film_in, 16)
            sp.dma_start(wflat[0:33, LS:TOK], consts["k_pos_p"]).then_inc(film_in, 16)
            sp.dma_start(w3, a["hyena_ffn_w3"][0]).then_inc(film_in, 16)
            sp.dma_start(window[:, 0:TS, :], consts["k_window"].rearrange("(t p) n -> p t n", p=P)).then_inc(film_in, 16)
            sp.dma_start(window[:, TP, :], consts["k_window_p"]).then_inc(film_in, 16)
            sp.dma_start(wflat[0:1, 1024:2048], a["hyena_bias"].rearrange("l o c -> l (o c)")).then_inc(film_in, 16)
            sp.dma_start(dft, consts["k_dft"].rearrange("(t p) n -> p t n", p=P)).then_inc(dft_in, 16)
            sp.dma_start(dft_p, consts["k_dft_p"]).then_inc(dft_in, 16)
            sp.dma_start(x[:, 0:TS, :], a["x_sample"][0].rearrange("(t p) d -> p t d", p=P)).then_inc(x_in, 16)
            sp.dma_start(x[:, TP, :], a["x_prompt"][0]).then_inc(x_in, 16)
            for i, (w, c0, n, last) in enumerate(chunks):
                if i == WSLOTS - 1:
                    sp.wait_ge(taps_ready, 2 * NT)
                if i >= WSLOTS:
                    wait_full(sp, chunks[i - WSLOTS][3])
                sp.dma_start(wchunk(i)[:, :, 0:n], w[:, c0:c0 + n].rearrange("(k p) n -> p k n", p=P))\
                  .then_inc(w_landed[i % WSLOTS], 16)

        @block.gpsimd
        def _(pool):
            steps = [0]

            def chained(ins):
                steps[0] += 1
                ins.then_inc(pool_step, 1)
                pool.wait_ge(pool_step, steps[0])

            nc.gpsimd.memset(ones[:, :], 1.0).then_inc(const_ok, 1)
            pool.dma_start(idft, consts["k_idft"].rearrange("(t p) n -> p t n", p=P)).then_inc(idft_in, 16)
            pool.dma_start(idft_p, consts["k_idft_p"].rearrange("(t p) n -> p t n", p=P)).then_inc(idft_in, 16)
            pool.dma_start(masks[:, :], consts["k_masks"]).then_inc(idft_in, 16)

            wait_full(pool, start["fft1"] + 14)
            pool.wait_ge(hy_done, 5)
            pool.dma_start(levels, consts["k_levels"]).then_inc(gdn_in, 16)
            pool.dma_start(abw, a["even_in_w"][0][:, AB0:AB0 + 16].rearrange("(k p) n -> p k n", p=P))\
                .then_inc(gdn_in, 16)
            pool.dma_start(dtb, a["gdn_dt_bias"].rearrange("l a b -> l (a b)").broadcast_to([P, 8])).then_inc(gdn_in, 16)
            pool.dma_start(alog, a["gdn_a_log"].rearrange("l a b -> l (a b)").broadcast_to([P, 8])).then_inc(gdn_in, 16)
            nc.gpsimd.memset(o_acc, 0.0).then_inc(gmask_ready, 1)

            for t in range(NT):
                for d in range(2):
                    n = 2 * t + d
                    if n == 0:
                        pool.wait_ge(g_ready, 1)
                        wait_full(pool, start["tr_v"] + NT - 1)
                        pool.wait_ge(idft_in, 48)
                        pool.wait_ge(gdn_in, 64)
                    if t >= 1:
                        wait_full(pool, inv0(t - 1) + 3)
                    nc.gpsimd.tensor_tensor(
                        gm[:, d, :].rearrange("p (h c) -> p h c", h=H),
                        masks[:, 2 * d * P:2 * d * P + P].unsqueeze(1).broadcast_to([P, H, P]),
                        gsm[:, GE, t, 4 * d:4 * d + 4].unsqueeze(2).broadcast_to([P, H, P]),
                        ALU.mult).then_inc(gmask_ready, 1)
                for d in range(2):
                    n = 2 * t + d
                    pool.wait_ge(expd, n + 1)
                    m_incl = masks[:, 2 * d * P:2 * d * P + P].unsqueeze(1).broadcast_to([P, H, P])
                    m_strict = masks[:, (2 * d + 1) * P:(2 * d + 2) * P].unsqueeze(1).broadcast_to([P, H, P])
                    dv = dec[:, d, :].rearrange("p (h c) -> p h c", h=H)
                    nc.gpsimd.tensor_tensor(intraT[:, n, :].rearrange("p (h c) -> p h c", h=H), dv, m_incl,
                                            ALU.mult).then_inc(masked, 1)
                    nc.gpsimd.tensor_tensor(dv, dv, m_strict, ALU.mult).then_inc(masked, 1)
                for d in range(2):
                    n = 2 * t + d
                    if d == 0:
                        pool.wait_ge(LT_ready, t + 1)
                    else:
                        wait_drained(pool, inv0(t))
                    m0 = levels[:, d * P:d * P + P].unsqueeze(1).broadcast_to([P, H, P])
                    Uv = Uinv[:, n, :].rearrange("p (h c) -> p h c", h=H)
                    chained(nc.gpsimd.tensor_tensor(Uv, LT[:, d, :].rearrange("p (h c) -> p h c", h=H), m0, ALU.mult))
                    nc.gpsimd.tensor_tensor(Uv, ident[:, :].unsqueeze(1).broadcast_to([P, H, P]), Uv,
                                            ALU.subtract).then_inc(U1_ready, 1)
            for s in range(NT):
                for d in range(2):
                    n = 2 * s + d
                    t = s if d == 0 or s == TP else TS - 1 - s
                    if s >= 1:
                        wait_full(pool, start["scan"] + 10 * (s - 1) + 6 + d)
                    elif d == 0:
                        pool.wait_ge(normed, 2 * NT)
                        pool.wait_ge(g_act, 2)
                    nc.gpsimd.tensor_tensor(kd[:, d, :].rearrange("p (h c) -> p h c", h=H),
                                            k_tm[:, t, :].rearrange("p (h c) -> p h c", h=H),
                                            gsm[:, KDF, t, 4 * d:4 * d + 4].unsqueeze(2).broadcast_to([P, H, P]),
                                            ALU.mult).then_inc(kd_ready, 1)
            wait_drained(pool, start["scan"] + 10 * NT - 1)
            for n, nm in enumerate(("new_gdn_fwd", "new_gdn_bwd")):
                pool.dma_start(out[nm][0, 0].rearrange("h k v -> k h v"),
                               Sp[:, n, :].rearrange("p (h v) -> p h v", h=H)).then_inc(stored, 16)

            def gate_diagonals(layer):
                for n in range(2 * KD):
                    nc.gpsimd.tensor_tensor(view(19968, 16, P)[:, n, :], ident[:, :],
                                            gcol_l[layer][:, n % KD, n // KD:n // KD + 1].broadcast_to([P, P]),
                                            ALU.mult).then_inc(diag_ready, 1)

            gate_diagonals(0)
            pool.wait_ge(stored, 32)
            pool.dma_start(x[:, 0:TS, :], a["x_sample"][0].rearrange("(t p) d -> p t d", p=P)).then_inc(xback_in, 16)
            pool.dma_start(x[:, TP, :], a["x_prompt"][0]).then_inc(xback_in, 16)
            pool.wait_ge(xback_in, 32)
            for t in range(NT):
                pool.wait_ge(ys_ready, t + 1)
                nc.gpsimd.tensor_tensor(x[:, t, :], x[:, t, :], ys[:, t % 2, :], ALU.add).then_inc(x_ready, 1)

            pool.wait_ge(ys_ready, NT)
            pool.dma_start(v_all[:, NT, :], a["cache_gqa_v"][0, 0].rearrange("t h d -> t (h d)")).then_inc(odd_in, 16)
            pool.dma_start(rope, consts["k_rope"].rearrange("(t p) n -> p t n", p=P)).then_inc(odd_in, 16)
            for n, nm in enumerate(("gqa_q_norm_g", "gqa_k_norm_g", "mla_kv_norm_g")):
                pool.dma_start(g_rows[:, n, :], a[nm].broadcast_to([P, P])).then_inc(odd_in, 16)
            pool.dma_start(q_up, a["mla_q_up"][0].rearrange("(k p) n -> p k n", p=P)).then_inc(odd_in, 16)
            pool.dma_start(kv_up, a["mla_kv_up"][0]).then_inc(odd_in, 16)
            pool.dma_start(c_k, a["cache_gqa_k"][0, 0].rearrange("t h d -> t (h d)")).then_inc(odd_in, 16)
            pool.dma_start(c_ckv, a["cache_mla_ckv"][0, 0]).then_inc(odd_in, 16)
            pool.dma_start(c_kpe, a["cache_mla_kpe"][0, 0]).then_inc(odd_in, 16)
            pool.wait_ge(onorm_ready, NT)
            wait_drained(pool, start["in_tm"] + 6 * NT - 1)
            pool.dma_start(out["new_gqa_k"][0, 0].rearrange("t h d -> t (h d)"), ztm[:, TP, 2, :]).then_inc(stored, 16)
            pool.dma_start(out["new_gqa_v"][0, 0].rearrange("t h d -> t (h d)"), v_all[:, TP, :]).then_inc(stored, 16)
            pool.dma_start(out["new_mla_ckv"][0, 0], ztm[:, TP, 4, 0:RKV]).then_inc(stored, 16)
            pool.dma_start(out["new_mla_kpe"][0, 0], ztm[:, TP, 4, RKV:RKV + ROPE]).then_inc(stored, 16)
            pool.wait_ge(stored, 96)
            nc.gpsimd.memset(rsum[:, :, :], 0.0).then_inc(cache_out, 1)
            for u, (kind, h) in enumerate(UNITS):
                pool.wait_ge(exp_ready, u + 1)
                width = 640 if kind == "sample" else P
                for g in range(4):
                    nc.gpsimd.tensor_tensor(prob[u % 2][:, g, 0:width], prob[u % 2][:, g, 0:width],
                                            rsum[:, u % 2, g:g + 1].broadcast_to([P, width]), ALU.mult)\
                        .then_inc(prob_ready, 1)
            wait_full(pool, units[-1]["p"])
            gate_diagonals(1)
            for t in range(NT):
                pool.wait_ge(ys_ready, NT + t + 1)
                nc.gpsimd.tensor_tensor(x[:, t, :], x[:, t, :], ys[:, t % 2, :], ALU.add).then_inc(x_ready, 1)
                pool.wait_ge(x_ready, NT + t + 1)
                dst = out["y_sample"][0, toks(t), :] if t < TS else out["y_prompt"][0]
                pool.dma_start(dst, x[:, t, :]).then_inc(stored, 16)
            pool.wait_ge(stored, 96 + 16 * NT)

        @block.scalar
        def _(act):
            steps = [0]

            def chained(ins):
                steps[0] += 1
                ins.then_inc(act_step, 1)
                act.wait_ge(act_step, steps[0])

            wait_full(act, start["vectors"])
            nc.scalar.activation(vec1[:, :], bank(start["vectors"])[:, 0:99], ACT.Copy).then_inc(free(0), 1)
            wait_full(act, start["vectors"] + 1)
            nc.scalar.activation(vec2[:, :], bank(start["vectors"] + 1)[:, 0:108], ACT.Copy).then_inc(free(1), 1)
            act.wait_ge(bank_free[1], 1)
            nc.scalar.activation(scond[:, :, 0], vec1[:, 80:88], ACT.Silu).then_inc(scond_ready, 1)
            nc.scalar.activation(scond[:, :, 1], vec1[:, 88:96], ACT.Silu).then_inc(scond_ready, 1)
            for layer in range(2):
                act.wait_ge(arg_ready, layer + 1)
                nc.scalar.activation(h2[0:64, :], h2[0:64, :], ACT.Sin).then_inc(sin_ready, 1)
            for o in range(2):
                f0 = start[f"spec{o}"]
                for j in range(12):
                    f = f0 + j
                    wait_full(act, f)
                    if j < 10:
                        dst = (specP if j % 2 == 0 else specQ)[o][:, j // 2, :]
                        src = bank(f)
                        nc.scalar.activation(dst, src, ACT.Copy).then_inc(free(f), 1)
                    else:
                        act.wait_ge(free(f0 + 8 * (j - 10)), (f0 + 8 * (j - 10)) // BANKS + 1)
                        act.wait_ge(free(f0 + 8 * (j - 10) + 1), (f0 + 8 * (j - 10) + 1) // BANKS + 1)
                        t = 0 if j == 10 else TP
                        chained(nc.scalar.activation(specX[o][:, j - 10, :], specP[o][:, t, :], ACT.Copy))
                        nc.scalar.mul(specQ[o][0:1, t, :], specQ[o][0:1, t, :], 0.0)
                        nc.scalar.activation(specX[o][0:1, j - 10, :], bank(f)[0:1, :], ACT.Copy).then_inc(free(f), 1)
            def pre_norm(layer):
                for t in range(NT):
                    if layer == 0:
                        act.wait_ge(x_in, 32)
                    else:
                        act.wait_ge(x_ready, t + 1)
                    if t >= 1:
                        act.wait_ge(sq_ready, NT * layer + t)
                    nc.scalar.activation(pflat[:, 0:1024], x[:, t, :], ACT.Square,
                                         accum_out=stat[:, 0, t:t + 1]).then_inc(sq_ready, 1)
                act.wait_ge(prestat_ready, layer + 1)
                chained(nc.scalar.activation(stat[:, 1, 0:NT], stat[:, 0, 0:NT], ACT.Ln))
                nc.scalar.activation(stat[:, 1, 0:NT], stat[:, 1, 0:NT], ACT.Exp, scale=-0.5).then_inc(rstd_ready, 1)

            pre_norm(0)
            def modulate_x(base, layer):
                for t in range(NT):
                    for g in range(2):
                        f = base + 2 * t + g
                        wait_full(act, f)
                        if t == 0 and g == 0:
                            act.wait_ge(acol_ready, 2 * layer + 2)
                        for k in range(4 * g, 4 * g + 4):
                            c = 0 if t < TS else 1
                            ins = nc.scalar.activation(hT[:, k, toks(t)], bank(f)[:, (k % 4) * P:(k % 4) * P + P],
                                                       ACT.Identity, bias=modc_l[layer][:, k, c:c + 1],
                                                       scale=acol_l[layer][:, k, c:c + 1])
                        ins.then_inc(free(f), 1)

            modulate_x(start["hT0"], 0)
            npad = 0

            def take_gates(f, m0):
                for m in range(2):
                    wait_full(act, f + m)
                    nc.scalar.activation(mix[:, m0 + m, 0:LS], bank(f + m), ACT.Silu).then_inc(free(f + m), 1)
                wait_full(act, f + 2)
                nc.scalar.activation(mix[:, m0:m0 + 2, LS:TOK],
                                     bank(f + 2)[:, 0:2 * P].rearrange("p (m n) -> p m n", m=2), ACT.Silu)\
                    .then_inc(free(f + 2), 1)

            def take_rows(f, n):
                if n == 6:
                    act.wait_ge(pad_zero, 2)
                if n >= 1:
                    act.wait_ge(conv_ready, 2 * n)
                else:
                    act.wait_ge(pad_zero, 1)
                for m in range(2):
                    wait_full(act, f + m)
                    nc.scalar.activation(pad[:, m, 2:2 + LS], bank(f + m), ACT.Copy).then_inc(free(f + m), 1)
                wait_full(act, f + 2)
                nc.scalar.activation(pad[:, :, LS + 6:LS + 6 + LP],
                                     bank(f + 2)[:, 0:2 * P].rearrange("p (m n) -> p m n", m=2), ACT.Copy)\
                    .then_inc(free(f + 2), 1)

            for j in range(2):
                take_gates(start["in_hy"] + 3 * j, 4 + 2 * j)
            for j in range(6):
                take_rows(start["in_hy"] + 6 + 3 * j, j)
            for j in range(2):
                take_gates(start["in_gd"] + 3 * j, 2 * j)

            def silu_rows(dst, n):
                for m in range(4):
                    act.wait_ge(conv_ready, n + m + 1)
                    nc.scalar.activation(dst[:, m, :], dst[:, m, :], ACT.Silu).then_inc(cm_ready, 1)

            def take_tm(dst, base, square):
                for t in range(NT):
                    f = base + t
                    wait_full(act, f)
                    if square is not None:
                        nc.scalar.activation(dst[:, t, :], bank(f), ACT.Copy).then_inc(tm_ready, 1)
                        if square + t >= 1:
                            act.wait_ge(ss_ready, square + t)
                        nc.scalar.activation(pflat[:, 0:512], bank(f), ACT.Square).then_inc(free(f), 1)
                    else:
                        nc.scalar.activation(dst[:, t, :], bank(f), ACT.Copy).then_inc(free(f), 1)

            for n, dst in enumerate((cm[:, 0, :, :], cm[:, 1, :, :], v_cm)):
                for j in range(2):
                    take_rows(start["in_gd"] + 6 + 3 * (2 * n + j), 6 + 2 * n + j)
                silu_rows(dst, 12 + 4 * n)
            take_tm(q_tm, start["tr_q"], 0)
            take_tm(k_tm, start["tr_k"], NT)
            take_tm(v_tm, start["tr_v"], None)
            act.wait_ge(ss_ready, 2 * NT + 1)
            chained(nc.scalar.activation(stat[:, 1, :], stat[:, 0, :], ACT.Ln, scale=float(P)))
            chained(nc.scalar.activation(gsm[:, T3, :, 0:4], gsm[:, T3, :, 0:4], ACT.Ln))
            chained(nc.scalar.activation(stat[:, 1, :], stat[:, 1, :], ACT.Exp, scale=-0.5))
            nc.scalar.activation(gsm[:, T3, :, 0:4], gsm[:, T3, :, 0:4], ACT.Exp, scale=-0.5).then_inc(rinv_ready, 1)
            act.wait_ge(g_chain, 1)
            chained(nc.scalar.activation(gsm[:, T1, :, :], gsm[:, T1, :, :], ACT.Exp))
            nc.scalar.activation(gsm[:, T1, :, :], gsm[:, T1, :, :], ACT.Ln, bias=1.0)
            nc.scalar.activation(alog, alog, ACT.Exp)
            nc.scalar.activation(gsm[:, BE, :, :], ab[:, :, 8:16], ACT.Exp, scale=-1.0).then_inc(g_act, 1)
            act.wait_ge(scal_ready, 1)
            nc.scalar.activation(gsm[:, EG, :, :], gsm[:, CS, :, :], ACT.Exp)
            nc.scalar.activation(gsm[:, GL, :, :], gsm[:, TOT, :, :], ACT.Exp)
            nc.scalar.activation(gsm[:, KDF, :, :], gsm[:, KDF, :, :], ACT.Exp).then_inc(g_act, 1)
            for t in range(NT):
                for n, dst in enumerate((qT, kT)):
                    f = start["back"] + 2 * t + n
                    wait_full(act, f)
                    nc.scalar.activation(dst[:, :, toks(t)], bank(f).rearrange("p (h c) -> p h c", h=H), ACT.Copy)\
                        .then_inc(free(f), 1)
            for t in range(NT):
                f0 = inv0(t)
                for d in range(2):
                    wait_drained(act, f0 + 2 + d)
                    nc.scalar.activation(dec[:, d, :], dec[:, d, :], ACT.Exp).then_inc(expd, 1)
                for d in range(2):
                    f = f0 + 4 + d
                    wait_full(act, f)
                    nc.scalar.activation(Tinv[:, d, :], bank(f), ACT.Copy).then_inc(free(f), 1)
                for l in range(len(LEVELS)):
                    for d in range(2):
                        f = f0 + 6 + 6 * l + 4 + d
                        wait_full(act, f)
                        nc.scalar.activation(Uinv[:, 2 * t + d, :], bank(f), ACT.Copy).then_inc(free(f), 1)
            wait_drained(act, inv0(NT - 1) + INV - 1)
            wait_drained(act, inv0(NT - 1))
            for d, nm in enumerate(("state_gdn_fwd", "state_gdn_bwd")):
                act.dma_start(S[:, d, :].rearrange("p (h v) -> p h v", h=H),
                              a[nm][0, 0].rearrange("h k v -> k h v")).then_inc(state_in, 16)
            for t in range(NT):
                if t >= 1:
                    act.wait_ge(oss_ready, t)
                else:
                    wait_drained(act, start["scan"] + 10 * NT - 1)
                nc.scalar.activation(kd[:, 0, :], o_acc[:, t, :], ACT.Square).then_inc(osq_ready, 1)
            act.wait_ge(oss_ready, NT + 1)
            chained(nc.scalar.activation(stat[:, 1, :], stat[:, 0, :], ACT.Ln))
            nc.scalar.activation(stat[:, 1, :], stat[:, 1, :], ACT.Exp, scale=-0.5).then_inc(orstd_ready, 1)

            def post_norm(layer):
                for n in range(4):
                    f = start[f"gate{layer}"] + n
                    wait_full(act, f)
                    nc.scalar.activation(gb[:, n // 2, (n % 2) * 512:(n % 2) * 512 + 512], bank(f), ACT.Copy)\
                        .then_inc(free(f), 1)
                for j in range(4):
                    for t in range(NT):
                        f = start[f"out{layer}"] + NT * j + t
                        wait_full(act, f)
                        nc.scalar.activation(y[:, t, WC * j:WC * j + WC], bank(f)[:, 0:WC], ACT.Copy)\
                            .then_inc(free(f), 1)
                for t in range(NT):
                    wait_drained(act, start[f"out{layer}"] + 3 * NT + t)
                    if t >= 1:
                        act.wait_ge(yss_ready, NT * layer + t)
                    nc.scalar.activation(pflat[:, 0:D], y[:, t, :], ACT.Square,
                                         accum_out=yst[:, 0, t:t + 1]).then_inc(yss_ready, 1)
                act.wait_ge(yrstd_ready, 2 * layer + 1)
                chained(nc.scalar.activation(yst[:, 1, :], yst[:, 0, :], ACT.Ln))
                nc.scalar.activation(yst[:, 1, :], yst[:, 1, :], ACT.Exp, scale=-0.5).then_inc(yrstd_ready, 1)

            post_norm(0)

            pre_norm(1)
            modulate_x(start["hT1"], 1)
            for j in range(6):
                for t in range(NT):
                    f = start["in_tm"] + NT * j + t
                    n = WC if j < 5 else RKV + ROPE
                    dst = v_all[:, t, :] if j == 3 else ztm[:, t, j - (j > 3), 0:n]
                    wait_full(act, f)
                    nc.scalar.activation(dst, bank(f)[:, 0:n], ACT.Copy).then_inc(free(f), 1)
            wait_drained(act, start["in_tm"] + 6 * NT - 1)
            for t in range(NT):
                z = ztm[:, t, :, :].rearrange("p j c -> p (j c)")
                for n in range(8):
                    lo, w = [(0, P), (P, P), (2 * P, P), (3 * P, P), (4 * P, P), (5 * P, P), (8 * P, P), (6 * P, 2 * P)][n]
                    if n == 0 and t >= 1:
                        act.wait_ge(z_ready, 8 * t)
                    nc.scalar.activation(pflat[:, lo:lo + w], z[:, lo:lo + w], ACT.Square,
                                         accum_out=ostat[:, 0, t, n:n + 1]).then_inc(z_ready, 1)
            act.wait_ge(osum_ready, 1)
            chained(nc.scalar.activation(ostat[:, 1, :, :], ostat[:, 0, :, :], ACT.Ln))
            nc.scalar.activation(ostat[:, 1, :, :], ostat[:, 1, :, :], ACT.Exp, scale=-0.5).then_inc(oinv_ready, 1)
            for j in range(4):
                take_gates(start["in_g"] + 3 * j, 2 * j)
            for t in range(NT + 1):
                f = start["tr_att"] + 3 * t
                if t < NT:
                    wait_full(act, f)
                    nc.scalar.activation(oq[:, :, toks(t)], bank(f).rearrange("p (h c) -> p h c", h=H), ACT.Copy)\
                        .then_inc(free(f), 1)
                    f += 1
                    wait_full(act, f)
                    nc.scalar.activation(ok[:, :, toks(t)], bank(f)[:, 0:2 * P].rearrange("p (h c) -> p h c", h=2),
                                         ACT.Copy)
                    for k in range(2):
                        ins = nc.scalar.activation(mqT[:, k, toks(t)], bank(f)[:, (2 + k) * P:(3 + k) * P], ACT.Copy,
                                                   scale=vec1[:, 97 + k:98 + k])
                    ins.then_inc(free(f), 1)
                    f += 1
                    wait_full(act, f)
                    nc.scalar.activation(ckvT[:, toks(t)], bank(f)[:, 0:P], ACT.Copy)
                    nc.scalar.activation(kpT[0:ROPE, toks(t)], bank(f)[0:ROPE, P:2 * P], ACT.Copy).then_inc(free(f), 1)
                else:
                    wait_full(act, f)
                    nc.scalar.activation(ok[:, :, toks(t)], bank(f)[:, 0:2 * P].rearrange("p (h c) -> p h c", h=2),
                                         ACT.Copy)
                    nc.scalar.activation(ckvT[:, toks(t)], bank(f)[:, 2 * P:3 * P], ACT.Copy)
                    nc.scalar.activation(kpT[0:ROPE, toks(t)], bank(f)[0:ROPE, 3 * P:4 * P], ACT.Copy)\
                        .then_inc(free(f), 1)
            for n, dst in ((0, qnT),):
                for h in range(H):
                    f = start["q_nope"] + h
                    wait_full(act, f)
                    nc.scalar.activation(dst[:, h, 0:LS], bank(f), ACT.Copy).then_inc(free(f), 1)
                f = start["q_nope"] + H
                wait_full(act, f)
                nc.scalar.activation(dst[:, :, LS:TOK], bank(f).rearrange("p (h c) -> p h c", h=H), ACT.Copy)\
                    .then_inc(free(f), 1)
            for t in range(NT):
                f = start["q_pe"] + t
                wait_full(act, f)
                nc.scalar.activation(qpe[:, t, :], bank(f)[:, 0:WC], ACT.Copy).then_inc(free(f), 1)
            for h in range(H):
                f = start["k_nope"] + h
                wait_full(act, f)
                nc.scalar.activation(knT[:, h, 0:LS], bank(f), ACT.Copy).then_inc(free(f), 1)
            for g in range(2):
                f = start["k_nope"] + H + g
                wait_full(act, f)
                nc.scalar.activation(knT[:, 2 * g:2 * g + 2, LS:TOK + P],
                                     bank(f).rearrange("p (h c) -> p h c", h=2), ACT.Copy).then_inc(free(f), 1)
            for t in range(NT + 1):
                f = start["v_up"] + t
                wait_full(act, f)
                nc.scalar.activation(vm[:, t, :], bank(f), ACT.Copy).then_inc(free(f), 1)
            for t in range(NT):
                f = start["tr_qpe"] + t
                wait_full(act, f)
                nc.scalar.activation(qpT[0:ROPE, :, toks(t)], bank(f)[0:ROPE, :].rearrange("p (h c) -> p h c", h=H),
                                     ACT.Copy).then_inc(free(f), 1)
            def exponentials(u):
                kind, h = UNITS[u]
                scale = (P if h < 4 else P + ROPE) ** -0.5
                f = units[u]["s"]
                act.wait_ge(max_ready, u + 1)
                if u >= 2:
                    wait_full(act, units[u - 2]["p"])
                else:
                    act.wait_ge(cache_out, 1)
                for g in range(4):
                    if kind == "sample":
                        ins = nc.scalar.activation(prob[u % 2][:, g, 0:LS], bank(f + g), ACT.Exp, scale=scale,
                                                   bias=nmax[:, u % 2, g:g + 1], accum_out=ssum[:, u % 2, 0, g:g + 1])
                        ins.then_inc(free(f + g), 1)
                    src = bank(f + 4) if kind == "sample" else bank(f)
                    ins = nc.scalar.activation(prob[u % 2][:, g, LS:640] if kind == "sample" else prob[u % 2][:, g, 0:P],
                                               src[:, g * P:g * P + P], ACT.Exp, scale=scale,
                                               bias=nmax[:, u % 2, g:g + 1], accum_out=ssum[:, u % 2, 1, g:g + 1])
                ins.then_inc(free(f + 4 if kind == "sample" else f), 1)

            def take_probT(u):
                kind, h = UNITS[u]
                for k in range(5 if kind == "sample" else 1):
                    f = units[u]["t"] + k
                    wait_full(act, f)
                    nc.scalar.activation(probT[u % 2][:, k, :], bank(f), ACT.Copy).then_inc(free(f), 1)

            exponentials(0)
            for u in range(len(UNITS)):
                if u + 1 < len(UNITS):
                    exponentials(u + 1)
                take_probT(u)
            post_norm(1)


        @block.tensor
        def _(pe):
            def mm(o, l, r, first=True, last=True):
                return nc.tensor.matmul(o, l, r, start=first, stop=last)

            idn = ident[:, :]
            pe.wait_ge(rows_in, 16 * 11)
            f = start["vectors"]
            nc.tensor.transpose(bank(f)[:, 0:99], rows[0:99, 0:128], ident[0:99, 0:99]).then_inc(full(f), 1)
            nc.tensor.transpose(bank(f + 1)[:, 0:108], rows[0:108, 128:256], ident[0:108, 0:108])\
                .then_inc(full(f + 1), 1)
            pe.wait_ge(film_in, 16 * 13)
            f = start["film"]
            mm(bank(f)[0:64, 0:LS], film_w[0:33, 0:64], wflat[0:33, 0:LS]).then_inc(full(f), 1)
            mm(bank(f + 1)[0:64, 0:LP], film_w[0:33, 0:64], wflat[0:33, LS:TOK]).then_inc(full(f + 1), 1)
            pe.wait_ge(sin_ready, 1)
            mm(bank(f + 2)[0:64, 0:LS], film_w[0:64, 64:128], h2[0:64, 0:LS]).then_inc(full(f + 2), 1)
            mm(bank(f + 3)[0:64, 0:LP], film_w[0:64, 64:128], h2[0:64, LS:TOK]).then_inc(full(f + 3), 1)
            pe.wait_ge(sin_ready, 2)
            for o in range(2):
                for t in range(NT):
                    for s in range(2):
                        f = start[f"filt{o}"] + 2 * t + s
                        wait_free(pe, f)
                        mm(bank(f), h2[0:64, toks(t)], w3[:, (2 * o + s) * CH:(2 * o + s + 1) * CH])\
                            .then_inc(full(f), 1)
            pe.wait_ge(dft_in, 32)
            for o in range(2):
                f = start[f"spec{o}"]
                pe.wait_ge(taps_ready, NT * (o + 1))
                for ft in range(TS):
                    for s, taps in enumerate((plus[o], minus[o])):
                        wait_free(pe, f)
                        for k in range(TS):
                            ins = mm(bank(f), dft[:, k, s * 512 + ft * P:s * 512 + ft * P + P], taps[:, k, :],
                                     k == 0, k == TS - 1)
                        ins.then_inc(full(f), 1)
                        f += 1
                for s, taps in enumerate((plus[o], minus[o])):
                    wait_free(pe, f)
                    mm(bank(f), dft_p[:, s * P:s * P + P], taps[:, TP, :]).then_inc(full(f), 1)
                    f += 1
                wait_free(pe, f)
                for k in range(TS):
                    ins = mm(bank(f)[0:1, :], film_w[:, 132:133], plus[o][:, k, :], k == 0, k == TS - 1)
                ins.then_inc(full(f), 1)
                wait_free(pe, f + 1)
                mm(bank(f + 1)[0:1, :], film_w[:, 132:133], plus[o][:, TP, :]).then_inc(full(f + 1), 1)

            def modulation(j, f):
                i = chunk_of[f]
                wait_chunk(pe, i)
                wait_free(pe, f)
                for m in range(2):
                    for k in range(KD):
                        ins = mm(bank(f)[:, 2 * m:2 * m + 2], wchunk(i)[:, k, m * P:m * P + P], scond[:, k, :],
                                 k == 0, k == KD - 1)
                ins.then_inc(full(f), 1)

            def turn_x(base, before, src):
                for t in range(NT):
                    pe.wait_ge(xn_ready, before + t + 1)
                    for g in range(2):
                        f = base + 2 * t + g
                        wait_free(pe, f)
                        for k in range(4):
                            ins = nc.tensor.transpose(bank(f)[:, k * P:k * P + P],
                                                      src(t)[:, (4 * g + k) * P:(4 * g + k + 1) * P], idn)
                        ins.then_inc(full(f), 1)

            def project_cm(f, i):
                wait_chunk(pe, i)
                w = wchunk(i)
                for m in range(2):
                    wait_free(pe, f + m)
                    for k in range(KD):
                        ins = mm(bank(f + m), w[:, k, m * P:m * P + P], hT[:, k, 0:LS], k == 0, k == KD - 1)
                    ins.then_inc(full(f + m), 1)
                wait_free(pe, f + 2)
                for m in range(2):
                    for k in range(KD):
                        ins = mm(bank(f + 2)[:, m * P:m * P + P], w[:, k, m * P:m * P + P], hT[:, k, LS:TOK],
                                 k == 0, k == KD - 1)
                ins.then_inc(full(f + 2), 1)

            def turn4(f, src):
                wait_free(pe, f)
                for h in range(H):
                    ins = nc.tensor.transpose(bank(f)[:, h * P:h * P + P], src(h), idn)
                ins.then_inc(full(f), 1)

            pe.wait_ge(scond_ready, 2)
            for j in range(12):
                modulation(j, start["mod0"] + j)
            turn_x(start["hT0"], 0, lambda t: x[:, t, :])
            wait_drained(pe, start["hT0"] + 2 * NT - 1)
            for j in range(8):
                f = start["in_hy"] + 3 * j
                project_cm(f, chunk_of[f + 2])
            for n in range(2):
                pe.wait_ge(conv_ready, 4 * n + 4)
                for t in range(NT):
                    turn4(start["tr_hy"] + NT * n + t, lambda m: cm[:, n, m, cols(t)])
            for o in range(2):
                f = start[f"fft{o}"]
                if o == 0:
                    wait_drained(pe, start["tr_hy"] + NT - 1)
                else:
                    wait_drained(pe, f - 1)
                for ft in range(TS):
                    for s in range(2):
                        wait_free(pe, f)
                        for k in range(TS):
                            ins = mm(bank(f), dft[:, k, s * 512 + ft * P:s * 512 + ft * P + P], hy_v[:, k, :],
                                     k == 0, k == TS - 1)
                        ins.then_inc(full(f), 1)
                        f += 1
                for s in range(2):
                    wait_free(pe, f)
                    mm(bank(f), dft_p[:, s * P:s * P + P], hy_v[:, TP, :]).then_inc(full(f), 1)
                    f += 1
                pe.wait_ge(idft_in, 48)
                pe.wait_ge(Y_ready, NT * (o + 1))
                Y = [(YP if k < TS else YQ)[:, k % TS, :] for k in range(2 * TS)]
                Yp = [YP[:, TP, :], YQ[:, TP, :]]
                if o == 0:
                    for t in range(TS):
                        wait_free(pe, f)
                        for k in range(8):
                            ins = mm(bank(f), idft[:, k, toks(t)], Y[k], k == 0, k == 7)
                        ins.then_inc(full(f), 1)
                        f += 1
                    wait_free(pe, f)
                    for k in range(2):
                        ins = mm(bank(f), idft_p[:, k, :], Yp[k], k == 0, k == 1)
                    ins.then_inc(full(f), 1)
                else:
                    for m in range(4):
                        wait_free(pe, f)
                        for k in range(8):
                            ins = mm(bank(f), Y[k][:, m * P:m * P + P], idft[:, k, :], k == 0, k == 7)
                        ins.then_inc(full(f), 1)
                        f += 1
                    wait_free(pe, f)
                    for m in range(4):
                        for k in range(2):
                            ins = mm(bank(f)[:, m * P:m * P + P], Yp[k][:, m * P:m * P + P], idft_p[:, k, :],
                                     k == 0, k == 1)
                    ins.then_inc(full(f), 1)

            f = start["ab"]
            pe.wait_ge(gdn_in, 64)
            wait_free(pe, f)
            for t in range(NT):
                for k in range(KD):
                    ins = mm(bank(f)[:, 16 * t:16 * t + 16], hT[:, k, toks(t)], abw[:, k, :], k == 0, k == KD - 1)
            ins.then_inc(full(f), 1)
            for j in range(8):
                f = start["in_gd"] + 3 * j
                project_cm(f, chunk_of[f + 2])
            for n, src in enumerate((cm[:, 0, :, :], cm[:, 1, :, :], v_cm)):
                pe.wait_ge(cm_ready, 4 * n + 4)
                for t in range(NT):
                    turn4(start["tr_q"] + NT * n + t, lambda m: src[:, m, cols(t)])
            f = start["cumsum"]
            pe.wait_ge(g_ready, 1)
            pe.wait_ge(const_ok, 1)
            pe.wait_ge(idft_in, 48)
            wait_free(pe, f)
            for d in range(2):
                mm(bank(f)[:, 20 * d:20 * d + 20], masks[:, 2 * d * P:2 * d * P + P], gsm[:, GE, :, 4 * d:4 * d + 4])
            mm(bank(f)[:, 40:80], ones[:, :], gsm[:, GE, :, :]).then_inc(full(f), 1)
            for t in range(NT):
                for n, src in enumerate((q_tm, k_tm)):
                    pe.wait_ge(normed, 2 * t + n + 1)
                    turn4(start["back"] + 2 * t + n, lambda h: src[:, t, h * P:h * P + P])
            for t in range(NT):
                f0 = inv0(t)
                wait_drained(pe, start["back"] + 2 * t + 1)
                for n, other in enumerate((kT, qT)):
                    wait_free(pe, f0 + n)
                    for h in range(H):
                        ins = mm(bank(f0 + n)[:, h * P:h * P + P], kT[:, h, toks(t)], other[:, h, toks(t)])
                    ins.then_inc(full(f0 + n), 1)
                for d in range(2):
                    pe.wait_ge(gmask_ready, 2 * t + d + 2)
                    wait_free(pe, f0 + 2 + d)
                    mm(bank(f0 + 2 + d), ones[:, :], gm[:, d, :]).then_inc(full(f0 + 2 + d), 1)
                for d in range(2):
                    pe.wait_ge(U1_ready, 2 * t + d + 1)
                    turn4(f0 + 4 + d, lambda h: Uinv[:, 2 * t + d, h * P:h * P + P])
                for l, b in enumerate(LEVELS):
                    fl = f0 + 6 + 6 * l
                    for d in range(2):
                        wait_drained(pe, f0 + 4 + d if l == 0 else fl - 4 + d)
                        wait_free(pe, fl + d)
                        Tv = halves(Tinv[:, d, :], b)
                        for h in range(H):
                            ins = mm(bank(fl + d)[:, h * 64:h * 64 + 64], LT[:, d, h * P:h * P + P],
                                     Tv[:, h, :, d, :])
                        ins.then_inc(full(fl + d), 1)
                    for d in range(2):
                        if l > 0:
                            wait_drained(pe, fl - 2 + d)
                        wait_drained(pe, fl + d)
                        wait_free(pe, fl + 2 + d)
                        for h in range(H):
                            ins = mm(bank(fl + 2 + d)[:, h * 64:h * 64 + 64], Uinv[:, 2 * t + d, h * P:h * P + P],
                                     Xl[:, d, h * 64:h * 64 + 64])
                        ins.then_inc(full(fl + 2 + d), 1)
                    for d in range(2):
                        wait_drained(pe, fl + 2 + d)
                        turn4(fl + 4 + d, lambda h: Tinv[:, d, h * P:h * P + P])
                for j in range(MODS[t], MODS[t + 1]):
                    modulation(j, mod1(j))
            wait_drained(pe, inv0(NT - 1) + INV - 1)
            pe.wait_ge(state_in, 32)
            for s in range(NT):
                fs = start["scan"] + 10 * s
                St = Sp if s == TP else S
                tt = [s, s if s == TP else TS - 1 - s]
                for d in range(2):
                    if s > 0:
                        wait_drained(pe, fs - 4 + d)
                    if s == TP and d == 0:
                        pe.wait_ge(S_ready, 1)
                    wait_free(pe, fs + d)
                    for h in range(H):
                        ins = mm(bank(fs + d)[:, h * P:h * P + P], kT[:, h, toks(tt[d])], St[:, d, h * P:h * P + P])
                    ins.then_inc(full(fs + d), 1)
                for d in range(2):
                    wait_free(pe, fs + 2 + d)
                    for h in range(H):
                        ins = mm(bank(fs + 2 + d)[:, h * P:h * P + P], qT[:, h, toks(tt[d])],
                                 St[:, d, h * P:h * P + P])
                    ins.then_inc(full(fs + 2 + d), 1)
                for d in range(2):
                    wait_drained(pe, fs + d)
                    wait_free(pe, fs + 4 + d)
                    for h in range(H):
                        ins = mm(bank(fs + 4 + d)[:, h * P:h * P + P], Uinv[:, 2 * tt[d] + d, h * P:h * P + P],
                                 rr[:, d, h * P:h * P + P])
                    ins.then_inc(full(fs + 4 + d), 1)
                for d in range(2):
                    wait_drained(pe, fs + 4 + d)
                    pe.wait_ge(kd_ready, 2 * s + d + 1)
                    wait_free(pe, fs + 6 + d)
                    for h in range(H):
                        ins = mm(bank(fs + 6 + d)[:, h * P:h * P + P], kd[:, d, h * P:h * P + P],
                                 vn[:, d, h * P:h * P + P])
                    ins.then_inc(full(fs + 6 + d), 1)
                for d in range(2):
                    wait_free(pe, fs + 8 + d)
                    for h in range(H):
                        ins = mm(bank(fs + 8 + d)[:, h * P:h * P + P], intraT[:, 2 * tt[d] + d, h * P:h * P + P],
                                 vn[:, d, h * P:h * P + P])
                    ins.then_inc(full(fs + 8 + d), 1)
            for t in range(NT):
                pe.wait_ge(on_ready, t + 1)
                turn4(start["tr_o"] + t, lambda h: o_acc[:, t, h * P:h * P + P])

            def spread_gates(base, diag, before):
                for n in range(4):
                    pe.wait_ge(diag_ready, before + 4 * n + 4)
                    wait_free(pe, base + n)
                    for k in range(4):
                        ins = mm(bank(base + n)[:, k * P:k * P + P], ones[:, :], diag[:, 4 * n + k, :])
                    ins.then_inc(full(base + n), 1)

            def project_out(base):
                for j in range(4):
                    i = chunk_of[base + NT * j + NT - 1]
                    wait_chunk(pe, i)
                    for t in range(NT):
                        f = base + NT * j + t
                        wait_free(pe, f)
                        for k in range(KD):
                            ins = mm(bank(f)[:, 0:WC], mix[:, k, toks(t)], wchunk(i)[:, k, :], k == 0, k == KD - 1)
                        ins.then_inc(full(f), 1)

            spread_gates(start["gate0"], view(19968, 16, P), 0)
            pe.wait_ge(hy_done, 5)
            wait_drained(pe, start["tr_o"] + NT - 1)
            project_out(start["out0"])

            turn_x(start["hT1"], NT, lambda t: xn[:, t % 2, :])
            wait_drained(pe, start["hT1"] + 2 * NT - 1)
            for j in range(6):
                n = WC if j < 5 else RKV + ROPE
                i = chunk_of[start["in_tm"] + NT * j + NT - 1]
                wait_chunk(pe, i)
                for t in range(NT):
                    f = start["in_tm"] + NT * j + t
                    wait_free(pe, f)
                    for k in range(KD):
                        ins = mm(bank(f)[:, 0:n], hT[:, k, toks(t)], wchunk(i)[:, k, 0:n], k == 0, k == KD - 1)
                    ins.then_inc(full(f), 1)
            for j in range(4):
                f = start["in_g"] + 3 * j
                project_cm(f, chunk_of[f + 2])
            for t in range(NT + 1):
                f = start["tr_att"] + 3 * t
                if t < NT:
                    pe.wait_ge(onorm_ready, t + 1)
                    turn4(f, lambda h: ztm[:, t, h // 2, (h % 2) * P:(h % 2) * P + P])
                    turn4(f + 1, lambda h: ztm[:, t, 2 + h // 2, (h % 2) * P:(h % 2) * P + P])
                    wait_free(pe, f + 2)
                    nc.tensor.transpose(bank(f + 2)[:, 0:P], ztm[:, t, 4, 0:P], idn)
                    nc.tensor.transpose(bank(f + 2)[0:ROPE, P:2 * P], ztm[:, t, 4, P:P + ROPE], idn)\
                        .then_inc(full(f + 2), 1)
                else:
                    pe.wait_ge(odd_in, 160)
                    wait_free(pe, f)
                    for h in range(2):
                        nc.tensor.transpose(bank(f)[:, h * P:h * P + P], c_k[:, h * P:h * P + P], idn)
                    nc.tensor.transpose(bank(f)[:, 2 * P:3 * P], c_ckv, idn)
                    nc.tensor.transpose(bank(f)[0:ROPE, 3 * P:4 * P], c_kpe, idn).then_inc(full(f), 1)
            wait_drained(pe, start["tr_att"] + 3 * NT)
            qw = q_up.rearrange("p k (h c) -> p k h c", h=H)
            kw = kv_up.rearrange("p (h c) -> p h c", h=H)
            for h in range(H):
                f = start["q_nope"] + h
                wait_free(pe, f)
                for k in range(2):
                    ins = mm(bank(f), qw[:, k, h, 0:P], mqT[:, k, 0:LS], k == 0, k == 1)
                ins.then_inc(full(f), 1)
            f = start["q_nope"] + H
            wait_free(pe, f)
            for h in range(H):
                for k in range(2):
                    ins = mm(bank(f)[:, h * P:h * P + P], qw[:, k, h, 0:P], mqT[:, k, LS:TOK], k == 0, k == 1)
            ins.then_inc(full(f), 1)
            for t in range(NT):
                f = start["q_pe"] + t
                wait_free(pe, f)
                for k in range(2):
                    ins = mm(bank(f)[:, 0:WC], mqT[:, k, toks(t)], qw[:, k, :, P:P + ROPE], k == 0, k == 1)
                ins.then_inc(full(f), 1)
            for h in range(H):
                f = start["k_nope"] + h
                wait_free(pe, f)
                mm(bank(f), kw[:, h, 0:P], ckvT[:, 0:LS]).then_inc(full(f), 1)
            for g in range(2):
                f = start["k_nope"] + H + g
                wait_free(pe, f)
                for h in range(2):
                    ins = mm(bank(f)[:, h * WC:h * WC + WC], kw[:, 2 * g + h, 0:P], ckvT[:, LS:TOK + P])
                ins.then_inc(full(f), 1)
            for t in range(NT + 1):
                f = start["v_up"] + t
                wait_free(pe, f)
                mm(bank(f), ckvT[:, toks(t)], kw[:, :, P:2 * P]).then_inc(full(f), 1)
            for t in range(NT):
                f = start["tr_qpe"] + t
                if t < TS:
                    pe.wait_ge(qpe_ready, t + 1)
                else:
                    wait_drained(pe, start["q_pe"] + t)
                wait_free(pe, f)
                for h in range(H):
                    ins = nc.tensor.transpose(bank(f)[0:ROPE, h * P:h * P + P], qpe[:, t, h * ROPE:(h + 1) * ROPE], idn)
                ins.then_inc(full(f), 1)

            def scores(u):
                kind, h0 = UNITS[u]
                f = units[u]["s"]

                def product(o, h, q, keys):
                    if h < 4:
                        return mm(o, oq[:, h, q], ok[:, h // 2, keys])
                    mm(o, qnT[:, h - 4, q], knT[:, h - 4, keys], True, False)
                    return mm(o, qpT[0:ROPE, h - 4, q], kpT[0:ROPE, keys], False, True)

                if kind == "sample":
                    for g in range(4):
                        wait_free(pe, f + g)
                        product(bank(f + g), h0, toks(g), slice(0, LS)).then_inc(full(f + g), 1)
                    wait_free(pe, f + 4)
                    for g in range(4):
                        ins = product(bank(f + 4)[:, g * P:g * P + P], h0, toks(g), toks(NT))
                    ins.then_inc(full(f + 4), 1)
                else:
                    wait_free(pe, f)
                    for g in range(4):
                        ins = product(bank(f)[:, g * P:g * P + P], h0 + g, toks(TP), toks(TP))
                    ins.then_inc(full(f), 1)

            def values(u):
                kind, h0 = UNITS[u]
                pe.wait_ge(prob_ready, 4 * u + 4)
                f = units[u]["t"]
                n = 5 if kind == "sample" else 1
                for k in range(n):
                    turn4(f + k, lambda g: prob[u % 2][:, g, k * P:k * P + P])
                f = units[u]["p"]
                wait_free(pe, f)
                wait_drained(pe, units[u]["t"] + n - 1)

                def vals(h, t):
                    return v_all[:, t, (h // 2) * P:(h // 2) * P + P] if h < 4 else vm[:, t, (h - 4) * P:(h - 3) * P]

                if kind == "sample":
                    for k in range(5):
                        ins = mm(bank(f), vals(h0, k if k < TS else NT), probT[u % 2][:, k, :], k == 0, k == 4)
                else:
                    for g in range(4):
                        ins = mm(bank(f)[:, g * P:g * P + P], vals(h0 + g, TP), probT[u % 2][:, 0, g * P:g * P + P])
                ins.then_inc(full(f), 1)

            wait_drained(pe, start["tr_qpe"] + NT - 1)
            scores(0)
            for u in range(len(UNITS)):
                if u + 1 < len(UNITS):
                    scores(u + 1)
                values(u)
            spread_gates(start["gate1"], view(19968, 16, P), 16)
            wait_drained(pe, units[-1]["p"])
            project_out(start["out1"])

        @block.vector
        def _(dve):
            steps = [0]

            def chained(ins):
                steps[0] += 1
                ins.then_inc(dve_step, 1)
                dve.wait_ge(dve_step, steps[0])

            tt, ts, stt = nc.vector.tensor_tensor, nc.vector.tensor_scalar, nc.vector.scalar_tensor_tensor

            def heads(ap):
                return ap.rearrange("p (h c) -> p h c", h=H)

            two_pi = 2.0 * math.pi
            hi = float(np.float32(np.round(two_pi * 1024) / 1024))
            lo = two_pi - hi
            for layer in range(2):
                for n, (c0, c1) in enumerate(((0, LS), (LS, TOK))):
                    f = start["film"] + 2 * layer + n
                    wait_full(dve, f)
                    ts(h2[0:64, c0:c1], bank(f)[0:64, 0:c1 - c0], film_w[0:64, 128 + layer:129 + layer],
                       film_w[0:64, 130 + layer:131 + layer], ALU.add, ALU.mult).then_inc(free(f), 1)
                    wait_drained(dve, f)
                chained(ts(turns[0:64, :].bitcast(I32), h2[0:64, :], 1.0 / two_pi, None, ALU.mult))
                chained(nc.vector.tensor_copy(turns_f[0:64, :], turns[0:64, :].bitcast(I32)))
                chained(stt(h2[0:64, :], turns_f[0:64, :], -hi, h2[0:64, :], ALU.mult, ALU.add))
                chained(stt(h2[0:64, :], turns_f[0:64, :], -lo, h2[0:64, :], ALU.mult, ALU.add))
                ts(h2[0:64, :], h2[0:64, :], 3.1415925, -3.1415925, ALU.min, ALU.max).then_inc(arg_ready, 1)
            dve.wait_ge(film_in, 16 * 13)
            for o in range(2):
                for t in range(NT):
                    f = start[f"filt{o}"] + 2 * t
                    pl, mi = plus[o][:, t, :], minus[o][:, t, :]
                    wait_full(dve, f)
                    tt(pl, bank(f), window[:, t, :], ALU.mult).then_inc(free(f), 1)
                    wait_full(dve, f + 1)
                    tt(mi, bank(f + 1), window[:, t, :], ALU.mult).then_inc(free(f + 1), 1)
                    wait_drained(dve, f + 1)
                    if t in (0, TP):
                        chained(nc.vector.memset(mi[0:1, :], 0.0))
                        chained(tt(pl[0:1, :], pl[0:1, :], wflat[0:1, 1024 + CH * o:1024 + CH * (o + 1)], ALU.add))
                    chained(tt(pl, pl, mi, ALU.add))
                    stt(mi, mi, -2.0, pl, ALU.mult, ALU.add).then_inc(taps_ready, 1)

            def pre_norm(base_sq):
                dve.wait_ge(sq_ready, base_sq + NT)
                ts(stat[:, 0, 0:NT], stat[:, 0, 0:NT], 1.0 / D, EPS, ALU.mult, ALU.add).then_inc(prestat_ready, 1)

            def take_modulation(j, f, layer):
                wait_full(dve, f)
                tt(modc_l[layer][:, 2 * j:2 * j + 2, :], bank(f)[:, 0:4].rearrange("p (m c) -> p m c", m=2),
                   vec1[:, 24 * layer + 2 * j:24 * layer + 2 * j + 2].unsqueeze(2).broadcast_to([P, 2, 2]),
                   ALU.add).then_inc(free(f), 1)

            def modulation_columns(layer, last):
                wait_drained(dve, last)
                stt(acol_l[layer][:, :, :], modc_l[layer][:, 8:16, :], 1.0,
                    vec1[:, 48 + 8 * layer:56 + 8 * layer].unsqueeze(2).broadcast_to([P, KD, 2]),
                    ALU.add, ALU.mult).then_inc(acol_ready, 1)
                tt(gcol_l[layer][:, :, :], modc_l[layer][:, 16:24, :],
                   vec1[:, 64 + 8 * layer:72 + 8 * layer].unsqueeze(2).broadcast_to([P, KD, 2]),
                   ALU.mult).then_inc(acol_ready, 1)

            pre_norm(0)
            nc.vector.memset(pad[:, :, :], 0.0).then_inc(pad_zero, 1)
            dve.wait_ge(rstd_ready, 1)
            for t in range(NT):
                ts(x[:, t, :], x[:, t, :], stat[:, 1, t:t + 1], None, ALU.mult).then_inc(xn_ready, 1)
            wait_drained(dve, start["vectors"] + 1)
            for j in range(12):
                take_modulation(j, start["mod0"] + j, 0)
            modulation_columns(0, start["mod0"] + 11)

            def convolve(f, width, w0, b0, dst, m0):
                wait_drained(dve, f + 2)
                for m in range(2):
                    o = dst[:, m0 + m, :]
                    for j in range(width):
                        src = pad[:, m, 2 - width // 2 + j:2 - width // 2 + j + CMW]
                        w = vec2[:, w0 + 12 * j + m0 + m:w0 + 12 * j + m0 + m + 1]
                        if j == 0 and b0 is None:
                            chained(ts(o, src, w, None, ALU.mult))
                        elif j == 0:
                            chained(ts(o, src, w, vec2[:, b0 + m0 + m:b0 + m0 + m + 1], ALU.mult, ALU.add))
                        elif j < width - 1:
                            chained(stt(o, src, w, o, ALU.mult, ALU.add))
                        else:
                            stt(o, src, w, o, ALU.mult, ALU.add).then_inc(conv_ready, 1)

            for j in range(6):
                convolve(start["in_hy"] + 6 + 3 * j, 3, 60 + 4 * (j // 2), 96 + 4 * (j // 2),
                         (cm[:, 0, :, :], cm[:, 1, :, :], hy_x2)[j // 2], 2 * (j % 2))
            for n, dst in enumerate((hy_v, hy_x1)):
                for t in range(NT):
                    f = start["tr_hy"] + NT * n + t
                    wait_full(dve, f)
                    nc.vector.tensor_copy(dst[:, t, :], bank(f)).then_inc(free(f), 1)
            wait_drained(dve, start["spec1"] + 11)
            s0, s1 = pflat[:, 0:512], pflat[:, 512:1024]
            for o in range(2):
                f = start[f"fft{o}"]
                if o == 0:
                    wait_full(dve, start["tr_hy"] + 2 * NT - 1)
                for ft in range(NT):
                    hx = specX[o][:, 0 if ft == 0 else 1, :] if ft in (0, TP) else specP[o][:, ft, :]
                    wait_full(dve, f)
                    tt(YP[:, ft, :], bank(f), specP[o][:, ft, :], ALU.mult)
                    tt(YQ[:, ft, :], bank(f), specQ[o][:, ft, :], ALU.mult).then_inc(free(f), 1)
                    wait_full(dve, f + 1)
                    tt(s0, bank(f + 1), specQ[o][:, ft, :], ALU.mult)
                    tt(s1, bank(f + 1), hx, ALU.mult).then_inc(free(f + 1), 1)
                    wait_drained(dve, f + 1)
                    tt(YP[:, ft, :], YP[:, ft, :], s0, ALU.subtract)
                    tt(YQ[:, ft, :], YQ[:, ft, :], s1, ALU.add).then_inc(Y_ready, 1)
                    dve.wait_ge(Y_ready, NT * o + ft + 1)
                    f += 2
                if o == 0:
                    for t in range(NT):
                        wait_full(dve, f)
                        tt(hy_v[:, t, :], bank(f), hy_x1[:, t, :], ALU.mult).then_inc(free(f), 1)
                        f += 1
                else:
                    for m in range(4):
                        wait_full(dve, f)
                        tt(hy_x2[:, m, 0:LS], bank(f), hy_x2[:, m, 0:LS], ALU.mult).then_inc(free(f), 1)
                        wait_drained(dve, f)
                        tt(mix[:, 4 + m, 0:LS], hy_x2[:, m, 0:LS], mix[:, 4 + m, 0:LS], ALU.mult).then_inc(hy_done, 1)
                        f += 1
                    wait_full(dve, f)
                    tt(hy_x2[:, :, CMP:CMP + LP], heads(bank(f)), hy_x2[:, :, CMP:CMP + LP], ALU.mult)\
                        .then_inc(free(f), 1)
                    wait_drained(dve, f)
                    tt(mix[:, 4:8, LS:TOK], hy_x2[:, :, CMP:CMP + LP], mix[:, 4:8, LS:TOK], ALU.mult)\
                        .then_inc(hy_done, 1)

            nc.vector.memset(pad[:, :, :], 0.0).then_inc(pad_zero, 1)
            f = start["ab"]
            wait_full(dve, f)
            dve.wait_ge(gdn_in, 64)
            nc.vector.tensor_copy(ab, bank(f)[:, 0:16 * NT].rearrange("p (t c) -> p t c", t=NT)).then_inc(free(f), 1)
            wait_drained(dve, f)
            chained(tt(gsm[:, T0, :, :], ab[:, :, 0:8], dtb.unsqueeze(1).broadcast_to([P, NT, 8]), ALU.add))
            chained(ts(gsm[:, T1, :, :], gsm[:, T0, :, :], -1.0, None, ALU.mult))
            tt(gsm[:, T1, :, :], gsm[:, T0, :, :], gsm[:, T1, :, :], ALU.min).then_inc(g_chain, 1)
            for j in range(6):
                convolve(start["in_gd"] + 6 + 3 * j, 5, 4 * (j // 2), None,
                         (cm[:, 0, :, :], cm[:, 1, :, :], v_cm)[j // 2], 2 * (j % 2))
            for n in range(2):
                for t in range(NT):
                    wait_drained(dve, start["tr_q"] + NT * n + t)
                    dst = stat[:, 0, 4 * t:4 * t + 4] if n == 0 else gsm[:, T3, t, 0:4]
                    nc.vector.tensor_reduce(dst, heads(pflat[:, 0:512]), AXX, ALU.add).then_inc(ss_ready, 1)
            dve.wait_ge(ss_ready, 2 * NT)
            ts(stat[:, 0, :], stat[:, 0, :], EPS, None, ALU.add)
            ts(gsm[:, T3, :, 0:4], gsm[:, T3, :, 0:4], EPS, None, ALU.add).then_inc(ss_ready, 1)
            dve.wait_ge(rinv_ready, 1)
            for t in range(NT):
                tt(heads(q_tm[:, t, :]), heads(q_tm[:, t, :]),
                   stat[:, 1, 4 * t:4 * t + 4].unsqueeze(2).broadcast_to([P, H, P]), ALU.mult).then_inc(normed, 1)
                tt(heads(k_tm[:, t, :]), heads(k_tm[:, t, :]),
                   gsm[:, T3, t, 0:4].unsqueeze(2).broadcast_to([P, H, P]), ALU.mult).then_inc(normed, 1)
            dve.wait_ge(g_act, 1)
            chained(stt(gsm[:, GE, :, :], gsm[:, T0, :, :], 0.0, gsm[:, T1, :, :], ALU.max, ALU.add))
            stt(gsm[:, GE, :, :], gsm[:, GE, :, :], -1.0, alog.unsqueeze(1).broadcast_to([P, NT, 8]),
                ALU.mult, ALU.mult).then_inc(g_ready, 1)
            chained(ts(gsm[:, BE, :, :], gsm[:, BE, :, :], 1.0, None, ALU.add))
            chained(nc.vector.reciprocal(gsm[:, BE, :, :], gsm[:, BE, :, :]))
            f = start["cumsum"]
            wait_full(dve, f)
            for d in range(2):
                nc.vector.tensor_copy(gsm[:, CS, :, 4 * d:4 * d + 4],
                                      bank(f)[:, 20 * d:20 * d + 20].rearrange("p (t h) -> p t h", t=NT))
            nc.vector.tensor_copy(gsm[:, TOT, :, :], bank(f)[:, 40:80].rearrange("p (t h) -> p t h", t=NT))\
                .then_inc(free(f), 1)
            wait_drained(dve, f)
            tt(gsm[:, KDF, :, :], gsm[:, TOT, :, :], gsm[:, CS, :, :], ALU.subtract).then_inc(scal_ready, 1)
            dve.wait_ge(g_act, 2)
            chained(ts(gsm[:, NEG, :, :], gsm[:, EG, :, :], -1.0, None, ALU.mult))
            for t in range(NT):
                f0 = inv0(t)
                for d in range(2):
                    f = f0 + 2 + d
                    wait_full(dve, f)
                    for h in range(H):
                        ins = ts(dec[:, d, h * P:h * P + P], bank(f)[:, h * P:h * P + P],
                                 gsm[:, CS, t, 4 * d + h:4 * d + h + 1], 0.0, ALU.subtract, ALU.min)
                    ins.then_inc(free(f), 1)
                wait_full(dve, f0)
                for d in range(2):
                    dve.wait_ge(masked, 4 * t + 2 * d + 2)
                    for h in range(H):
                        ins = stt(LT[:, d, h * P:h * P + P], bank(f0)[:, h * P:h * P + P],
                                  gsm[:, BE, t, 4 * d + h:4 * d + h + 1], dec[:, d, h * P:h * P + P],
                                  ALU.mult, ALU.mult)
                    ins.then_inc(LT_ready if d == 0 else free(f0), 1)
                wait_full(dve, f0 + 1)
                for d in range(2):
                    iv = intraT[:, 2 * t + d, :]
                    ins = tt(iv, bank(f0 + 1), iv, ALU.mult)
                ins.then_inc(free(f0 + 1), 1)
                for l, b in enumerate(LEVELS):
                    fl = f0 + 6 + 6 * l
                    for d in range(2):
                        wait_full(dve, fl + d)
                        at = 2 * P + 64 * (len(LEVELS) * d + l)
                        stt(Xl[:, d, :].rearrange("p (h c) -> p h c", h=H),
                            bank(fl + d)[:, 0:256].rearrange("p (h c) -> p h c", h=H), -1.0,
                            levels[:, at:at + 64].unsqueeze(1).broadcast_to([P, H, 64]), ALU.mult, ALU.mult)\
                            .then_inc(free(fl + d), 1)
                    for d in range(2):
                        wait_full(dve, fl + 2 + d)
                        Tv = halves(Tinv[:, d, :], b)[:, :, :, d, :]
                        tt(Tv, Tv, bank(fl + 2 + d)[:, 0:256].rearrange("p (h n b) -> p h n b", h=H, b=b), ALU.add)\
                            .then_inc(free(fl + 2 + d), 1)
                for j in range(MODS[t], MODS[t + 1]):
                    take_modulation(j, mod1(j), 1)
            modulation_columns(1, mod1(11))
            wait_full(dve, inv0(NT - 1) + INV - 1)
            nc.vector.memset(Sp[:, :, :], 0.0).then_inc(S_ready, 1)
            dve.wait_ge(state_in, 32)
            dve.wait_ge(S_ready, 1)
            dve.wait_ge(gmask_ready, 1)
            for s in range(NT):
                fs = start["scan"] + 10 * s
                St = Sp if s == TP else S
                tl = [s, s if s == TP else TS - 1 - s]

                def sc(which, d, h):
                    return gsm[:, which, tl[d], 4 * d + h:4 * d + h + 1]

                for d in range(2):
                    f = fs + d
                    wait_full(dve, f)
                    for h in range(H):
                        ins = stt(rr[:, d, h * P:h * P + P], bank(f)[:, h * P:h * P + P], sc(NEG, d, h),
                                  v_tm[:, tl[d], h * P:h * P + P], ALU.mult, ALU.add)
                    ins.then_inc(free(f), 1)
                for d in range(2):
                    f = fs + 2 + d
                    wait_full(dve, f)
                    for h in range(H):
                        oh = o_acc[:, tl[d], h * P:h * P + P]
                        ins = stt(oh, bank(f)[:, h * P:h * P + P], sc(EG, d, h), oh, ALU.mult, ALU.add)
                    ins.then_inc(free(f), 1)
                    wait_drained(dve, f)
                for d in range(2):
                    f = fs + 4 + d
                    wait_full(dve, f)
                    tt(heads(vn[:, d, :]), heads(bank(f)),
                       gsm[:, BE, tl[d], 4 * d:4 * d + 4].unsqueeze(2).broadcast_to([P, H, P]), ALU.mult)\
                        .then_inc(free(f), 1)
                for d in range(2):
                    f = fs + 6 + d
                    wait_full(dve, f)
                    for h in range(H):
                        Sh = St[:, d, h * P:h * P + P]
                        ins = stt(Sh, Sh, sc(GL, d, h), bank(f)[:, h * P:h * P + P], ALU.mult, ALU.add)
                    ins.then_inc(free(f), 1)
                for d in range(2):
                    f = fs + 8 + d
                    wait_full(dve, f)
                    tt(o_acc[:, tl[d], :], bank(f), o_acc[:, tl[d], :], ALU.add).then_inc(free(f), 1)
                    wait_drained(dve, f)
            for t in range(NT):
                dve.wait_ge(osq_ready, t + 1)
                nc.vector.tensor_reduce(stat[:, 0, 4 * t:4 * t + 4], heads(kd[:, 0, :]), AXX, ALU.add)\
                    .then_inc(oss_ready, 1)
            dve.wait_ge(oss_ready, NT)
            ts(stat[:, 0, :], stat[:, 0, :], 1.0 / P, EPS, ALU.mult, ALU.add).then_inc(oss_ready, 1)
            dve.wait_ge(orstd_ready, 1)
            for t in range(NT):
                tt(heads(o_acc[:, t, :]), heads(o_acc[:, t, :]),
                   stat[:, 1, 4 * t:4 * t + 4].unsqueeze(2).broadcast_to([P, H, P]), ALU.mult).then_inc(on_ready, 1)
            for t in range(NT):
                f = start["tr_o"] + t
                wait_full(dve, f)
                mv = mix[:, 0:4, toks(t)]
                stt(mv, heads(bank(f)), vec1[:, 96:97], mv, ALU.mult, ALU.mult).then_inc(free(f), 1)

            def post_norm(layer):
                dve.wait_ge(yss_ready, NT * (layer + 1))
                ts(yst[:, 0, 0:NT], yst[:, 0, 0:NT], 1.0 / D, EPS, ALU.mult, ALU.add).then_inc(yrstd_ready, 1)
                dve.wait_ge(yrstd_ready, 2 * layer + 2)
                for t in range(NT):
                    if t >= 2:
                        dve.wait_ge(x_ready, NT * layer + t - 1)
                    stt(ys[:, t % 2, :], y[:, t, :], yst[:, 1, t:t + 1], gb[:, 0 if t < TS else 1, :],
                        ALU.mult, ALU.mult).then_inc(ys_ready, 1)

            post_norm(0)

            pre_norm(NT)
            dve.wait_ge(rstd_ready, 2)
            for t in range(NT):
                if t >= 2:
                    wait_full(dve, start["hT1"] + 2 * (t - 2) + 1)
                ts(xn[:, t % 2, :], x[:, t, :], stat[:, 1, t:t + 1], None, ALU.mult).then_inc(xn_ready, 1)
            dve.wait_ge(z_ready, 8 * NT)
            ts(ostat[:, 0, :, 0:7], ostat[:, 0, :, 0:7], 1.0 / P, EPS, ALU.mult, ALU.add)
            ts(ostat[:, 0, :, 7:8], ostat[:, 0, :, 7:8], 1.0 / RQ, EPS, ALU.mult, ALU.add).then_inc(osum_ready, 1)
            dve.wait_ge(oinv_ready, 1)
            dve.wait_ge(odd_in, 160)

            def rotate(v, n, width, cos, sin):
                b = width // 4
                scratch = pflat[:, 0:n * width]

                def split(ap, heads_):
                    return ap.rearrange("p (h a two b) -> p h a two b", h=heads_, a=2, two=2, b=b)

                def table(ap, i):
                    return ap.rearrange("p (a two b) -> p a two b", a=2, two=2, b=b)[:, :, i, :]\
                        .unsqueeze(1).broadcast_to([P, n, 2, b])

                for i in range(2):
                    ins = tt(split(scratch, n)[:, :, :, i, :], split(v, n)[:, :, :, 1 - i, :], table(sin, i), ALU.mult)
                chained(ins)
                vh = v.rearrange("p (h c) -> p h c", h=n)
                chained(tt(vh, vh, cos.unsqueeze(1).broadcast_to([P, n, width]), ALU.mult))
                return tt(v, v, scratch, ALU.add)

            for t in range(NT):
                z = ztm[:, t, :, :].rearrange("p j c -> p (j c)")
                for lo, n, w, i, g in ((0, 4, P, 0, 0), (4 * P, 2, P, 4, 1), (8 * P, 1, P, 6, 2), (6 * P, 1, 2 * P, 7, None)):
                    v = z[:, lo:lo + n * w].rearrange("p (h c) -> p h c", h=n)
                    ins = tt(v, v, ostat[:, 1, t, i:i + n].unsqueeze(2).broadcast_to([P, n, w]), ALU.mult)
                    if g is not None:
                        chained(ins)
                        chained(tt(v, v, g_rows[:, g, :].unsqueeze(1).broadcast_to([P, n, w]), ALU.mult))
                if t < TS:
                    chained(ins)
                    chained(rotate(z[:, 0:4 * P], 4, P, rope[:, t, 0:P], rope[:, t, P:2 * P]))
                    chained(rotate(z[:, 4 * P:6 * P], 2, P, rope[:, t, 0:P], rope[:, t, P:2 * P]))
                    ins = rotate(z[:, 9 * P:9 * P + ROPE], 1, ROPE, rope[:, t, 2 * P:2 * P + ROPE],
                                 rope[:, t, 2 * P + ROPE:2 * P + 2 * ROPE])
                ins.then_inc(onorm_ready, 1)
                dve.wait_ge(onorm_ready, t + 1)
            for t in range(TS):
                wait_drained(dve, start["q_pe"] + t)
                rotate(qpe[:, t, :], 4, ROPE, rope[:, t, 2 * P:2 * P + ROPE],
                       rope[:, t, 2 * P + ROPE:2 * P + 2 * ROPE]).then_inc(qpe_ready, 1)
                dve.wait_ge(qpe_ready, t + 1)

            def maxima(u):
                kind, h = UNITS[u]
                scale = (P if h < 4 else P + ROPE) ** -0.5
                f = units[u]["s"]
                if kind == "sample":
                    for g in range(4):
                        wait_full(dve, f + g)
                        nc.vector.tensor_reduce(smax[:, u % 2, 0, g:g + 1], bank(f + g), AXX, ALU.max)
                    wait_full(dve, f + 4)
                    chained(nc.vector.tensor_reduce(smax[:, u % 2, 1, :], heads(bank(f + 4)), AXX, ALU.max))
                    chained(tt(smax[:, u % 2, 0, :], smax[:, u % 2, 0, :], smax[:, u % 2, 1, :], ALU.max))
                else:
                    wait_full(dve, f)
                    chained(nc.vector.tensor_reduce(smax[:, u % 2, 0, :], heads(bank(f)), AXX, ALU.max))
                ts(nmax[:, u % 2, :], smax[:, u % 2, 0, :], -scale, None, ALU.mult).then_inc(max_ready, 1)

            def inverse_sums(u):
                kind, h = UNITS[u]
                f = units[u]["s"]
                if kind == "sample":
                    wait_drained(dve, f + 4)
                    chained(tt(ssum[:, u % 2, 1, :], ssum[:, u % 2, 0, :], ssum[:, u % 2, 1, :], ALU.add))
                else:
                    wait_drained(dve, f)
                nc.vector.reciprocal(rsum[:, u % 2, :], ssum[:, u % 2, 1, :]).then_inc(exp_ready, 1)

            def gate_output(u):
                kind, h = UNITS[u]
                f = units[u]["p"]
                wait_full(dve, f)
                if kind == "sample":
                    tt(mix[:, h, 0:LS], bank(f), mix[:, h, 0:LS], ALU.mult).then_inc(free(f), 1)
                else:
                    tt(mix[:, h:h + 4, LS:TOK], heads(bank(f)), mix[:, h:h + 4, LS:TOK], ALU.mult).then_inc(free(f), 1)

            dve.wait_ge(cache_out, 1)
            maxima(0)
            inverse_sums(0)
            for u in range(len(UNITS)):
                if u + 1 < len(UNITS):
                    maxima(u + 1)
                    inverse_sums(u + 1)
                gate_output(u)
            post_norm(1)


_INS = ['x_prompt', 'x_sample', 'state_gdn_fwd', 'state_gdn_bwd', 'cache_gqa_k', 'cache_gqa_v', 'cache_mla_ckv',
        'cache_mla_kpe', 'c', 'c_ctx', 'mod_w', 'mod_b', 'pre_norm_g', 'post_norm_g', 'even_in_w', 'gdn_conv_w',
        'gdn_a_log', 'gdn_dt_bias', 'gdn_norm_g', 'hyena_conv_w', 'hyena_conv_b', 'hyena_ffn_w1', 'hyena_ffn_b1',
        'hyena_ffn_w2', 'hyena_ffn_b2', 'hyena_ffn_w3', 'hyena_sin_freq', 'hyena_bias', 'even_out_w', 'odd_in_w',
        'gqa_q_norm_g', 'gqa_k_norm_g', 'mla_q_norm_g', 'mla_q_up', 'mla_kv_norm_g', 'mla_kv_up', 'odd_out_w']
_OUTS = [('y_prompt', (1, LP, D)), ('y_sample', (1, LS, D)), ('new_gdn_fwd', (1, 1, H, P, P)),
         ('new_gdn_bwd', (1, 1, H, P, P)), ('new_gqa_k', (1, 1, LP, 2, P)), ('new_gqa_v', (1, 1, LP, 2, P)),
         ('new_mla_ckv', (1, 1, LP, RKV)), ('new_mla_kpe', (1, 1, LP, ROPE))]


def kernel(**inputs):
    import concourse.bacc as bacc
    from concourse.bass_utils import run_bass_kernel_spmd as run

    nc = bacc.Bacc("TRN2", target_bir_lowering=False, num_devices=1)
    arrays, ins, outs, tables = {}, {}, {}, {}
    for name in _INS:
        v = np.ascontiguousarray(inputs[name])
        arrays[f"in_{name}"] = v
        ins[name] = nc.dram_tensor(f"in_{name}", v.shape, mybir.dt.from_np(v.dtype), kind="ExternalInput").ap()
    for name, v in constants().items():
        arrays[name] = v
        tables[name] = nc.dram_tensor(name, v.shape, F32, kind="ExternalInput").ap()
    for name, shape in _OUTS:
        outs[name] = nc.dram_tensor(f"out_{name}", shape, F32, kind="ExternalOutput").ap()
    program(nc, ins, outs, tables)
    r = run(nc, [arrays], core_ids=[0])
    return tuple(r.results[0][f"out_{name}"] for name, _ in _OUTS)
```

```python
import math
from contextlib import ExitStack

import numpy as np

import concourse.bass as bass
from concourse import mybir

F32 = mybir.dt.float32
I32 = mybir.dt.int32
ALU = mybir.AluOpType
ACT = mybir.ActivationFunctionType
AXX = mybir.AxisListType.X

P = 128
D = 1024
KD = D // P
LS, LP = 512, 128
NT = (LS + LP) // P
TS = LS // P
TP = TS
TOK = LS + LP
H = 4
CH = 512
EPS = 1e-6
BANKS = 8

Q0, K0, V0, AB0, ZG0, HV0, HX10, HX20, HG0 = 0, 512, 1024, 1536, 1552, 2064, 2576, 3088, 3600
GQ0, GK0, GG0, MQ0, MG0 = 0, 512, 1024, 1536, 1984
RQ, RKV, ROPE = 256, 128, 64
WC = 256
WSLOTS = 3

ZPAD = TOK + 8
CMW = TOK + 4
CMP = LS + 4

INV = 42
GROUPS = [[0, 1], [2, 3], [4]]
LEVELS = [2, 4, 8, 16, 32, 64]

FILLS = [("film", 4), ("vectors", 2), ("filt0", 2 * NT), ("filt1", 2 * NT), ("spec_mod", 24 + 24),
         ("hT0", 2 * NT), ("in_hy", 24), ("tr_hy", 2 * NT), ("fft0", 15), ("fft1", 15),
         ("ab", 1), ("in_qkv", 18), ("cumsum", 1), ("in_z0", 3), ("tr_q", NT), ("tr_k", NT), ("tr_v", NT), ("in_z1", 3),
         ("back", 2 * NT), ("inv", NT * INV + 24), ("scan", 10 * NT), ("gate0", 4), ("tr_o", NT), ("out0", 4 * NT),
         ("hT1", 2 * NT), ("in_tm", 6 * NT), ("in_g", 12), ("tr_att", 3 * NT + 1),
         ("q_nope", 5), ("q_pe", NT), ("k_nope", 6), ("v_up", NT + 1), ("tr_qpe", NT),
         ("att", 8 * 11 + 2 * 3 + 4), ("out1", 4 * NT)]

UNITS = [("sample", 0), ("sample", 1), ("sample", 2), ("sample", 3), ("prompt", 0),
         ("sample", 4), ("sample", 5), ("sample", 6), ("sample", 7), ("prompt", 4)]


def fill_starts(fills):
    start, at = {}, 0
    for name, n in fills:
        start[name] = at
        at += n
    return start


GATE_UNITS = (4, 6)


def unit_fills(at):
    table = [None] * len(UNITS)
    order = [("s", 0)]
    for u in range(len(UNITS)):
        order += ([("s", u + 1)] if u + 1 < len(UNITS) else []) + [("t", u), ("p", u)]
    for kind, u in order:
        n = {"s": 5, "t": 5, "p": 1}[kind] if UNITS[u][0] == "sample" else 1
        table[u] = dict(table[u] or {}, **{kind: at})
        at += n
        if kind == "p" and u in GATE_UNITS:
            table[u]["g"] = at
            at += 2
    return table


def spec_mod_fills(at):
    spec, rows, cols = [[], []], [], []
    for n in range(12):
        for o_j in (2 * n, 2 * n + 1):
            spec[o_j // 12].append(at)
            at += 1
        rows.append(at)
        at += 1
        if n >= 1:
            cols.append(at)
            at += 1
    cols.append(at)
    return spec, rows, cols


def inverse_fills(at):
    groups, rows, cols = [], [], []
    for n, tiles in enumerate(GROUPS):
        chains = [(t, d) for t in tiles for d in range(2)]
        g = {"at": at, "tiles": tiles, "chains": chains, "T1": at + 4 * len(tiles), "levels": [], "mod": []}
        at += 4 * len(tiles) + len(chains)
        for _ in LEVELS:
            g["levels"].append(at)
            at += 3 * len(chains)
            if n >= 1:
                g["mod"].append(len(rows))
                rows.append(at)
                cols.append(at + 1)
                at += 2
        groups.append(g)
    return groups, rows, cols


SCAN = [TP, 0, 1, 2, 3]
NORM_ORDER = [TP, 1, 2, 0, 3]


def constants():
    f32 = np.float32
    out = {}
    out["k_ident"] = np.eye(P, dtype=f32)
    e, c = np.arange(P)[:, None], np.arange(P)[None, :]
    out["k_masks"] = np.concatenate([e <= c, e < c, e >= c, e > c], axis=1).astype(f32)
    lvl = []
    for d in range(2):
        first, second = (e, c) if d == 0 else (c, e)
        lvl.append(((first // 2 == second // 2) & (first % 2 == 0) & (second % 2 == 1)).astype(f32))
    for d in range(2):
        for b in LEVELS:
            cols = np.arange(P).reshape(-1, 2, b)[:, d, :].reshape(1, -1)
            rows = np.arange(P)[:, None]
            lvl.append(((rows // (2 * b) == cols // (2 * b)) & ((rows // b) % 2 == 1 - d)).astype(f32))
    out["k_levels"] = np.concatenate(lvl, axis=1)
    for name, n in (("", LS), ("_p", LP)):
        k, t = np.arange(n), np.arange(n)
        ang = 2 * np.pi * ((t[:, None] * k[None, :]) % (2 * n)) / (2 * n)
        alt = 1.0 - 2.0 * (t % 2)
        fc, fs = np.cos(ang), np.sin(ang)
        fs[:, 0] = alt
        out["k_dft" + name] = np.concatenate([fc, fs], axis=1).astype(f32)
        wgt = np.full((n, 1), 2.0 / (2 * n))
        wgt[0] = 1.0 / (2 * n)
        out["k_idft" + name] = np.concatenate([fc.T * wgt, fs.T * wgt], axis=0).astype(f32)
        tt = np.linspace(0.0, 1.0, n, dtype=f32)[:, None]
        wpos = (f32(2.0 * math.pi) * np.arange(n, dtype=f32)[:, None] / f32(n)).astype(f32)
        f = np.linspace(1e-4, 15, 16, dtype=f32)[None, :]
        out["k_pos" + name] = np.ascontiguousarray(
            np.concatenate([tt, np.cos(f * wpos), -np.sin(f * wpos)], axis=-1).astype(f32).T)
        deltas = np.abs(np.linspace(math.log(1e-2) / 1.5, math.log(1e-2) / 0.3, CH, dtype=f32))
        out["k_window" + name] = np.exp(-tt * deltas[None, :]).astype(f32)
    out["k_alt"] = (1.0 - 2.0 * (np.arange(P) % 2)).astype(f32)[:, None]
    pos = np.arange(LS)
    parts = []
    for width in (128, ROPE):
        r = width // 2
        half = r // 2
        inv = (10000.0 ** (-np.arange(half, dtype=f32) * 2.0 / r)).astype(f32)
        cs, sn = [], []
        for where in (pos // 64, pos % 64):
            a = (where.astype(f32)[:, None] * inv[None, :]).astype(f32)
            cs += [np.cos(a), np.cos(a)]
            sn += [-np.sin(a), np.sin(a)]
        parts += cs + sn
    out["k_rope"] = np.concatenate(parts, axis=1).astype(f32)
    return out


def program(nc, a, out, consts):
    start = fill_starts(FILLS)
    ctx = ExitStack()
    with ctx:
        def sb(name, shape, dt=F32):
            return ctx.enter_context(nc.sbuf_tensor(name, shape, dt))

        def sem(name):
            return ctx.enter_context(nc.semaphore(name))

        ps = ctx.enter_context(nc.psum_tensor("ps", [P, BANKS, 512], F32))
        ctx.enter_context(nc.allow_non_contiguous_dma("small parameter vectors"))

        hT = sb("hT", [P, KD, TOK])
        mix = sb("mix", [P, 8, TOK])
        wring = sb("wring", [P, WSLOTS, KD, WC])
        xreg = sb("xreg", [P, 2 * 4 * CMW])
        pad = sb("pad", [P, 2, ZPAD])
        ident = sb("ident", [P, P])
        ones = sb("ones", [P, P])
        masks = sb("masks", [P, 4 * P])
        vec1 = sb("vec1", [P, 99])
        vec2 = sb("vec2", [P, 108])
        modc_l = [sb(f"modc{n}", [P, 24, 2]) for n in range(2)]
        acol_l = [sb(f"acol{n}", [P, KD, 2]) for n in range(2)]
        gcol_l = [sb(f"gcol{n}", [P, KD, 2]) for n in range(2)]
        scond = sb("scond", [P, KD, 2])
        stat = sb("stat", [P, 2, 4 * NT])
        yst = sb("yst", [P, 2, NT])
        ostat = sb("ostat", [P, 2, NT, 8])
        smax = sb("smax", [P, 2, 2, 4])
        ssum = sb("ssum", [P, 2, 2, 4])
        nmax = sb("nmax", [P, 2, 4])
        rsum = sb("rsum", [P, 2, 4])
        abw = sb("abw", [P, KD, 16])
        dtb, alog = sb("dtb", [P, 8])[:, :], sb("alog", [P, 8])[:, :]
        eps = sb("eps", [P, 3])
        phase = sb("phase", [P, 28704])

        def view(at, *shape):
            n = int(np.prod(shape))
            v = phase[:, at:at + n]
            if len(shape) == 1:
                return v
            names = "abcd"[:len(shape)]
            return v.rearrange(f"p ({' '.join(names)}) -> p {' '.join(names)}",
                               **{k: s for k, s in zip(names, shape)})

        x = xreg[:, 0:NT * D].rearrange("p (t d) -> p t d", t=NT)
        cm = xreg[:, :].rearrange("p (s m c) -> p s m c", s=2, m=4)

        dft, idft = view(0, 4, 1024), view(4096, 8, 512)
        dft_p, idft_p = view(8192, 256), view(8448, 2, 128)
        specP = [view(8704 + 6144 * o, NT, 512) for o in range(2)]
        specQ = [view(8704 + 6144 * o + 2560, NT, 512) for o in range(2)]
        specX = [view(8704 + 6144 * o + 5120, 2, 512) for o in range(2)]
        hy_v, hy_x1, hy_x2 = view(20992, NT, 512), view(23552, NT, 512), view(26112, 4, CMW)
        plus = [view(20992, NT, 512), hT[:, 0:4, :].rearrange("p k n -> p (k n)").rearrange("p (t n) -> p t n", t=NT)]
        minus = [view(23552, NT, 512), hT[:, 4:8, :].rearrange("p k n -> p (k n)").rearrange("p (t n) -> p t n", t=NT)]
        pflat = pad[:, :, :].rearrange("p s n -> p (s n)")
        mflat = mix[:, :, :].rearrange("p k n -> p (k n)")
        sqs = pflat[:, 0:D]
        sqs_l = [view(20992, D), sqs]
        modrow = pflat[:, 0:512].rearrange("p (s n) -> p s n", s=2)
        window = mflat[:, 0:NT * 512].rearrange("p (t n) -> p t n", t=NT)
        w3 = mflat[:, 2560:2560 + 2048].rearrange("p (o s c) -> p o s c", o=2, s=2)
        wflat = wring[:, WSLOTS - 1, :, :].rearrange("p k c -> p (k c)")
        rows = view(26120, 256)
        film_w = view(26376, 264)
        h2, turns, turns_f = view(26640, TOK), view(27280, TOK), view(27920, TOK)
        YP = xreg[:, 0:NT * 512].rearrange("p (t n) -> p t n", t=NT)
        YQ = xreg[:, NT * 512:2 * NT * 512].rearrange("p (t n) -> p t n", t=NT)

        q_tm, k_tm, v_tm = view(0, NT, 512), view(2560, NT, 512), view(5120, NT, 512)
        qT, kT = view(7680, H, TOK), view(10240, H, TOK)
        v_cm = view(12800, 4, CMW)
        Uinv = view(12800, 2 * NT, 512)
        intraT = view(17920, 2 * NT, 512)
        o_acc = view(23040, NT, 512)
        levels = view(25600, 1024)
        ab = view(26752, NT, 16)
        gsm = view(26832, 14, NT, 8)
        kd = view(27408, 2, 512)
        xs = xreg[:, :]
        hflat = hT[:, :, :].rearrange("p k n -> p (k n)")
        Tinv = [m[:, 0:1024].rearrange("p (d n) -> p d n", d=2) for m in (xs, hflat)]
        LT = [m[:, 1024:2048].rearrange("p (d n) -> p d n", d=2) for m in (xs, hflat)]
        dec = [m[:, 2048:3072].rearrange("p (d n) -> p d n", d=2) for m in (xs, hflat)]
        Xl = [m[:, 3072:3584].rearrange("p (d n) -> p d n", d=2) for m in (xs, hflat)]
        gm = [m[:, 3584:4608].rearrange("p (d n) -> p d n", d=2) for m in (xs, hflat)]
        rr, vn, S, Sp = Tinv[0], LT[0], dec[0], gm[0]
        diag0 = hflat[:, 0:2048].rearrange("p (n c) -> p n c", c=P)
        y = view(0, NT, D)
        gb_l = [view(12800, 2, D), view(17152, 2, D)]
        diag1 = view(5120, 8, P)

        xn = view(23040, NT, D)
        ztm, v_all = view(0, NT, 5, WC), view(6400, NT + 1, WC)
        rope, g_rows = view(7936, TS, 384), view(9472, 3, P)
        q_up, kv_up = view(9856, 2, 768), view(11392, 1024)
        c_k, c_ckv, c_kpe = view(12416, 2 * P), view(12672, P), view(12800, ROPE)
        oq, ok = view(13056, H, TOK), view(15616, 2, TOK + P)
        mqT, ckvT = view(17152, 2, TOK), view(18432, TOK + P)
        qnT, qpT = view(19200, H, TOK), view(21760, H, TOK)
        qpe, knT = view(24320, NT, WC), view(25600, H, TOK + P)
        vm, kpT = hflat[:, 0:3072].rearrange("p (t n) -> p t n", t=NT + 1), hflat[:, 3072:3072 + TOK + P]
        prob = [view(0, H, 640), view(2560, H, 640)]
        probT = [view(7936, NT, 512), view(10496, NT, 512)]
        GA, GE, GS, BE, CS, EG, NEG, TOT, KDF, GL, T0, T1, T2, T3 = range(14)

        bank_full = [sem(f"bank_full{b}") for b in range(BANKS)]
        bank_free = [sem(f"bank_free{b}") for b in range(BANKS)]
        w_landed = [sem(f"w_landed{s}") for s in range(WSLOTS)]
        dve_step, act_step, pool_step = sem("dve_step"), sem("act_step"), sem("pool_step")
        rows_in, film_in, tap_in, dft_in, idft_in, x_in, xback_in, gdn_in, ab_in, state_in = (sem(n) for n in (
            "rows_in", "film_in", "tap_in", "dft_in", "idft_in", "x_in", "xback_in", "gdn_in", "ab_in", "state_in"))
        const_ok = sem("const_ok")
        vec_ready, arg_ready, sin_ready, scond_ready = (sem(n) for n in (
            "vec_ready", "arg_ready", "sin_ready", "scond_ready"))
        h2_ready, w3_ready, taps_ready = (sem(n) for n in ("h2_ready", "w3_ready", "taps_ready"))
        prestat_ready, pad_zero, acol_ready, sq_ready, rstd_ready, xn_ready, hT_ready = (sem(n) for n in (
            "prestat_ready", "pad_zero", "acol_ready", "sq_ready", "rstd_ready", "xn_ready", "hT_ready"))
        gates_ready, pad_ready, conv_ready, cm_ready, tm_ready = (sem(n) for n in (
            "gates_ready", "pad_ready", "conv_ready", "cm_ready", "tm_ready"))
        Y_ready, z1_ready, hy_done = (sem(n) for n in ("Y_ready", "z1_ready", "hy_done"))
        ab_copied, g_chain, g_act, g_ready, gmask_ready, scal_ready = (sem(n) for n in (
            "ab_copied", "g_chain", "g_act", "g_ready", "gmask_ready", "scal_ready"))
        sq2_ready, ss_ready, rinv_ready, normed, back_ready = (sem(n) for n in (
            "sq2_ready", "ss_ready", "rinv_ready", "normed", "back_ready"))
        diff_ready, expd, masked, LT_ready, intra_ready, U1_ready, T_ready, U_ready, X_ready = (sem(n) for n in (
            "diff_ready", "expd", "masked", "LT_ready", "intra_ready", "U1_ready", "T_ready", "U_ready", "X_ready"))
        kd_ready, r_ready, vn_ready, S_ready, o_ready = (sem(n) for n in (
            "kd_ready", "r_ready", "vn_ready", "S_ready", "o_ready"))
        osq_ready, oss_ready, orstd_ready, on_ready, mix_ready = (sem(n) for n in (
            "osq_ready", "oss_ready", "orstd_ready", "on_ready", "mix_ready"))
        odd_in, z_ready, osum_ready, oinv_ready, onorm_ready, qpe_ready, cache_out, max_ready, exp_ready, prob_ready = (
            sem(n) for n in ("odd_in", "z_ready", "osum_ready", "oinv_ready", "onorm_ready", "qpe_ready", "cache_out",
                             "max_ready", "exp_ready", "prob_ready"))
        diag_ready, gb_ready, y_ready, ysq_ready, yrstd_ready, ys_ready, x_ready = (sem(n) for n in (
            "diag_ready", "gb_ready", "y_ready", "ysq_ready", "yrstd_ready", "ys_ready", "x_ready"))
        stored = sem("stored")

        spec_f, mod_rows0, mod_cols0 = spec_mod_fills(start["spec_mod"])
        inv_groups, mod_rows1, mod_cols1 = inverse_fills(start["inv"])
        units = unit_fills(start["att"])
        last_tr = [g["levels"][-1] + 3 * len(g["chains"]) - 1 for g in inv_groups]

        def bank(f):
            return ps[:, f % BANKS, :]

        def wait_full(eng, f):
            eng.wait_ge(bank_full[f % BANKS], f // BANKS + 1)

        def wait_free(eng, f):
            if f >= BANKS:
                eng.wait_ge(bank_free[f % BANKS], f // BANKS)

        def wait_drained(eng, f):
            eng.wait_ge(bank_free[f % BANKS], f // BANKS + 1)

        def full(f):
            return bank_full[f % BANKS]

        def free(f):
            return bank_free[f % BANKS]

        def wchunk(i):
            return wring[:, i % WSLOTS, :, :]

        def wait_chunk(eng, i):
            eng.wait_ge(w_landed[i % WSLOTS], 16 * (i // WSLOTS + 1))

        def toks(t):
            return slice(t * P, t * P + P)

        def cols(t):
            return slice(t * P, t * P + P) if t < TS else slice(CMP, CMP + P)

        def halves(ap, b):
            return ap.rearrange("p (h n two b) -> p h n two b", h=H, two=2, b=b)

        def chunk_list():
            lst = []
            mod = a["mod_w"]
            even, odd = a["even_in_w"][0], a["odd_in_w"][0]
            for j in range(12):
                lst.append((mod[0], WC * j, WC, mod_rows0[j]))
            for n, c0 in enumerate((HG0, HV0, HX10, HX20)):
                for j in range(2):
                    lst.append((even, c0 + WC * j, WC, start["in_hy"] + 3 * (2 * n + j) + 2))
            for n, c0 in enumerate((Q0, K0, V0)):
                for j in range(2):
                    lst.append((even, c0 + WC * j, WC, start["in_qkv"] + 3 * (2 * n + j) + 2))
            for j in range(2):
                lst.append((even, ZG0 + WC * j, WC, start[f"in_z{j}"] + 2))
            for j in range(12):
                lst.append((mod[1], WC * j, WC, mod_rows1[j]))
            for j in range(4):
                lst.append((a["even_out_w"][0], WC * j, WC, start["out0"] + NT * j + NT - 1))
            for n, c0 in enumerate((GQ0, GQ0 + WC, GK0, GK0 + WC, MQ0, MQ0 + WC)):
                lst.append((odd, c0, WC if n < 5 else RKV + ROPE, start["in_tm"] + NT * n + NT - 1))
            for j, c0 in enumerate((GG0, GG0 + WC, MG0, MG0 + WC)):
                lst.append((odd, c0, WC, start["in_g"] + 3 * j + 2))
            for j in range(4):
                lst.append((a["odd_out_w"][0], WC * j, WC, start["out1"] + NT * j + NT - 1))
            return lst

        chunks = chunk_list()
        chunk_of = {}
        for i, ch in enumerate(chunks):
            chunk_of[ch[3]] = i

        block = ctx.enter_context(nc.Block())

        @block.sync
        def _(sp):
            w1, w2 = a["hyena_ffn_w1"][0], a["hyena_ffn_w2"][0]
            sp.dma_start(film_w[0:33, 0:128].rearrange("k (r c) -> k r c", r=2),
                         w1.unsqueeze(1).broadcast_to([33, 2, 64])).then_inc(film_in, 16)
            sp.dma_start(wflat[0:33, 0:LS], consts["k_pos"]).then_inc(film_in, 16)
            sp.dma_start(wflat[0:33, LS:TOK], consts["k_pos_p"]).then_inc(film_in, 16)
            for half in range(2):
                at = slice(64 * half, 64 * half + 64)
                sp.dma_start(film_w[at, 256:257], a["hyena_ffn_b1"][0].rearrange("(c o) -> c o", o=1))\
                  .then_inc(film_in, 16)
                sp.dma_start(film_w[at, 257:258], a["hyena_ffn_b2"][0].rearrange("(c o) -> c o", o=1))\
                  .then_inc(film_in, 16)
                sp.dma_start(film_w[at, 258:260], a["hyena_sin_freq"][0].rearrange("l c -> c l")).then_inc(film_in, 16)
            sp.dma_start(film_w[0:64, 128:256].rearrange("k (r c) -> k r c", r=2),
                         w2.unsqueeze(1).broadcast_to([64, 2, 64])).then_inc(film_in, 16)
            w3_in = a["hyena_ffn_w3"][0].rearrange("k (o s c) -> k o s c", o=2, s=2)
            for half in range(2):
                for sign in range(2):
                    sp.dma_start(w3[64 * half:64 * half + 64, :, sign, :], w3_in[:, :, half, :]).then_inc(tap_in, 16)
            sp.dma_start(window[:, 0:TS, :], consts["k_window"].rearrange("(t p) n -> p t n", p=P)).then_inc(tap_in, 16)
            sp.dma_start(window[:, TP, :], consts["k_window_p"]).then_inc(tap_in, 16)
            sp.dma_start(wflat[0:1, 1024:2048], a["hyena_bias"].rearrange("l o c -> l (o c)")).then_inc(tap_in, 16)
            sp.dma_start(film_w[:, 260:261], consts["k_alt"]).then_inc(tap_in, 16)
            sp.dma_start(dft, consts["k_dft"].rearrange("(t p) n -> p t n", p=P)).then_inc(dft_in, 16)
            sp.dma_start(dft_p, consts["k_dft_p"]).then_inc(dft_in, 16)
            sp.dma_start(x[:, 0:TS, :], a["x_sample"][0].rearrange("(t p) d -> p t d", p=P)).then_inc(x_in, 16)
            sp.dma_start(x[:, TP, :], a["x_prompt"][0]).then_inc(x_in, 16)
            for i, (w, c0, n, last) in enumerate(chunks):
                if i == WSLOTS - 1:
                    sp.wait_ge(taps_ready, 4)
                if i >= WSLOTS:
                    wait_full(sp, chunks[i - WSLOTS][3])
                sp.dma_start(wchunk(i)[:, :, 0:n], w[:, c0:c0 + n].rearrange("(k p) n -> p k n", p=P))\
                  .then_inc(w_landed[i % WSLOTS], 16)

        @block.gpsimd
        def _(pool):
            steps = [0]

            def chained(ins):
                steps[0] += 1
                ins.then_inc(pool_step, 1)
                pool.wait_ge(pool_step, steps[0])

            nc.gpsimd.memset(ones[:, :], 1.0).then_inc(const_ok, 1)
            nc.gpsimd.memset(eps[:, 0:1], EPS).then_inc(const_ok, 1)
            nc.gpsimd.memset(eps[:, 1:2], EPS * P).then_inc(const_ok, 1)
            chained(nc.gpsimd.memset(eps[:, 2:3], -0.5))
            pool.dma_start(idft, consts["k_idft"].rearrange("(t p) n -> p t n", p=P)).then_inc(idft_in, 16)
            pool.dma_start(idft_p, consts["k_idft_p"].rearrange("(t p) n -> p t n", p=P)).then_inc(idft_in, 16)
            pool.dma_start(masks[:, :], consts["k_masks"]).then_inc(idft_in, 16)
            pool.dma_start(abw[:, :, :], a["even_in_w"][0][:, AB0:AB0 + 16].rearrange("(k p) n -> p k n", p=P))\
                .then_inc(ab_in, 16)
            pool.dma_start(dtb, a["gdn_dt_bias"].rearrange("l a b -> l (a b)").broadcast_to([P, 8])).then_inc(ab_in, 16)
            pool.dma_start(alog, a["gdn_a_log"].rearrange("l a b -> l (a b)").broadcast_to([P, 8])).then_inc(ab_in, 16)

            pool.wait_ge(tap_in, 16 * 8)
            nc.gpsimd.tensor_scalar(w3[64:128, :, 1, :], w3[64:128, :, 1, :], -1.0, None, ALU.mult)                .then_inc(w3_ready, 1)

            def inverse_roots(dst, src, n, ready):
                chained(nc.gpsimd.tensor_scalar(src, src, 1.0 / n, EPS, ALU.mult, ALU.add))
                nc.gpsimd.tensor_tensor(dst, src, eps[:, 2:3].broadcast_to([P, src.shape[1]]), ALU.pow)\
                    .then_inc(ready, 1)

            for t in range(NT):
                pool.wait_ge(sq_ready, t + 1)
                inverse_roots(stat[:, 1, t:t + 1], stat[:, 0, t:t + 1], D, rstd_ready)

            wait_full(pool, start["fft1"] + 14)
            pool.wait_ge(hy_done, 5)
            pool.dma_start(levels, consts["k_levels"]).then_inc(gdn_in, 16)
            nc.gpsimd.memset(o_acc, 0.0).then_inc(gmask_ready, 1)

            for n, src in enumerate((q_tm, k_tm)):
                for t in range(NT):
                    i = NT * n + t
                    wait_drained(pool, start["tr_q"] + i)
                    if i >= 2:
                        pool.wait_ge(ss_ready, i - 1)
                    nc.gpsimd.tensor_tensor(pflat[:, (i % 2) * 512:(i % 2) * 512 + 512], src[:, t, :], src[:, t, :],
                                            ALU.mult).then_inc(sq2_ready, 1)
            pool.wait_ge(g_ready, 1)
            pool.wait_ge(idft_in, 48)
            pool.wait_ge(gdn_in, 16)
            wait_full(pool, start["in_z1"] + 2)
            at_chain = 0
            for g, group in enumerate(inv_groups):
                if g >= 1:
                    wait_full(pool, last_tr[g - 1])
                for t, d in group["chains"]:
                    nc.gpsimd.tensor_tensor(
                        gm[t % 2][:, d, :].rearrange("p (h c) -> p h c", h=H),
                        masks[:, 2 * d * P:2 * d * P + P].unsqueeze(1).broadcast_to([P, H, P]),
                        gsm[:, GE, t, 4 * d:4 * d + 4].unsqueeze(2).broadcast_to([P, H, P]),
                        ALU.mult).then_inc(gmask_ready, 1)
                for n, (t, d) in enumerate(group["chains"]):
                    pool.wait_ge(expd, at_chain + n + 1)
                    m_incl = masks[:, 2 * d * P:2 * d * P + P].unsqueeze(1).broadcast_to([P, H, P])
                    m_strict = masks[:, (2 * d + 1) * P:(2 * d + 2) * P].unsqueeze(1).broadcast_to([P, H, P])
                    dv = dec[t % 2][:, d, :].rearrange("p (h c) -> p h c", h=H)
                    nc.gpsimd.tensor_tensor(intraT[:, 2 * t + d, :].rearrange("p (h c) -> p h c", h=H), dv, m_incl,
                                            ALU.mult).then_inc(masked, 1)
                    nc.gpsimd.tensor_tensor(dv, dv, m_strict, ALU.mult).then_inc(masked, 1)
                for n, (t, d) in enumerate(group["chains"]):
                    if d == 0:
                        pool.wait_ge(LT_ready, t + 1)
                    else:
                        wait_drained(pool, group["at"] + 4 * (n // 2))
                    m0 = levels[:, d * P:d * P + P].unsqueeze(1).broadcast_to([P, H, P])
                    Uv = Uinv[:, 2 * t + d, :].rearrange("p (h c) -> p h c", h=H)
                    chained(nc.gpsimd.tensor_tensor(Uv, LT[t % 2][:, d, :].rearrange("p (h c) -> p h c", h=H), m0,
                                                    ALU.mult))
                    nc.gpsimd.tensor_tensor(Uv, ident[:, :].unsqueeze(1).broadcast_to([P, H, P]), Uv,
                                            ALU.subtract).then_inc(U1_ready, 1)
                at_chain += len(group["chains"])
            pool.wait_ge(normed, 2 * NT)
            pool.wait_ge(g_act, 2)
            def root_heads(n):
                pool.wait_ge(oss_ready, n + 1)
                st = slice(4 * NORM_ORDER[n], 4 * NORM_ORDER[n] + 4)
                inverse_roots(stat[:, 1, st], stat[:, 0, st], P, orstd_ready)

            for i, s in enumerate(SCAN):
                for d in range(2):
                    t = s if d == 0 or s == TP else TS - 1 - s
                    if i >= 1:
                        wait_full(pool, start["scan"] + 10 * (i - 1) + 6 + d)
                    nc.gpsimd.tensor_tensor(kd[:, d, :].rearrange("p (h c) -> p h c", h=H),
                                            k_tm[:, t, :].rearrange("p (h c) -> p h c", h=H),
                                            gsm[:, KDF, t, 4 * d:4 * d + 4].unsqueeze(2).broadcast_to([P, H, P]),
                                            ALU.mult).then_inc(kd_ready, 1)
                if i == 0:
                    wait_full(pool, last_tr[-1])
                    for n in range(2 * KD):
                        nc.gpsimd.tensor_tensor(diag0[:, n, :], ident[:, :],
                                                gcol_l[0][:, n % KD, n // KD:n // KD + 1].broadcast_to([P, P]),
                                                ALU.mult).then_inc(diag_ready, 1)
                if i == 2:
                    root_heads(0)
                if i == 1:
                    wait_drained(pool, start["scan"] + 7)
                    for n, nm in enumerate(("new_gdn_fwd", "new_gdn_bwd")):
                        pool.dma_start(out[nm][0, 0].rearrange("h k v -> k h v"),
                                       Sp[:, n, :].rearrange("p (h v) -> p h v", h=H)).then_inc(stored, 16)
            wait_drained(pool, start["scan"] + 10 * NT - 3)
            wait_full(pool, start["scan"] + 10 * NT - 1)
            pool.wait_ge(stored, 32)
            pool.dma_start(x[:, 0:TS, :], a["x_sample"][0].rearrange("(t p) d -> p t d", p=P)).then_inc(xback_in, 16)
            pool.dma_start(x[:, TP, :], a["x_prompt"][0]).then_inc(xback_in, 16)
            for n in range(1, NT):
                root_heads(n)
            for t in range(NT + 1):
                if t < NT:
                    pool.wait_ge(ysq_ready, t + 1)
                    inverse_roots(yst[:, 1, t:t + 1], yst[:, 0, t:t + 1], D, yrstd_ready)
                if t >= 1:
                    pool.wait_ge(sq_ready, NT + t)
                    inverse_roots(stat[:, 1, t - 1:t], stat[:, 0, t - 1:t], D, rstd_ready)

            pool.wait_ge(x_ready, NT)
            pool.dma_start(v_all[:, NT, :], a["cache_gqa_v"][0, 0].rearrange("t h d -> t (h d)")).then_inc(odd_in, 16)
            pool.dma_start(rope, consts["k_rope"].rearrange("(t p) n -> p t n", p=P)).then_inc(odd_in, 16)
            for n, nm in enumerate(("gqa_q_norm_g", "gqa_k_norm_g", "mla_kv_norm_g")):
                pool.dma_start(g_rows[:, n, :], a[nm].broadcast_to([P, P])).then_inc(odd_in, 16)
            pool.dma_start(q_up, a["mla_q_up"][0].rearrange("(k p) n -> p k n", p=P)).then_inc(odd_in, 16)
            pool.dma_start(kv_up, a["mla_kv_up"][0]).then_inc(odd_in, 16)
            pool.dma_start(c_k, a["cache_gqa_k"][0, 0].rearrange("t h d -> t (h d)")).then_inc(odd_in, 16)
            pool.dma_start(c_ckv, a["cache_mla_ckv"][0, 0]).then_inc(odd_in, 16)
            pool.dma_start(c_kpe, a["cache_mla_kpe"][0, 0]).then_inc(odd_in, 16)
            pool.wait_ge(onorm_ready, NT)
            wait_drained(pool, start["in_tm"] + 6 * NT - 1)
            pool.dma_start(out["new_gqa_k"][0, 0].rearrange("t h d -> t (h d)"), ztm[:, TP, 2, :]).then_inc(stored, 16)
            pool.dma_start(out["new_gqa_v"][0, 0].rearrange("t h d -> t (h d)"), v_all[:, TP, :]).then_inc(stored, 16)
            pool.dma_start(out["new_mla_ckv"][0, 0], ztm[:, TP, 4, 0:RKV]).then_inc(stored, 16)
            pool.dma_start(out["new_mla_kpe"][0, 0], ztm[:, TP, 4, RKV:RKV + ROPE]).then_inc(stored, 16)
            pool.wait_ge(stored, 96)
            nc.gpsimd.memset(rsum[:, :, :], 0.0).then_inc(cache_out, 1)
            pool.wait_ge(acol_ready, 4)
            wait_full(pool, start["tr_att"] + 3 * NT - 1)
            for n in range(2 * KD):
                if n == KD:
                    wait_full(pool, units[GATE_UNITS[0]]["g"] + 1)
                nc.gpsimd.tensor_tensor(diag1[:, n % KD, :], ident[:, :],
                                        gcol_l[1][:, n % KD, n // KD:n // KD + 1].broadcast_to([P, P]),
                                        ALU.mult).then_inc(diag_ready, 1)
            for t in range(NT):
                pool.wait_ge(ysq_ready, NT + t + 1)
                inverse_roots(yst[:, 1, t:t + 1], yst[:, 0, t:t + 1], D, yrstd_ready)
            for t in range(NT):
                pool.wait_ge(x_ready, NT + t + 1)
                dst = out["y_sample"][0, toks(t), :] if t < TS else out["y_prompt"][0]
                pool.dma_start(dst, x[:, t, :]).then_inc(stored, 16)
            pool.wait_ge(stored, 96 + 16 * NT)

        @block.scalar
        def _(act):
            steps = [0]

            def chained(ins):
                steps[0] += 1
                ins.then_inc(act_step, 1)
                act.wait_ge(act_step, steps[0])

            act.dma_start(ident[:, :], consts["k_ident"]).then_inc(rows_in, 16)
            mb = a["mod_b"].rearrange("l (r c) -> (l r) c", c=P)
            r1, r2 = rows[:, 0:128], rows[:, 128:256]
            act.dma_start(r1[0:48, :], mb).then_inc(rows_in, 16)
            act.dma_start(r1[48:64, :], a["pre_norm_g"].rearrange("l (r c) -> (l r) c", c=P)).then_inc(rows_in, 16)
            act.dma_start(r1[64:80, :], a["post_norm_g"].rearrange("l (r c) -> (l r) c", c=P)).then_inc(rows_in, 16)
            act.dma_start(r1[80:88, :], a["c"].rearrange("l (r c) -> (l r) c", c=P)).then_inc(rows_in, 16)
            act.dma_start(r1[88:96, :], a["c_ctx"].rearrange("(r c) -> r c", c=P)).then_inc(rows_in, 16)
            act.dma_start(r1[96:97, :], a["gdn_norm_g"]).then_inc(rows_in, 16)
            act.dma_start(r1[97:99, :], a["mla_q_norm_g"].rearrange("l (r c) -> (l r) c", c=P)).then_inc(rows_in, 16)
            act.dma_start(r2[0:60, :], a["gdn_conv_w"].rearrange("l j (r c) -> (l j r) c", c=P)).then_inc(rows_in, 16)
            act.dma_start(r2[60:96, :], a["hyena_conv_w"].rearrange("l j (r c) -> (l j r) c", c=P))\
                .then_inc(rows_in, 16)
            act.dma_start(r2[96:108, :], a["hyena_conv_b"].rearrange("l (r c) -> (l r) c", c=P)).then_inc(rows_in, 16)
            def square_x(layer, t):
                if layer == 0:
                    act.wait_ge(x_in, 32)
                else:
                    act.wait_ge(x_ready, t + 1)
                if t >= 1 or layer == 1:
                    act.wait_ge(sq_ready, NT * layer + t)
                nc.scalar.activation(sqs_l[layer], x[:, t, :], ACT.Square, accum_out=stat[:, 0, t:t + 1])                    .then_inc(sq_ready, 1)

            for layer in range(2):
                act.wait_ge(arg_ready, layer + 1)
                nc.scalar.activation(h2, h2, ACT.Sin).then_inc(sin_ready, 1)
            f = start["vectors"]
            wait_full(act, f)
            nc.scalar.activation(vec1[:, :], bank(f)[:, 0:99], ACT.Copy).then_inc(free(f), 1)
            wait_full(act, f + 1)
            nc.scalar.activation(vec2[:, :], bank(f + 1)[:, 0:108], ACT.Copy).then_inc(free(f + 1), 1)
            wait_drained(act, f + 1)
            nc.scalar.activation(scond[:, :, 0], vec1[:, 80:88], ACT.Silu).then_inc(scond_ready, 1)
            nc.scalar.activation(scond[:, :, 1], vec1[:, 88:96], ACT.Silu).then_inc(scond_ready, 1)
            for o in range(2):
                for j in range(12):
                    f = spec_f[o][j]
                    wait_full(act, f)
                    if j < 10:
                        dst = (specP if j % 2 == 0 else specQ)[o][:, j // 2, :]
                        nc.scalar.activation(dst, bank(f), ACT.Copy).then_inc(free(f), 1)
                    else:
                        for p in spec_f[o][8 * (j - 10):8 * (j - 10) + 2]:
                            wait_drained(act, p)
                        t = 0 if j == 10 else TP
                        chained(nc.scalar.activation(specX[o][:, j - 10, :], specP[o][:, t, :], ACT.Copy))
                        nc.scalar.mul(specQ[o][0:1, t, :], specQ[o][0:1, t, :], 0.0)
                        nc.scalar.activation(specX[o][0:1, j - 10, :], bank(f)[0:1, :], ACT.Copy).then_inc(free(f), 1)
                if o == 0:
                    for t in range(NT):
                        square_x(0, t)
            def modulate_x(base, layer, tiles):
                for t in tiles:
                    f = base + 2 * t
                    wait_full(act, f)
                    if t == 0:
                        act.wait_ge(acol_ready, 2 * layer + 2)
                    for k in range(4):
                        c = 0 if t < TS else 1
                        ins = nc.scalar.activation(hT[:, k, toks(t)], bank(f)[:, k * P:k * P + P],
                                                   ACT.Identity, bias=modc_l[layer][:, k, c:c + 1],
                                                   scale=acol_l[layer][:, k, c:c + 1])
                    ins.then_inc(free(f), 1)

            modulate_x(start["hT0"], 0, range(NT))

            def take_gates(f, m0):
                for m in range(2):
                    wait_full(act, f + m)
                    nc.scalar.activation(mix[:, m0 + m, 0:LS], bank(f + m), ACT.Silu).then_inc(free(f + m), 1)
                wait_full(act, f + 2)
                nc.scalar.activation(mix[:, m0:m0 + 2, LS:TOK],
                                     bank(f + 2)[:, 0:2 * P].rearrange("p (m n) -> p m n", m=2), ACT.Silu)\
                    .then_inc(free(f + 2), 1)

            def take_rows(f, n):
                if n == 6:
                    act.wait_ge(pad_zero, 2)
                if n >= 1:
                    act.wait_ge(conv_ready, 2 * n)
                else:
                    act.wait_ge(pad_zero, 1)
                for m in range(2):
                    wait_full(act, f + m)
                    nc.scalar.activation(pad[:, m, 2:2 + LS], bank(f + m), ACT.Copy).then_inc(free(f + m), 1)
                wait_full(act, f + 2)
                nc.scalar.activation(pad[:, :, LS + 6:LS + 6 + LP],
                                     bank(f + 2)[:, 0:2 * P].rearrange("p (m n) -> p m n", m=2), ACT.Copy)\
                    .then_inc(free(f + 2), 1)

            for j in range(2):
                take_gates(start["in_hy"] + 3 * j, 4 + 2 * j)
            for j in range(6):
                take_rows(start["in_hy"] + 6 + 3 * j, j)
            act.wait_ge(g_chain, 1)
            act.wait_ge(ab_in, 48)
            chained(nc.scalar.activation(gsm[:, T1, :, :], gsm[:, T1, :, :], ACT.Exp))
            nc.scalar.activation(gsm[:, T1, :, :], gsm[:, T1, :, :], ACT.Ln, bias=1.0)
            nc.scalar.activation(alog, alog, ACT.Exp)
            nc.scalar.activation(gsm[:, BE, :, :], ab[:, :, 8:16], ACT.Exp, scale=-1.0).then_inc(g_act, 1)

            def silu_rows(dst, n):
                for m in range(4):
                    act.wait_ge(conv_ready, n + m + 1)
                    nc.scalar.activation(dst[:, m, :], dst[:, m, :], ACT.Silu).then_inc(cm_ready, 1)

            for n, dst in enumerate((cm[:, 0, :, :], cm[:, 1, :, :], v_cm)):
                for j in range(2):
                    take_rows(start["in_qkv"] + 3 * (2 * n + j), 6 + 2 * n + j)
                silu_rows(dst, 12 + 4 * n)
            act.wait_ge(scal_ready, 1)
            nc.scalar.activation(gsm[:, EG, :, :], gsm[:, CS, :, :], ACT.Exp)
            nc.scalar.activation(gsm[:, GL, :, :], gsm[:, TOT, :, :], ACT.Exp)
            nc.scalar.activation(gsm[:, KDF, :, :], gsm[:, KDF, :, :], ACT.Exp).then_inc(g_act, 1)
            take_gates(start["in_z0"], 0)
            for n, dst in enumerate((q_tm, k_tm)):
                for t in range(NT):
                    f = start["tr_q"] + NT * n + t
                    wait_full(act, f)
                    nc.scalar.activation(dst[:, t, :], bank(f), ACT.Copy).then_inc(free(f), 1)
            act.wait_ge(ss_ready, 2 * NT)
            act.wait_ge(const_ok, 3)
            chained(nc.scalar.activation(stat[:, 1, :], stat[:, 0, :], ACT.Ln, scale=float(P), bias=eps[:, 1:2]))
            chained(nc.scalar.activation(gsm[:, T3, :, 0:4], gsm[:, T3, :, 0:4], ACT.Ln, bias=eps[:, 0:1]))
            nc.scalar.activation(stat[:, 1, :], stat[:, 1, :], ACT.Exp, scale=-0.5)
            nc.scalar.activation(gsm[:, T3, :, 0:4], gsm[:, T3, :, 0:4], ACT.Exp, scale=-0.5).then_inc(rinv_ready, 1)
            take_gates(start["in_z1"], 2)
            for t in range(NT):
                for n, dst in enumerate((qT, kT)):
                    f = start["back"] + 2 * t + n
                    wait_full(act, f)
                    nc.scalar.activation(dst[:, :, toks(t)], bank(f).rearrange("p (h c) -> p h c", h=H), ACT.Copy)\
                        .then_inc(free(f), 1)
            for g in inv_groups:
                nc_ = len(g["chains"])
                for n, (t, d) in enumerate(g["chains"]):
                    wait_drained(act, g["at"] + 4 * (n // 2) + 2 + d)
                    nc.scalar.activation(dec[t % 2][:, d, :], dec[t % 2][:, d, :], ACT.Exp).then_inc(expd, 1)
                for n, (t, d) in enumerate(g["chains"]):
                    f = g["T1"] + n
                    wait_full(act, f)
                    nc.scalar.activation(Tinv[t % 2][:, d, :], bank(f), ACT.Copy).then_inc(free(f), 1)
                for l in range(len(LEVELS)):
                    for n, (t, d) in enumerate(g["chains"]):
                        f = g["levels"][l] + 2 * nc_ + n
                        wait_full(act, f)
                        nc.scalar.activation(Uinv[:, 2 * t + d, :], bank(f), ACT.Copy).then_inc(free(f), 1)
            wait_drained(act, last_tr[-1])
            wait_drained(act, inv_groups[-1]["at"])
            for d, nm in enumerate(("state_gdn_fwd", "state_gdn_bwd")):
                act.dma_start(S[:, d, :].rearrange("p (h v) -> p h v", h=H),
                              a[nm][0, 0].rearrange("h k v -> k h v")).then_inc(state_in, 16)
            def square_heads(n):
                t = NORM_ORDER[n]
                step = {TP: 0, 1: 3, 2: 3, 0: 4, 3: 4}[t]
                wait_drained(act, start["scan"] + 10 * step + 9)
                if n >= 2:
                    act.wait_ge(oss_ready, n - 1)
                nc.scalar.activation(pflat[:, (n % 2) * 512:(n % 2) * 512 + 512], o_acc[:, t, :], ACT.Square)\
                    .then_inc(osq_ready, 1)

            for n in range(NT):
                square_heads(n)

            def take_gate_rows(f0, n, layer):
                for i in range(n, n + 2):
                    f = f0 + i - n
                    wait_full(act, f)
                    nc.scalar.activation(gb_l[layer][:, i // 2, (i % 2) * 512:(i % 2) * 512 + 512], bank(f), ACT.Copy)\
                        .then_inc(free(f), 1)

            take_gate_rows(start["gate0"], 0, 0)
            take_gate_rows(start["gate0"] + 2, 2, 0)

            def take_output(layer):
                for j in range(4):
                    for t in range(NT):
                        f = start[f"out{layer}"] + NT * j + t
                        wait_full(act, f)
                        nc.scalar.activation(y[:, t, WC * j:WC * j + WC], bank(f)[:, 0:WC], ACT.Copy)                            .then_inc(free(f), 1)
                        if j == 3:
                            wait_drained(act, f)
                            if t >= 1:
                                act.wait_ge(ysq_ready, NT * layer + t)
                            if t >= 2 and layer == 0:
                                act.wait_ge(sq_ready, NT + t - 1)
                            nc.scalar.activation(sqs, y[:, t, :], ACT.Square, accum_out=yst[:, 0, t:t + 1])                                .then_inc(ysq_ready, 1)
                            if t >= 1 and layer == 0:
                                act.wait_ge(ysq_ready, t + 1)
                                square_x(1, t - 1)

            take_output(0)

            modulate_x(start["hT1"], 1, range(0, 1))
            square_x(1, NT - 1)
            modulate_x(start["hT1"], 1, range(1, NT))
            for j in range(6):
                for t in range(NT):
                    f = start["in_tm"] + NT * j + t
                    n = WC if j < 5 else RKV + ROPE
                    dst = v_all[:, t, :] if j == 3 else ztm[:, t, j - (j > 3), 0:n]
                    wait_full(act, f)
                    nc.scalar.activation(dst, bank(f)[:, 0:n], ACT.Copy).then_inc(free(f), 1)
            wait_drained(act, start["in_tm"] + 6 * NT - 1)
            for t in range(NT):
                z = ztm[:, t, :, :].rearrange("p j c -> p (j c)")
                for n in range(8):
                    lo, w = [(0, P), (P, P), (2 * P, P), (3 * P, P), (4 * P, P), (5 * P, P), (8 * P, P), (6 * P, 2 * P)][n]
                    if n == 0 and t >= 1:
                        act.wait_ge(z_ready, 8 * t)
                    nc.scalar.activation(pflat[:, lo:lo + w], z[:, lo:lo + w], ACT.Square,
                                         accum_out=ostat[:, 0, t, n:n + 1]).then_inc(z_ready, 1)
            act.wait_ge(osum_ready, 1)
            chained(nc.scalar.activation(ostat[:, 1, :, :], ostat[:, 0, :, :], ACT.Ln))
            nc.scalar.activation(ostat[:, 1, :, :], ostat[:, 1, :, :], ACT.Exp, scale=-0.5).then_inc(oinv_ready, 1)
            for j in range(4):
                take_gates(start["in_g"] + 3 * j, 2 * j)
            for t in range(NT + 1):
                f = start["tr_att"] + 3 * t
                if t < NT:
                    wait_full(act, f)
                    nc.scalar.activation(oq[:, :, toks(t)], bank(f).rearrange("p (h c) -> p h c", h=H), ACT.Copy)\
                        .then_inc(free(f), 1)
                    f += 1
                    wait_full(act, f)
                    nc.scalar.activation(ok[:, :, toks(t)], bank(f)[:, 0:2 * P].rearrange("p (h c) -> p h c", h=2),
                                         ACT.Copy)
                    for k in range(2):
                        ins = nc.scalar.activation(mqT[:, k, toks(t)], bank(f)[:, (2 + k) * P:(3 + k) * P], ACT.Copy,
                                                   scale=vec1[:, 97 + k:98 + k])
                    ins.then_inc(free(f), 1)
                    f += 1
                    wait_full(act, f)
                    nc.scalar.activation(ckvT[:, toks(t)], bank(f)[:, 0:P], ACT.Copy)
                    nc.scalar.activation(kpT[0:ROPE, toks(t)], bank(f)[0:ROPE, P:2 * P], ACT.Copy).then_inc(free(f), 1)
                else:
                    wait_full(act, f)
                    nc.scalar.activation(ok[:, :, toks(t)], bank(f)[:, 0:2 * P].rearrange("p (h c) -> p h c", h=2),
                                         ACT.Copy)
                    nc.scalar.activation(ckvT[:, toks(t)], bank(f)[:, 2 * P:3 * P], ACT.Copy)
                    nc.scalar.activation(kpT[0:ROPE, toks(t)], bank(f)[0:ROPE, 3 * P:4 * P], ACT.Copy)\
                        .then_inc(free(f), 1)
            for n, dst in ((0, qnT),):
                for h in range(H):
                    f = start["q_nope"] + h
                    wait_full(act, f)
                    nc.scalar.activation(dst[:, h, 0:LS], bank(f), ACT.Copy).then_inc(free(f), 1)
                f = start["q_nope"] + H
                wait_full(act, f)
                nc.scalar.activation(dst[:, :, LS:TOK], bank(f).rearrange("p (h c) -> p h c", h=H), ACT.Copy)\
                    .then_inc(free(f), 1)
            for t in range(NT):
                f = start["q_pe"] + t
                wait_full(act, f)
                nc.scalar.activation(qpe[:, t, :], bank(f)[:, 0:WC], ACT.Copy).then_inc(free(f), 1)
            for h in range(H):
                f = start["k_nope"] + h
                wait_full(act, f)
                nc.scalar.activation(knT[:, h, 0:LS], bank(f), ACT.Copy).then_inc(free(f), 1)
            for g in range(2):
                f = start["k_nope"] + H + g
                wait_full(act, f)
                nc.scalar.activation(knT[:, 2 * g:2 * g + 2, LS:TOK + P],
                                     bank(f).rearrange("p (h c) -> p h c", h=2), ACT.Copy).then_inc(free(f), 1)
            for t in range(NT + 1):
                f = start["v_up"] + t
                wait_full(act, f)
                nc.scalar.activation(vm[:, t, :], bank(f), ACT.Copy).then_inc(free(f), 1)
            for t in range(NT):
                f = start["tr_qpe"] + t
                wait_full(act, f)
                nc.scalar.activation(qpT[0:ROPE, :, toks(t)], bank(f)[0:ROPE, :].rearrange("p (h c) -> p h c", h=H),
                                     ACT.Copy).then_inc(free(f), 1)
            def exponentials(u):
                kind, h = UNITS[u]
                scale = (P if h < 4 else P + ROPE) ** -0.5
                f = units[u]["s"]
                act.wait_ge(max_ready, u + 1)
                if u >= 2:
                    wait_full(act, units[u - 2]["p"])
                else:
                    act.wait_ge(cache_out, 1)
                for g in range(4):
                    if kind == "sample":
                        ins = nc.scalar.activation(prob[u % 2][:, g, 0:LS], bank(f + g), ACT.Exp, scale=scale,
                                                   bias=nmax[:, u % 2, g:g + 1], accum_out=ssum[:, u % 2, 0, g:g + 1])
                        ins.then_inc(free(f + g), 1)
                    src = bank(f + 4) if kind == "sample" else bank(f)
                    ins = nc.scalar.activation(prob[u % 2][:, g, LS:640] if kind == "sample" else prob[u % 2][:, g, 0:P],
                                               src[:, g * P:g * P + P], ACT.Exp, scale=scale,
                                               bias=nmax[:, u % 2, g:g + 1], accum_out=ssum[:, u % 2, 1, g:g + 1])
                ins.then_inc(free(f + 4 if kind == "sample" else f), 1)

            def take_probT(u):
                kind, h = UNITS[u]
                for k in range(5 if kind == "sample" else 1):
                    f = units[u]["t"] + k
                    wait_full(act, f)
                    nc.scalar.activation(probT[u % 2][:, k, :], bank(f), ACT.Copy).then_inc(free(f), 1)

            exponentials(0)
            for u in range(len(UNITS)):
                if u + 1 < len(UNITS):
                    exponentials(u + 1)
                take_probT(u)
                if u in GATE_UNITS:
                    take_gate_rows(units[u]["g"], 2 * GATE_UNITS.index(u), 1)
            take_output(1)


        @block.tensor
        def _(pe):
            def mm(o, l, r, first=True, last=True):
                return nc.tensor.matmul(o, l, r, start=first, stop=last)

            idn = ident[:, :]

            def spread_gates(f0, ns, diag, ready):
                pe.wait_ge(diag_ready, ready)
                for i, n in enumerate(ns):
                    f = f0 + i
                    wait_free(pe, f)
                    for k in range(4):
                        ins = mm(bank(f)[:, k * P:k * P + P], ones[:, :], diag[:, 4 * (n % (diag.shape[1] // 4)) + k, :])
                    ins.then_inc(full(f), 1)

            pe.wait_ge(film_in, 16 * 10)
            f = start["film"]
            mm(bank(f)[:, 0:LS], film_w[0:33, 0:128], wflat[0:33, 0:LS]).then_inc(full(f), 1)
            mm(bank(f + 1)[:, 0:LP], film_w[0:33, 0:128], wflat[0:33, LS:TOK]).then_inc(full(f + 1), 1)
            pe.wait_ge(sin_ready, 1)
            mm(bank(f + 2)[:, 0:LS], film_w[0:64, 128:256], h2[0:64, 0:LS]).then_inc(full(f + 2), 1)
            mm(bank(f + 3)[:, 0:LP], film_w[0:64, 128:256], h2[0:64, LS:TOK]).then_inc(full(f + 3), 1)
            pe.wait_ge(rows_in, 16 * 11)
            f = start["vectors"]
            nc.tensor.transpose(bank(f)[:, 0:99], rows[0:99, 0:128], ident[0:99, 0:99]).then_inc(full(f), 1)
            nc.tensor.transpose(bank(f + 1)[:, 0:108], rows[0:108, 128:256], ident[0:108, 0:108])\
                .then_inc(full(f + 1), 1)
            pe.wait_ge(h2_ready, 1)
            pe.wait_ge(tap_in, 16 * 8)
            pe.wait_ge(w3_ready, 1)
            for o in range(2):
                for t in range(NT):
                    for s in range(2):
                        f = start[f"filt{o}"] + 2 * t + s
                        wait_free(pe, f)
                        mm(bank(f), h2[:, toks(t)], w3[:, o, s, :]).then_inc(full(f), 1)
            def modulation_rows(j, f):
                i = chunk_of[f]
                wait_chunk(pe, i)
                wait_free(pe, f)
                for k in range(KD):
                    ins = mm(bank(f)[0:2, 0:WC], scond[:, k, :], wchunk(i)[:, k, :], k == 0, k == KD - 1)
                ins.then_inc(full(f), 1)

            def modulation_columns(j, f_rows, f):
                wait_drained(pe, f_rows)
                wait_free(pe, f)
                for m in range(2):
                    ins = nc.tensor.transpose(bank(f)[:, 2 * m:2 * m + 2], modrow[0:2, j % 2, m * P:m * P + P],
                                              ident[0:2, 0:2])
                ins.then_inc(full(f), 1)

            def spectrum(o, j):
                f = spec_f[o][j]
                wait_free(pe, f)
                taps = (plus, minus)[j % 2 if j < 10 else 0][o]
                if j < 8:
                    ft = j // 2
                    for k in range(TS):
                        ins = mm(bank(f), dft[:, k, (j % 2) * 512 + ft * P:(j % 2) * 512 + ft * P + P], taps[:, k, :],
                                 k == 0, k == TS - 1)
                elif j < 10:
                    ins = mm(bank(f), dft_p[:, (j % 2) * P:(j % 2) * P + P], taps[:, TP, :])
                elif j == 10:
                    for k in range(TS):
                        ins = mm(bank(f)[0:1, :], film_w[:, 260:261], taps[:, k, :], k == 0, k == TS - 1)
                else:
                    ins = mm(bank(f)[0:1, :], film_w[:, 260:261], taps[:, TP, :])
                ins.then_inc(full(f), 1)

            pe.wait_ge(dft_in, 32)
            pe.wait_ge(scond_ready, 2)
            for n in range(12):
                pe.wait_ge(taps_ready, 2 * (2 * n // 12 + 1))
                spectrum(2 * n // 12, 2 * n % 12)
                spectrum(2 * n // 12, 2 * n % 12 + 1)
                modulation_rows(n, mod_rows0[n])
                if n >= 1:
                    modulation_columns(n - 1, mod_rows0[n - 1], mod_cols0[n - 1])
            modulation_columns(11, mod_rows0[11], mod_cols0[11])

            def turn_x(base, before, src):
                for t in range(NT):
                    pe.wait_ge(xn_ready, before + t + 1)
                    for g in range(2):
                        f = base + 2 * t + g
                        wait_free(pe, f)
                        for k in range(4):
                            ins = nc.tensor.transpose(bank(f)[:, k * P:k * P + P],
                                                      src(t)[:, (4 * g + k) * P:(4 * g + k + 1) * P], idn)
                        ins.then_inc(full(f), 1)

            def project_cm(f, i):
                wait_chunk(pe, i)
                w = wchunk(i)
                for m in range(2):
                    wait_free(pe, f + m)
                    for k in range(KD):
                        ins = mm(bank(f + m), w[:, k, m * P:m * P + P], hT[:, k, 0:LS], k == 0, k == KD - 1)
                    ins.then_inc(full(f + m), 1)
                wait_free(pe, f + 2)
                for m in range(2):
                    for k in range(KD):
                        ins = mm(bank(f + 2)[:, m * P:m * P + P], w[:, k, m * P:m * P + P], hT[:, k, LS:TOK],
                                 k == 0, k == KD - 1)
                ins.then_inc(full(f + 2), 1)

            def turn4(f, src):
                wait_free(pe, f)
                for h in range(H):
                    ins = nc.tensor.transpose(bank(f)[:, h * P:h * P + P], src(h), idn)
                ins.then_inc(full(f), 1)

            turn_x(start["hT0"], 0, lambda t: x[:, t, :])
            for f in range(2 * NT - 2, 2 * NT):
                wait_drained(pe, start["hT0"] + f)
            for j in range(8):
                f = start["in_hy"] + 3 * j
                project_cm(f, chunk_of[f + 2])
            for n in range(2):
                pe.wait_ge(conv_ready, 4 * n + 4)
                for t in range(NT):
                    turn4(start["tr_hy"] + NT * n + t, lambda m: cm[:, n, m, cols(t)])
            for o in range(2):
                f = start[f"fft{o}"]
                if o == 0:
                    wait_drained(pe, start["tr_hy"] + NT - 1)
                else:
                    wait_drained(pe, f - 1)
                for ft in range(TS):
                    for s in range(2):
                        wait_free(pe, f)
                        for k in range(TS):
                            ins = mm(bank(f), dft[:, k, s * 512 + ft * P:s * 512 + ft * P + P], hy_v[:, k, :],
                                     k == 0, k == TS - 1)
                        ins.then_inc(full(f), 1)
                        f += 1
                for s in range(2):
                    wait_free(pe, f)
                    mm(bank(f), dft_p[:, s * P:s * P + P], hy_v[:, TP, :]).then_inc(full(f), 1)
                    f += 1
                pe.wait_ge(idft_in, 48)
                pe.wait_ge(Y_ready, NT * (o + 1))
                Y = [(YP if k < TS else YQ)[:, k % TS, :] for k in range(2 * TS)]
                Yp = [YP[:, TP, :], YQ[:, TP, :]]
                if o == 0:
                    for t in range(TS):
                        wait_free(pe, f)
                        for k in range(8):
                            ins = mm(bank(f), idft[:, k, toks(t)], Y[k], k == 0, k == 7)
                        ins.then_inc(full(f), 1)
                        f += 1
                    wait_free(pe, f)
                    for k in range(2):
                        ins = mm(bank(f), idft_p[:, k, :], Yp[k], k == 0, k == 1)
                    ins.then_inc(full(f), 1)
                else:
                    for m in range(4):
                        wait_free(pe, f)
                        for k in range(8):
                            ins = mm(bank(f), Y[k][:, m * P:m * P + P], idft[:, k, :], k == 0, k == 7)
                        ins.then_inc(full(f), 1)
                        f += 1
                    wait_free(pe, f)
                    for m in range(4):
                        for k in range(2):
                            ins = mm(bank(f)[:, m * P:m * P + P], Yp[k][:, m * P:m * P + P], idft_p[:, k, :],
                                     k == 0, k == 1)
                    ins.then_inc(full(f), 1)

            f = start["ab"]
            pe.wait_ge(ab_in, 48)
            wait_free(pe, f)
            for t in range(NT):
                for k in range(KD):
                    ins = mm(bank(f)[:, 16 * t:16 * t + 16], hT[:, k, toks(t)], abw[:, k, :], k == 0, k == KD - 1)
            ins.then_inc(full(f), 1)
            for j in range(6):
                f = start["in_qkv"] + 3 * j
                project_cm(f, chunk_of[f + 2])
            f = start["cumsum"]
            pe.wait_ge(g_ready, 1)
            pe.wait_ge(const_ok, 1)
            pe.wait_ge(idft_in, 48)
            wait_free(pe, f)
            for d in range(2):
                mm(bank(f)[:, 20 * d:20 * d + 20], masks[:, 2 * d * P:2 * d * P + P], gsm[:, GE, :, 4 * d:4 * d + 4])
            mm(bank(f)[:, 40:80], ones[:, :], gsm[:, GE, :, :]).then_inc(full(f), 1)
            project_cm(start["in_z0"], chunk_of[start["in_z0"] + 2])
            for n, src in enumerate((cm[:, 0, :, :], cm[:, 1, :, :], v_cm)):
                pe.wait_ge(cm_ready, 4 * n + 4)
                for t in range(NT):
                    turn4(start["tr_q"] + NT * n + t, lambda m: src[:, m, cols(t)])
            project_cm(start["in_z1"], chunk_of[start["in_z1"] + 2])
            for t in range(NT):
                for n, src in enumerate((q_tm, k_tm)):
                    pe.wait_ge(normed, 2 * t + n + 1)
                    turn4(start["back"] + 2 * t + n, lambda h: src[:, t, h * P:h * P + P])
            wait_drained(pe, start["back"] + 2 * NT - 1)
            at_chain = 0
            for g in inv_groups:
                chains, nch = g["chains"], len(g["chains"])
                for n, t in enumerate(g["tiles"]):
                    f0 = g["at"] + 4 * n
                    for m, other in enumerate((kT, qT)):
                        wait_free(pe, f0 + m)
                        for h in range(H):
                            ins = mm(bank(f0 + m)[:, h * P:h * P + P], kT[:, h, toks(t)], other[:, h, toks(t)])
                        ins.then_inc(full(f0 + m), 1)
                    for d in range(2):
                        pe.wait_ge(gmask_ready, 2 * t + d + 2)
                        wait_free(pe, f0 + 2 + d)
                        mm(bank(f0 + 2 + d), ones[:, :], gm[t % 2][:, d, :]).then_inc(full(f0 + 2 + d), 1)
                for n, (t, d) in enumerate(chains):
                    pe.wait_ge(U1_ready, at_chain + n + 1)
                    turn4(g["T1"] + n, lambda h: Uinv[:, 2 * t + d, h * P:h * P + P])
                at_chain += nch
                for l, b in enumerate(LEVELS):
                    fl = g["levels"][l]
                    for n, (t, d) in enumerate(chains):
                        wait_drained(pe, g["T1"] + n if l == 0 else g["levels"][l - 1] + nch + n)
                        wait_free(pe, fl + n)
                        Tv = halves(Tinv[t % 2][:, d, :], b)
                        for h in range(H):
                            ins = mm(bank(fl + n)[:, h * 64:h * 64 + 64], LT[t % 2][:, d, h * P:h * P + P],
                                     Tv[:, h, :, d, :])
                        ins.then_inc(full(fl + n), 1)
                    for n, (t, d) in enumerate(chains):
                        if l > 0:
                            wait_drained(pe, g["levels"][l - 1] + 2 * nch + n)
                        wait_drained(pe, fl + n)
                        wait_free(pe, fl + nch + n)
                        for h in range(H):
                            ins = mm(bank(fl + nch + n)[:, h * 64:h * 64 + 64],
                                     Uinv[:, 2 * t + d, h * P:h * P + P], Xl[t % 2][:, d, h * 64:h * 64 + 64])
                        ins.then_inc(full(fl + nch + n), 1)
                    for n, (t, d) in enumerate(chains):
                        wait_drained(pe, fl + nch + n)
                        turn4(fl + 2 * nch + n, lambda h: Tinv[t % 2][:, d, h * P:h * P + P])
                    if g["mod"]:
                        j = g["mod"][l]
                        modulation_rows(j, mod_rows1[j])
                        modulation_columns(j, mod_rows1[j], mod_cols1[j])
            wait_drained(pe, last_tr[-1])
            for i, s in enumerate(SCAN):
                fs = start["scan"] + 10 * i
                St = Sp if s == TP else S
                tt = [s, s if s == TP else TS - 1 - s]
                for d in range(2):
                    if i > 1:
                        wait_drained(pe, fs - 4 + d)
                    elif d == 0:
                        pe.wait_ge(S_ready, 1)
                        if i == 1:
                            pe.wait_ge(state_in, 32)
                    wait_free(pe, fs + d)
                    for h in range(H):
                        ins = mm(bank(fs + d)[:, h * P:h * P + P], kT[:, h, toks(tt[d])], St[:, d, h * P:h * P + P])
                    ins.then_inc(full(fs + d), 1)
                for d in range(2):
                    wait_free(pe, fs + 2 + d)
                    for h in range(H):
                        ins = mm(bank(fs + 2 + d)[:, h * P:h * P + P], qT[:, h, toks(tt[d])],
                                 St[:, d, h * P:h * P + P])
                    ins.then_inc(full(fs + 2 + d), 1)
                for d in range(2):
                    wait_drained(pe, fs + d)
                    wait_free(pe, fs + 4 + d)
                    for h in range(H):
                        ins = mm(bank(fs + 4 + d)[:, h * P:h * P + P], Uinv[:, 2 * tt[d] + d, h * P:h * P + P],
                                 rr[:, d, h * P:h * P + P])
                    ins.then_inc(full(fs + 4 + d), 1)
                for d in range(2):
                    wait_drained(pe, fs + 4 + d)
                    pe.wait_ge(kd_ready, 2 * i + d + 1)
                    wait_free(pe, fs + 6 + d)
                    for h in range(H):
                        ins = mm(bank(fs + 6 + d)[:, h * P:h * P + P], kd[:, d, h * P:h * P + P],
                                 vn[:, d, h * P:h * P + P])
                    ins.then_inc(full(fs + 6 + d), 1)
                for d in range(2):
                    wait_free(pe, fs + 8 + d)
                    for h in range(H):
                        ins = mm(bank(fs + 8 + d)[:, h * P:h * P + P], intraT[:, 2 * tt[d] + d, h * P:h * P + P],
                                 vn[:, d, h * P:h * P + P])
                    ins.then_inc(full(fs + 8 + d), 1)
            spread_gates(start["gate0"], range(4), diag0, 16)
            for n, t in enumerate(NORM_ORDER):
                pe.wait_ge(on_ready, n + 1)
                turn4(start["tr_o"] + n, lambda h: o_acc[:, t, h * P:h * P + P])

            def project_out(base):
                for j in range(4):
                    i = chunk_of[base + NT * j + NT - 1]
                    wait_chunk(pe, i)
                    for t in range(NT):
                        f = base + NT * j + t
                        wait_free(pe, f)
                        for k in range(KD):
                            ins = mm(bank(f)[:, 0:WC], mix[:, k, toks(t)], wchunk(i)[:, k, :], k == 0, k == KD - 1)
                        ins.then_inc(full(f), 1)

            pe.wait_ge(hy_done, 5)
            wait_drained(pe, start["tr_o"] + NT - 1)
            project_out(start["out0"])

            turn_x(start["hT1"], NT, lambda t: xn[:, t, :])
            for j in range(6):
                n = WC if j < 5 else RKV + ROPE
                i = chunk_of[start["in_tm"] + NT * j + NT - 1]
                wait_chunk(pe, i)
                for t in range(NT):
                    if j == 0:
                        for g in range(2):
                            wait_drained(pe, start["hT1"] + 2 * t + g)
                    f = start["in_tm"] + NT * j + t
                    wait_free(pe, f)
                    for k in range(KD):
                        ins = mm(bank(f)[:, 0:n], hT[:, k, toks(t)], wchunk(i)[:, k, 0:n], k == 0, k == KD - 1)
                    ins.then_inc(full(f), 1)
            for j in range(4):
                f = start["in_g"] + 3 * j
                project_cm(f, chunk_of[f + 2])
            for t in range(NT + 1):
                f = start["tr_att"] + 3 * t
                if t < NT:
                    pe.wait_ge(onorm_ready, t + 1)
                    turn4(f, lambda h: ztm[:, t, h // 2, (h % 2) * P:(h % 2) * P + P])
                    turn4(f + 1, lambda h: ztm[:, t, 2 + h // 2, (h % 2) * P:(h % 2) * P + P])
                    wait_free(pe, f + 2)
                    nc.tensor.transpose(bank(f + 2)[:, 0:P], ztm[:, t, 4, 0:P], idn)
                    nc.tensor.transpose(bank(f + 2)[0:ROPE, P:2 * P], ztm[:, t, 4, P:P + ROPE], idn)\
                        .then_inc(full(f + 2), 1)
                else:
                    pe.wait_ge(odd_in, 160)
                    wait_free(pe, f)
                    for h in range(2):
                        nc.tensor.transpose(bank(f)[:, h * P:h * P + P], c_k[:, h * P:h * P + P], idn)
                    nc.tensor.transpose(bank(f)[:, 2 * P:3 * P], c_ckv, idn)
                    nc.tensor.transpose(bank(f)[0:ROPE, 3 * P:4 * P], c_kpe, idn).then_inc(full(f), 1)
            wait_drained(pe, start["tr_att"] + 3 * NT)
            qw = q_up.rearrange("p k (h c) -> p k h c", h=H)
            kw = kv_up.rearrange("p (h c) -> p h c", h=H)
            for h in range(H):
                f = start["q_nope"] + h
                wait_free(pe, f)
                for k in range(2):
                    ins = mm(bank(f), qw[:, k, h, 0:P], mqT[:, k, 0:LS], k == 0, k == 1)
                ins.then_inc(full(f), 1)
            f = start["q_nope"] + H
            wait_free(pe, f)
            for h in range(H):
                for k in range(2):
                    ins = mm(bank(f)[:, h * P:h * P + P], qw[:, k, h, 0:P], mqT[:, k, LS:TOK], k == 0, k == 1)
            ins.then_inc(full(f), 1)
            for t in range(NT):
                f = start["q_pe"] + t
                wait_free(pe, f)
                for k in range(2):
                    ins = mm(bank(f)[:, 0:WC], mqT[:, k, toks(t)], qw[:, k, :, P:P + ROPE], k == 0, k == 1)
                ins.then_inc(full(f), 1)
            for h in range(H):
                f = start["k_nope"] + h
                wait_free(pe, f)
                mm(bank(f), kw[:, h, 0:P], ckvT[:, 0:LS]).then_inc(full(f), 1)
            for g in range(2):
                f = start["k_nope"] + H + g
                wait_free(pe, f)
                for h in range(2):
                    ins = mm(bank(f)[:, h * WC:h * WC + WC], kw[:, 2 * g + h, 0:P], ckvT[:, LS:TOK + P])
                ins.then_inc(full(f), 1)
            for t in range(NT + 1):
                f = start["v_up"] + t
                wait_free(pe, f)
                mm(bank(f), ckvT[:, toks(t)], kw[:, :, P:2 * P]).then_inc(full(f), 1)
            for t in range(NT):
                f = start["tr_qpe"] + t
                if t < TS:
                    pe.wait_ge(qpe_ready, t + 1)
                else:
                    wait_drained(pe, start["q_pe"] + t)
                wait_free(pe, f)
                for h in range(H):
                    ins = nc.tensor.transpose(bank(f)[0:ROPE, h * P:h * P + P], qpe[:, t, h * ROPE:(h + 1) * ROPE], idn)
                ins.then_inc(full(f), 1)

            def scores(u):
                kind, h0 = UNITS[u]
                f = units[u]["s"]

                def product(o, h, q, keys):
                    if h < 4:
                        return mm(o, oq[:, h, q], ok[:, h // 2, keys])
                    mm(o, qnT[:, h - 4, q], knT[:, h - 4, keys], True, False)
                    return mm(o, qpT[0:ROPE, h - 4, q], kpT[0:ROPE, keys], False, True)

                if kind == "sample":
                    for g in range(4):
                        wait_free(pe, f + g)
                        product(bank(f + g), h0, toks(g), slice(0, LS)).then_inc(full(f + g), 1)
                    wait_free(pe, f + 4)
                    for g in range(4):
                        ins = product(bank(f + 4)[:, g * P:g * P + P], h0, toks(g), toks(NT))
                    ins.then_inc(full(f + 4), 1)
                else:
                    wait_free(pe, f)
                    for g in range(4):
                        ins = product(bank(f)[:, g * P:g * P + P], h0 + g, toks(TP), toks(TP))
                    ins.then_inc(full(f), 1)

            def values(u):
                kind, h0 = UNITS[u]
                pe.wait_ge(prob_ready, 4 * u + 4)
                f = units[u]["t"]
                n = 5 if kind == "sample" else 1
                for k in range(n):
                    turn4(f + k, lambda g: prob[u % 2][:, g, k * P:k * P + P])
                f = units[u]["p"]
                wait_free(pe, f)
                wait_drained(pe, units[u]["t"] + n - 1)

                def vals(h, t):
                    return v_all[:, t, (h // 2) * P:(h // 2) * P + P] if h < 4 else vm[:, t, (h - 4) * P:(h - 3) * P]

                if kind == "sample":
                    for k in range(5):
                        ins = mm(bank(f), vals(h0, k if k < TS else NT), probT[u % 2][:, k, :], k == 0, k == 4)
                else:
                    for g in range(4):
                        ins = mm(bank(f)[:, g * P:g * P + P], vals(h0 + g, TP), probT[u % 2][:, 0, g * P:g * P + P])
                ins.then_inc(full(f), 1)

            wait_drained(pe, start["tr_qpe"] + NT - 1)
            scores(0)
            for u in range(len(UNITS)):
                if u + 1 < len(UNITS):
                    scores(u + 1)
                values(u)
                if u in GATE_UNITS:
                    n = GATE_UNITS.index(u)
                    spread_gates(units[u]["g"], (2 * n, 2 * n + 1), diag1, 16 + 8 * (n + 1))
            wait_drained(pe, units[-1]["p"])
            project_out(start["out1"])

        @block.vector
        def _(dve):
            steps = [0]

            def chained(ins):
                steps[0] += 1
                ins.then_inc(dve_step, 1)
                dve.wait_ge(dve_step, steps[0])

            tt, ts, stt = nc.vector.tensor_tensor, nc.vector.tensor_scalar, nc.vector.scalar_tensor_tensor

            def heads(ap):
                return ap.rearrange("p (h c) -> p h c", h=H)

            two_pi = 2.0 * math.pi
            hi = float(np.float32(np.round(two_pi * 1024) / 1024))
            lo = two_pi - hi
            for layer in range(2):
                for n, (c0, c1) in enumerate(((0, LS), (LS, TOK))):
                    f = start["film"] + 2 * layer + n
                    wait_full(dve, f)
                    ts(h2[:, c0:c1], bank(f)[:, 0:c1 - c0], film_w[:, 256 + layer:257 + layer],
                       film_w[:, 258 + layer:259 + layer], ALU.add, ALU.mult).then_inc(free(f), 1)
                    wait_drained(dve, f)
                chained(ts(turns[:, :].bitcast(I32), h2[:, :], 1.0 / two_pi, None, ALU.mult))
                chained(nc.vector.tensor_copy(turns_f[:, :], turns[:, :].bitcast(I32)))
                chained(stt(h2[:, :], turns_f[:, :], -hi, h2[:, :], ALU.mult, ALU.add))
                chained(stt(h2[:, :], turns_f[:, :], -lo, h2[:, :], ALU.mult, ALU.add))
                ts(h2[:, :], h2[:, :], 3.1415925, -3.1415925, ALU.min, ALU.max).then_inc(arg_ready, 1)
            dve.wait_ge(sin_ready, 2)
            nc.vector.memset(h2[64:128, 0:1], 0.0)
            nc.vector.memset(h2[64:128, LS:LS + 1], 0.0).then_inc(h2_ready, 1)
            dve.wait_ge(tap_in, 16 * 8)
            for o in range(2):
                for t in range(NT):
                    f = start[f"filt{o}"] + 2 * t
                    pl = plus[o][:, t, :]
                    for s, taps in enumerate((plus, minus)):
                        wait_full(dve, f + s)
                        ins = tt(taps[o][:, t, :], bank(f + s), window[:, t, :], ALU.mult)
                        ins.then_inc(free(f + s), 1)
                    if t in (0, TP):
                        wait_drained(dve, f)
                        tt(pl[0:1, :], pl[0:1, :], wflat[0:1, 1024 + CH * o:1024 + CH * (o + 1)], ALU.add)\
                            .then_inc(taps_ready, 1)

            def take_mod_rows(j, f):
                wait_full(dve, f)
                nc.vector.tensor_copy(modrow[0:2, j % 2, :], bank(f)[0:2, 0:WC]).then_inc(free(f), 1)

            def take_mod_columns(j, f, layer):
                wait_full(dve, f)
                tt(modc_l[layer][:, 2 * j:2 * j + 2, :], bank(f)[:, 0:4].rearrange("p (m c) -> p m c", m=2),
                   vec1[:, 24 * layer + 2 * j:24 * layer + 2 * j + 2].unsqueeze(2).broadcast_to([P, 2, 2]),
                   ALU.add).then_inc(free(f), 1)

            def modulation_factors(layer, last):
                wait_drained(dve, last)
                stt(acol_l[layer][:, :, :], modc_l[layer][:, 8:16, :], 1.0,
                    vec1[:, 48 + 8 * layer:56 + 8 * layer].unsqueeze(2).broadcast_to([P, KD, 2]),
                    ALU.add, ALU.mult).then_inc(acol_ready, 1)
                tt(gcol_l[layer][:, :, :], modc_l[layer][:, 16:24, :],
                   vec1[:, 64 + 8 * layer:72 + 8 * layer].unsqueeze(2).broadcast_to([P, KD, 2]),
                   ALU.mult).then_inc(acol_ready, 1)

            wait_drained(dve, start["vectors"] + 1)
            for j in range(12):
                take_mod_rows(j, mod_rows0[j])
                if j >= 1:
                    take_mod_columns(j - 1, mod_cols0[j - 1], 0)
                if 5 <= j < 5 + NT:
                    t = j - 5
                    dve.wait_ge(rstd_ready, t + 1)
                    ts(x[:, t, :], x[:, t, :], stat[:, 1, t:t + 1], None, ALU.mult).then_inc(xn_ready, 1)
            take_mod_columns(11, mod_cols0[11], 0)
            modulation_factors(0, mod_cols0[11])
            wait_drained(dve, mod_rows0[11])
            nc.vector.memset(pad[:, :, :], 0.0).then_inc(pad_zero, 1)

            def modulate_x(base, layer):
                for t in range(NT):
                    f = base + 2 * t + 1
                    wait_full(dve, f)
                    for k in range(4, KD):
                        c = 0 if t < TS else 1
                        ins = ts(hT[:, k, toks(t)], bank(f)[:, (k - 4) * P:(k - 4) * P + P],
                                 acol_l[layer][:, k, c:c + 1], modc_l[layer][:, k, c:c + 1], ALU.mult, ALU.add)
                    ins.then_inc(free(f), 1)

            dve.wait_ge(acol_ready, 2)
            modulate_x(start["hT0"], 0)

            def convolve(f, width, w0, b0, dst, m0):
                wait_drained(dve, f + 2)
                for m in range(2):
                    o = dst[:, m0 + m, :]
                    for j in range(width):
                        src = pad[:, m, 2 - width // 2 + j:2 - width // 2 + j + CMW]
                        w = vec2[:, w0 + 12 * j + m0 + m:w0 + 12 * j + m0 + m + 1]
                        if j == 0 and b0 is None:
                            chained(ts(o, src, w, None, ALU.mult))
                        elif j == 0:
                            chained(ts(o, src, w, vec2[:, b0 + m0 + m:b0 + m0 + m + 1], ALU.mult, ALU.add))
                        elif j < width - 1:
                            chained(stt(o, src, w, o, ALU.mult, ALU.add))
                        else:
                            stt(o, src, w, o, ALU.mult, ALU.add).then_inc(conv_ready, 1)

            for j in range(6):
                convolve(start["in_hy"] + 6 + 3 * j, 3, 60 + 4 * (j // 2), 96 + 4 * (j // 2),
                         (cm[:, 0, :, :], cm[:, 1, :, :], hy_x2)[j // 2], 2 * (j % 2))
            for n, dst in enumerate((hy_v, hy_x1)):
                for t in range(NT):
                    f = start["tr_hy"] + NT * n + t
                    wait_full(dve, f)
                    nc.vector.tensor_copy(dst[:, t, :], bank(f)).then_inc(free(f), 1)
            wait_drained(dve, spec_f[1][11])
            s0, s1 = pflat[:, 0:512], pflat[:, 512:1024]
            for o in range(2):
                f = start[f"fft{o}"]
                if o == 0:
                    wait_full(dve, start["tr_hy"] + 2 * NT - 1)
                for ft in range(NT):
                    hx = specX[o][:, 0 if ft == 0 else 1, :] if ft in (0, TP) else specP[o][:, ft, :]
                    wait_full(dve, f)
                    tt(YP[:, ft, :], bank(f), specP[o][:, ft, :], ALU.mult)
                    tt(YQ[:, ft, :], bank(f), specQ[o][:, ft, :], ALU.mult).then_inc(free(f), 1)
                    wait_full(dve, f + 1)
                    tt(s0, bank(f + 1), specQ[o][:, ft, :], ALU.mult)
                    tt(s1, bank(f + 1), hx, ALU.mult).then_inc(free(f + 1), 1)
                    wait_drained(dve, f + 1)
                    tt(YP[:, ft, :], YP[:, ft, :], s0, ALU.subtract)
                    tt(YQ[:, ft, :], YQ[:, ft, :], s1, ALU.add).then_inc(Y_ready, 1)
                    dve.wait_ge(Y_ready, NT * o + ft + 1)
                    f += 2
                if o == 0:
                    for t in range(NT):
                        wait_full(dve, f)
                        tt(hy_v[:, t, :], bank(f), hy_x1[:, t, :], ALU.mult).then_inc(free(f), 1)
                        f += 1
                else:
                    for m in range(4):
                        wait_full(dve, f)
                        tt(hy_x2[:, m, 0:LS], bank(f), hy_x2[:, m, 0:LS], ALU.mult).then_inc(free(f), 1)
                        wait_drained(dve, f)
                        tt(mix[:, 4 + m, 0:LS], hy_x2[:, m, 0:LS], mix[:, 4 + m, 0:LS], ALU.mult).then_inc(hy_done, 1)
                        f += 1
                    wait_full(dve, f)
                    tt(hy_x2[:, :, CMP:CMP + LP], heads(bank(f)), hy_x2[:, :, CMP:CMP + LP], ALU.mult)\
                        .then_inc(free(f), 1)
                    wait_drained(dve, f)
                    tt(mix[:, 4:8, LS:TOK], hy_x2[:, :, CMP:CMP + LP], mix[:, 4:8, LS:TOK], ALU.mult)\
                        .then_inc(hy_done, 1)

            nc.vector.memset(pad[:, :, :], 0.0).then_inc(pad_zero, 1)
            f = start["ab"]
            wait_full(dve, f)
            dve.wait_ge(ab_in, 48)
            dve.wait_ge(hy_done, 5)
            nc.vector.tensor_copy(ab, bank(f)[:, 0:16 * NT].rearrange("p (t c) -> p t c", t=NT)).then_inc(free(f), 1)
            wait_drained(dve, f)
            chained(tt(gsm[:, T0, :, :], ab[:, :, 0:8], dtb.unsqueeze(1).broadcast_to([P, NT, 8]), ALU.add))
            chained(ts(gsm[:, T1, :, :], gsm[:, T0, :, :], -1.0, None, ALU.mult))
            tt(gsm[:, T1, :, :], gsm[:, T0, :, :], gsm[:, T1, :, :], ALU.min).then_inc(g_chain, 1)
            dve.wait_ge(g_act, 1)
            chained(stt(gsm[:, GE, :, :], gsm[:, T0, :, :], 0.0, gsm[:, T1, :, :], ALU.max, ALU.add))
            stt(gsm[:, GE, :, :], gsm[:, GE, :, :], -1.0, alog.unsqueeze(1).broadcast_to([P, NT, 8]),
                ALU.mult, ALU.mult).then_inc(g_ready, 1)
            chained(ts(gsm[:, BE, :, :], gsm[:, BE, :, :], 1.0, None, ALU.add))
            chained(nc.vector.reciprocal(gsm[:, BE, :, :], gsm[:, BE, :, :]))
            for j in range(6):
                convolve(start["in_qkv"] + 3 * j, 5, 4 * (j // 2), None,
                         (cm[:, 0, :, :], cm[:, 1, :, :], v_cm)[j // 2], 2 * (j % 2))
            f = start["cumsum"]
            wait_full(dve, f)
            for d in range(2):
                nc.vector.tensor_copy(gsm[:, CS, :, 4 * d:4 * d + 4],
                                      bank(f)[:, 20 * d:20 * d + 20].rearrange("p (t h) -> p t h", t=NT))
            nc.vector.tensor_copy(gsm[:, TOT, :, :], bank(f)[:, 40:80].rearrange("p (t h) -> p t h", t=NT))\
                .then_inc(free(f), 1)
            wait_drained(dve, f)
            tt(gsm[:, KDF, :, :], gsm[:, TOT, :, :], gsm[:, CS, :, :], ALU.subtract).then_inc(scal_ready, 1)
            dve.wait_ge(g_act, 2)
            chained(ts(gsm[:, NEG, :, :], gsm[:, EG, :, :], -1.0, None, ALU.mult))
            for n in range(2):
                for t in range(NT):
                    i = NT * n + t
                    dve.wait_ge(sq2_ready, i + 1)
                    dst = stat[:, 0, 4 * t:4 * t + 4] if n == 0 else gsm[:, T3, t, 0:4]
                    nc.vector.tensor_reduce(dst, heads(pflat[:, (i % 2) * 512:(i % 2) * 512 + 512]), AXX, ALU.add)\
                        .then_inc(ss_ready, 1)
            for t in range(NT):
                f = start["tr_v"] + t
                wait_full(dve, f)
                nc.vector.tensor_copy(v_tm[:, t, :], bank(f)).then_inc(free(f), 1)
            dve.wait_ge(rinv_ready, 1)
            for t in range(NT):
                tt(heads(q_tm[:, t, :]), heads(q_tm[:, t, :]),
                   stat[:, 1, 4 * t:4 * t + 4].unsqueeze(2).broadcast_to([P, H, P]), ALU.mult).then_inc(normed, 1)
                tt(heads(k_tm[:, t, :]), heads(k_tm[:, t, :]),
                   gsm[:, T3, t, 0:4].unsqueeze(2).broadcast_to([P, H, P]), ALU.mult).then_inc(normed, 1)
            at_chain = 0
            for g in inv_groups:
                chains, nch = g["chains"], len(g["chains"])
                for n, (t, d) in enumerate(chains):
                    f = g["at"] + 4 * (n // 2) + 2 + d
                    wait_full(dve, f)
                    for h in range(H):
                        ins = ts(dec[t % 2][:, d, h * P:h * P + P], bank(f)[:, h * P:h * P + P],
                                 gsm[:, CS, t, 4 * d + h:4 * d + h + 1], 0.0, ALU.subtract, ALU.min)
                    ins.then_inc(free(f), 1)
                for n, (t, d) in enumerate(chains):
                    f0 = g["at"] + 4 * (n // 2)
                    wait_full(dve, f0)
                    dve.wait_ge(masked, 2 * (at_chain + n) + 2)
                    for h in range(H):
                        ins = stt(LT[t % 2][:, d, h * P:h * P + P], bank(f0)[:, h * P:h * P + P],
                                  gsm[:, BE, t, 4 * d + h:4 * d + h + 1], dec[t % 2][:, d, h * P:h * P + P],
                                  ALU.mult, ALU.mult)
                    ins.then_inc(LT_ready if d == 0 else free(f0), 1)
                for n, (t, d) in enumerate(chains):
                    f0 = g["at"] + 4 * (n // 2)
                    wait_full(dve, f0 + 1)
                    iv = intraT[:, 2 * t + d, :]
                    ins = tt(iv, bank(f0 + 1), iv, ALU.mult)
                    if d == 1:
                        ins.then_inc(free(f0 + 1), 1)
                at_chain += nch
                for l, b in enumerate(LEVELS):
                    fl = g["levels"][l]
                    for n, (t, d) in enumerate(chains):
                        wait_full(dve, fl + n)
                        at = 2 * P + 64 * (len(LEVELS) * d + l)
                        stt(Xl[t % 2][:, d, :].rearrange("p (h c) -> p h c", h=H),
                            bank(fl + n)[:, 0:256].rearrange("p (h c) -> p h c", h=H), -1.0,
                            levels[:, at:at + 64].unsqueeze(1).broadcast_to([P, H, 64]), ALU.mult, ALU.mult)\
                            .then_inc(free(fl + n), 1)
                    for n, (t, d) in enumerate(chains):
                        f = fl + nch + n
                        wait_full(dve, f)
                        Tv = halves(Tinv[t % 2][:, d, :], b)[:, :, :, d, :]
                        tt(Tv, Tv, bank(f)[:, 0:256].rearrange("p (h n b) -> p h n b", h=H, b=b), ALU.add)\
                            .then_inc(free(f), 1)
                    if g["mod"]:
                        j = g["mod"][l]
                        take_mod_rows(j, mod_rows1[j])
                        take_mod_columns(j, mod_cols1[j], 1)
            modulation_factors(1, mod_cols1[11])
            wait_full(dve, last_tr[-1])
            nc.vector.memset(Sp[:, :, :], 0.0).then_inc(S_ready, 1)
            dve.wait_ge(S_ready, 1)
            dve.wait_ge(gmask_ready, 1)
            def sum_squares(n):
                dve.wait_ge(osq_ready, n + 1)
                st = slice(4 * NORM_ORDER[n], 4 * NORM_ORDER[n] + 4)
                nc.vector.tensor_reduce(stat[:, 0, st], heads(pflat[:, (n % 2) * 512:(n % 2) * 512 + 512]), AXX,
                                        ALU.add).then_inc(oss_ready, 1)

            def norm_heads(n):
                t = NORM_ORDER[n]
                dve.wait_ge(orstd_ready, n + 1)
                tt(heads(o_acc[:, t, :]), heads(o_acc[:, t, :]),
                   stat[:, 1, 4 * t:4 * t + 4].unsqueeze(2).broadcast_to([P, H, P]), ALU.mult).then_inc(on_ready, 1)

            for i, s in enumerate(SCAN):
                if i == 1:
                    dve.wait_ge(state_in, 32)
                fs = start["scan"] + 10 * i
                St = Sp if s == TP else S
                tl = [s, s if s == TP else TS - 1 - s]

                def sc(which, d, h):
                    return gsm[:, which, tl[d], 4 * d + h:4 * d + h + 1]

                for d in range(2):
                    f = fs + d
                    wait_full(dve, f)
                    for h in range(H):
                        ins = stt(rr[:, d, h * P:h * P + P], bank(f)[:, h * P:h * P + P], sc(NEG, d, h),
                                  v_tm[:, tl[d], h * P:h * P + P], ALU.mult, ALU.add)
                    ins.then_inc(free(f), 1)
                for d in range(2):
                    f = fs + 2 + d
                    wait_full(dve, f)
                    for h in range(H):
                        oh = o_acc[:, tl[d], h * P:h * P + P]
                        ins = stt(oh, bank(f)[:, h * P:h * P + P], sc(EG, d, h), oh, ALU.mult, ALU.add)
                    ins.then_inc(free(f), 1)
                    wait_drained(dve, f)
                for d in range(2):
                    f = fs + 4 + d
                    wait_full(dve, f)
                    tt(heads(vn[:, d, :]), heads(bank(f)),
                       gsm[:, BE, tl[d], 4 * d:4 * d + 4].unsqueeze(2).broadcast_to([P, H, P]), ALU.mult)\
                        .then_inc(free(f), 1)
                for d in range(2):
                    f = fs + 6 + d
                    wait_full(dve, f)
                    for h in range(H):
                        Sh = St[:, d, h * P:h * P + P]
                        ins = stt(Sh, Sh, sc(GL, d, h), bank(f)[:, h * P:h * P + P], ALU.mult, ALU.add)
                    ins.then_inc(free(f), 1)
                for d in range(2):
                    f = fs + 8 + d
                    wait_full(dve, f)
                    tt(o_acc[:, tl[d], :], bank(f), o_acc[:, tl[d], :], ALU.add).then_inc(free(f), 1)
                    wait_drained(dve, f)
                if i == 1:
                    sum_squares(0)
                if i == 2:
                    norm_heads(0)
            sum_squares(1)
            for n in range(1, NT):
                if n > 1:
                    norm_heads(n - 1)
                if n + 1 < NT:
                    sum_squares(n + 1)
            norm_heads(NT - 1)
            for n, t in enumerate(NORM_ORDER):
                f = start["tr_o"] + n
                wait_full(dve, f)
                mv = mix[:, 0:4, toks(t)]
                stt(mv, heads(bank(f)), vec1[:, 96:97], mv, ALU.mult, ALU.mult).then_inc(free(f), 1)
            def post_norm(layer, t):
                dve.wait_ge(yrstd_ready, NT * layer + t + 1)
                chained(stt(y[:, t, :], y[:, t, :], yst[:, 1, t:t + 1], gb_l[layer][:, 0 if t < TS else 1, :],
                            ALU.mult, ALU.mult))
                tt(x[:, t, :], x[:, t, :], y[:, t, :], ALU.add).then_inc(x_ready, 1)

            dve.wait_ge(xback_in, 32)
            for t in range(NT + 1):
                if t < NT:
                    post_norm(0, t)
                if t >= 1:
                    dve.wait_ge(rstd_ready, NT + t)
                    ts(xn[:, t - 1, :], x[:, t - 1, :], stat[:, 1, t - 1:t], None, ALU.mult).then_inc(xn_ready, 1)
            dve.wait_ge(acol_ready, 4)
            modulate_x(start["hT1"], 1)
            dve.wait_ge(z_ready, 8 * NT)
            ts(ostat[:, 0, :, 0:7], ostat[:, 0, :, 0:7], 1.0 / P, EPS, ALU.mult, ALU.add)
            ts(ostat[:, 0, :, 7:8], ostat[:, 0, :, 7:8], 1.0 / RQ, EPS, ALU.mult, ALU.add).then_inc(osum_ready, 1)
            dve.wait_ge(oinv_ready, 1)
            dve.wait_ge(odd_in, 160)

            def rotate(v, n, width, cos, sin):
                b = width // 4
                scratch = pflat[:, 0:n * width]

                def split(ap, heads_):
                    return ap.rearrange("p (h a two b) -> p h a two b", h=heads_, a=2, two=2, b=b)

                def table(ap, i):
                    return ap.rearrange("p (a two b) -> p a two b", a=2, two=2, b=b)[:, :, i, :]\
                        .unsqueeze(1).broadcast_to([P, n, 2, b])

                for i in range(2):
                    ins = tt(split(scratch, n)[:, :, :, i, :], split(v, n)[:, :, :, 1 - i, :], table(sin, i), ALU.mult)
                chained(ins)
                vh = v.rearrange("p (h c) -> p h c", h=n)
                chained(tt(vh, vh, cos.unsqueeze(1).broadcast_to([P, n, width]), ALU.mult))
                return tt(v, v, scratch, ALU.add)

            for t in range(NT):
                z = ztm[:, t, :, :].rearrange("p j c -> p (j c)")
                for lo, n, w, i, g in ((0, 4, P, 0, 0), (4 * P, 2, P, 4, 1), (8 * P, 1, P, 6, 2), (6 * P, 1, 2 * P, 7, None)):
                    v = z[:, lo:lo + n * w].rearrange("p (h c) -> p h c", h=n)
                    ins = tt(v, v, ostat[:, 1, t, i:i + n].unsqueeze(2).broadcast_to([P, n, w]), ALU.mult)
                    if g is not None:
                        chained(ins)
                        chained(tt(v, v, g_rows[:, g, :].unsqueeze(1).broadcast_to([P, n, w]), ALU.mult))
                if t < TS:
                    chained(ins)
                    chained(rotate(z[:, 0:4 * P], 4, P, rope[:, t, 0:P], rope[:, t, P:2 * P]))
                    chained(rotate(z[:, 4 * P:6 * P], 2, P, rope[:, t, 0:P], rope[:, t, P:2 * P]))
                    ins = rotate(z[:, 9 * P:9 * P + ROPE], 1, ROPE, rope[:, t, 2 * P:2 * P + ROPE],
                                 rope[:, t, 2 * P + ROPE:2 * P + 2 * ROPE])
                ins.then_inc(onorm_ready, 1)
                dve.wait_ge(onorm_ready, t + 1)
            for t in range(TS):
                wait_drained(dve, start["q_pe"] + t)
                rotate(qpe[:, t, :], 4, ROPE, rope[:, t, 2 * P:2 * P + ROPE],
                       rope[:, t, 2 * P + ROPE:2 * P + 2 * ROPE]).then_inc(qpe_ready, 1)
                dve.wait_ge(qpe_ready, t + 1)

            def maxima(u):
                kind, h = UNITS[u]
                scale = (P if h < 4 else P + ROPE) ** -0.5
                f = units[u]["s"]
                if kind == "sample":
                    for g in range(4):
                        wait_full(dve, f + g)
                        nc.vector.tensor_reduce(smax[:, u % 2, 0, g:g + 1], bank(f + g), AXX, ALU.max)
                    wait_full(dve, f + 4)
                    chained(nc.vector.tensor_reduce(smax[:, u % 2, 1, :], heads(bank(f + 4)), AXX, ALU.max))
                    chained(tt(smax[:, u % 2, 0, :], smax[:, u % 2, 0, :], smax[:, u % 2, 1, :], ALU.max))
                else:
                    wait_full(dve, f)
                    chained(nc.vector.tensor_reduce(smax[:, u % 2, 0, :], heads(bank(f)), AXX, ALU.max))
                ts(nmax[:, u % 2, :], smax[:, u % 2, 0, :], -scale, None, ALU.mult).then_inc(max_ready, 1)

            def normalise(u):
                kind, h = UNITS[u]
                f = units[u]["s"]
                if kind == "sample":
                    wait_drained(dve, f + 4)
                    chained(tt(ssum[:, u % 2, 1, :], ssum[:, u % 2, 0, :], ssum[:, u % 2, 1, :], ALU.add))
                else:
                    wait_drained(dve, f)
                chained(nc.vector.reciprocal(rsum[:, u % 2, :], ssum[:, u % 2, 1, :]))
                width = 640 if kind == "sample" else P
                for g in range(4):
                    ts(prob[u % 2][:, g, 0:width], prob[u % 2][:, g, 0:width], rsum[:, u % 2, g:g + 1], None,
                       ALU.mult).then_inc(prob_ready, 1)

            def gate_output(u):
                kind, h = UNITS[u]
                f = units[u]["p"]
                wait_full(dve, f)
                if kind == "sample":
                    tt(mix[:, h, 0:LS], bank(f), mix[:, h, 0:LS], ALU.mult).then_inc(free(f), 1)
                else:
                    tt(mix[:, h:h + 4, LS:TOK], heads(bank(f)), mix[:, h:h + 4, LS:TOK], ALU.mult).then_inc(free(f), 1)

            dve.wait_ge(cache_out, 1)
            maxima(0)
            normalise(0)
            for u in range(len(UNITS)):
                if u + 1 < len(UNITS):
                    maxima(u + 1)
                    normalise(u + 1)
                gate_output(u)
            for t in range(NT):
                post_norm(1, t)


_INS = ['x_prompt', 'x_sample', 'state_gdn_fwd', 'state_gdn_bwd', 'cache_gqa_k', 'cache_gqa_v', 'cache_mla_ckv',
        'cache_mla_kpe', 'c', 'c_ctx', 'mod_w', 'mod_b', 'pre_norm_g', 'post_norm_g', 'even_in_w', 'gdn_conv_w',
        'gdn_a_log', 'gdn_dt_bias', 'gdn_norm_g', 'hyena_conv_w', 'hyena_conv_b', 'hyena_ffn_w1', 'hyena_ffn_b1',
        'hyena_ffn_w2', 'hyena_ffn_b2', 'hyena_ffn_w3', 'hyena_sin_freq', 'hyena_bias', 'even_out_w', 'odd_in_w',
        'gqa_q_norm_g', 'gqa_k_norm_g', 'mla_q_norm_g', 'mla_q_up', 'mla_kv_norm_g', 'mla_kv_up', 'odd_out_w']
_OUTS = [('y_prompt', (1, LP, D)), ('y_sample', (1, LS, D)), ('new_gdn_fwd', (1, 1, H, P, P)),
         ('new_gdn_bwd', (1, 1, H, P, P)), ('new_gqa_k', (1, 1, LP, 2, P)), ('new_gqa_v', (1, 1, LP, 2, P)),
         ('new_mla_ckv', (1, 1, LP, RKV)), ('new_mla_kpe', (1, 1, LP, ROPE))]


def kernel(**inputs):
    import concourse.bacc as bacc
    from concourse.bass_utils import run_bass_kernel_spmd as run

    nc = bacc.Bacc("TRN2", target_bir_lowering=False, num_devices=1)
    arrays, ins, outs, tables = {}, {}, {}, {}
    for name in _INS:
        v = np.ascontiguousarray(inputs[name])
        arrays[f"in_{name}"] = v
        ins[name] = nc.dram_tensor(f"in_{name}", v.shape, mybir.dt.from_np(v.dtype), kind="ExternalInput").ap()
    for name, v in constants().items():
        arrays[name] = v
        tables[name] = nc.dram_tensor(name, v.shape, F32, kind="ExternalInput").ap()
    for name, shape in _OUTS:
        outs[name] = nc.dram_tensor(f"out_{name}", shape, F32, kind="ExternalOutput").ap()
    program(nc, ins, outs, tables)
    r = run(nc, [arrays], core_ids=[0])
    return tuple(r.results[0][f"out_{name}"] for name, _ in _OUTS)
```

```python
import math
from contextlib import ExitStack

import numpy as np

import concourse.bass as bass
from concourse import mybir

F32 = mybir.dt.float32
I32 = mybir.dt.int32
ALU = mybir.AluOpType
ACT = mybir.ActivationFunctionType
AXX = mybir.AxisListType.X

P = 128
D = 1024
KD = D // P
LS, LP = 512, 128
NT = (LS + LP) // P
TS = LS // P
TP = TS
TOK = LS + LP
H = 4
CH = 512
EPS = 1e-6
BANKS = 8

Q0, K0, V0, AB0, ZG0, HV0, HX10, HX20, HG0 = 0, 512, 1024, 1536, 1552, 2064, 2576, 3088, 3600
GQ0, GK0, GG0, MQ0, MG0 = 0, 512, 1024, 1536, 1984
RQ, RKV, ROPE = 256, 128, 64
WC = 256
WSLOTS = 3

ZPAD = TOK + 8
CMW = TOK + 4
CMP = LS + 4

INV = 42
LEVELS = [2, 4, 8, 16, 32, 64]

GROUPS = [[0, 1], [2, 3], [4]]
FILLS = [("film", 4), ("vectors", 2), ("filt0", 2 * NT), ("filt1", 2 * NT), ("spec_mod", 24 + 12),
         ("hT0", 2 * NT), ("in_hy", 24 + 7), ("tr_hy", 2 * NT), ("fft0", 10), ("ab", 1), ("fft0_back", 5),
         ("fft1", 10), ("in_z0", 3), ("fft1_back", 5),
         ("in_qkv", 18 + 5), ("cumsum", 1), ("tr_q", NT), ("tr_k", NT), ("in_z1", 3), ("decays", 2 * len(GROUPS[0])),
         ("tr_v", NT), ("back", 2 * NT), ("inv", NT * INV - 2 * len(GROUPS[0])), ("scan", 10 * NT),
         ("gate0", 4), ("tr_o", NT), ("out0", 4 * NT),
         ("hT1", 2 * NT), ("in_tm", 6 * NT), ("in_g", 12), ("tr_att", 3 * NT + 1),
         ("q_nope", 5), ("q_pe", NT), ("k_nope", 6), ("v_up", NT + 1), ("tr_qpe", NT),
         ("att", 8 * 11 + 2 * 3 + 4), ("out1", 4 * NT)]

UNITS = [("sample", 0), ("sample", 1), ("sample", 2), ("sample", 3), ("prompt", 0),
         ("sample", 4), ("sample", 5), ("sample", 6), ("sample", 7), ("prompt", 4)]


def fill_starts(fills):
    start, at = {}, 0
    for name, n in fills:
        start[name] = at
        at += n
    return start


GATE_UNITS = (4, 6)


def unit_fills(at):
    table = [None] * len(UNITS)
    order = [("s", 0), ("s", 1)]
    for u in range(len(UNITS)):
        order += [("t", u)] + ([("s", u + 2)] if u + 2 < len(UNITS) else []) + [("p", u)]
    for kind, u in order:
        n = {"s": 5, "t": 5, "p": 1}[kind] if UNITS[u][0] == "sample" else 1
        table[u] = dict(table[u] or {}, **{kind: at})
        at += n
        if kind == "p" and u in GATE_UNITS:
            table[u]["g"] = at
            at += 2
    return table


def spec_mod_fills(at):
    spec, cols = [[], []], []
    for n in range(12):
        for o_j in (2 * n, 2 * n + 1):
            spec[o_j // 12].append(at)
            at += 1
        if n >= 1:
            cols.append(at)
            at += 1
    cols.append(at)
    return spec, cols


SUMMED = [[j for j in range(12) if j not in (1, 4, 7, 10)], list(range(12))]


def project_fill(at, j):
    return at + 3 * j + max(0, j - 1)


def inverse_fills(at, first):
    sums = {t: first + 2 * n for n, t in enumerate(GROUPS[0])}
    keys, groups = {}, []
    for t in GROUPS[0]:
        keys[t] = at
        at += 2
    for n, tiles in enumerate(GROUPS):
        chains = [(t, d) for t in tiles for d in range(2)]
        g = {"chains": chains, "T1": at, "levels": [], "prepare": [[] for _ in LEVELS]}
        at += len(chains)
        for m, t in enumerate(GROUPS[n + 1] if n + 1 < len(GROUPS) else []):
            g["prepare"][m].append(("sums", t))
            g["prepare"][m + 2].append(("keys", t))
        for l in range(len(LEVELS)):
            g["levels"].append(at)
            at += 3 * len(chains)
            for kind, t in g["prepare"][l]:
                (sums if kind == "sums" else keys)[t] = at
                at += 2
        groups.append(g)
    return groups, sums, keys


SCAN = [TP, 0, 1, 2, 3]
NORM_ORDER = [TP, 1, 2, 0, 3]


def constants():
    f32 = np.float32
    out = {}
    out["k_ident"] = np.eye(P, dtype=f32)
    e, c = np.arange(P)[:, None], np.arange(P)[None, :]
    out["k_masks"] = np.concatenate([e <= c, e < c, e >= c, e > c], axis=1).astype(f32)
    lvl = []
    for d in range(2):
        first, second = (e, c) if d == 0 else (c, e)
        lvl.append(((first // 2 == second // 2) & (first % 2 == 0) & (second % 2 == 1)).astype(f32))
    for d in range(2):
        for b in LEVELS:
            cols = np.arange(P).reshape(-1, 2, b)[:, d, :].reshape(1, -1)
            rows = np.arange(P)[:, None]
            lvl.append(((rows // (2 * b) == cols // (2 * b)) & ((rows // b) % 2 == 1 - d)).astype(f32))
    out["k_levels"] = np.concatenate(lvl, axis=1)
    n = LS
    times = np.concatenate([np.arange(0, n, 2), np.arange(1, n, 2)])
    k = np.arange(n // 2)
    ang = 2 * np.pi * ((times[:, None] * k[None, :]) % (2 * n)) / (2 * n)
    fc, fs = np.cos(ang), np.sin(ang)
    middle = np.pi * (times % 4) / 2
    fs[:, 0] = np.where(times % 2 == 0, np.cos(middle), np.sin(middle))
    out["k_dft"] = np.round(np.concatenate([fc, fs], axis=1), 15).astype(f32)
    wgt = np.full((n // 2, 1), 1.0 / n)
    sin_wgt = wgt.copy()
    wgt[0] = 0.5 / n
    out["k_idft"] = np.round(np.concatenate([fc.T * wgt, fs.T * sin_wgt], axis=0), 18).astype(f32)
    for name, n in (("", LS), ("_p", LP)):
        order = times if n == LS else np.arange(n)
        if n == LP:
            k, t = np.arange(n), np.arange(n)
            ang = 2 * np.pi * ((t[:, None] * k[None, :]) % (2 * n)) / (2 * n)
            fc, fs = np.cos(ang), np.sin(ang)
            fs[:, 0] = 1.0 - 2.0 * (t % 2)
            out["k_dft_p"] = np.concatenate([fc, fs], axis=1).astype(f32)
            wgt = np.full((n, 1), 2.0 / (2 * n))
            wgt[0] = 1.0 / (2 * n)
            out["k_idft_p"] = np.concatenate([fc.T * wgt, fs.T * wgt], axis=0).astype(f32)
        tt = np.linspace(0.0, 1.0, n, dtype=f32)[:, None]
        wpos = (f32(2.0 * math.pi) * np.arange(n, dtype=f32)[:, None] / f32(n)).astype(f32)
        f = np.linspace(1e-4, 15, 16, dtype=f32)[None, :]
        out["k_pos" + name] = np.ascontiguousarray(
            np.concatenate([tt, np.cos(f * wpos), -np.sin(f * wpos)], axis=-1).astype(f32)[order].T)
        deltas = np.abs(np.linspace(math.log(1e-2) / 1.5, math.log(1e-2) / 0.3, CH, dtype=f32))
        out["k_window" + name] = np.exp(-tt * deltas[None, :]).astype(f32)[order]
    pos = np.arange(LS)
    parts = []
    for width in (128, ROPE):
        r = width // 2
        half = r // 2
        inv = (10000.0 ** (-np.arange(half, dtype=f32) * 2.0 / r)).astype(f32)
        cs, sn = [], []
        for where in (pos // 64, pos % 64):
            a = (where.astype(f32)[:, None] * inv[None, :]).astype(f32)
            cs += [np.cos(a), np.cos(a)]
            sn += [-np.sin(a), np.sin(a)]
        parts += cs + sn
    out["k_rope"] = np.concatenate(parts, axis=1).astype(f32)
    return out


def program(nc, a, out, consts):
    start = fill_starts(FILLS)
    ctx = ExitStack()
    with ctx:
        def sb(name, shape, dt=F32):
            return ctx.enter_context(nc.sbuf_tensor(name, shape, dt))

        def sem(name):
            return ctx.enter_context(nc.semaphore(name))

        ps = ctx.enter_context(nc.psum_tensor("ps", [P, BANKS, 512], F32))
        ctx.enter_context(nc.allow_non_contiguous_dma("small parameter vectors"))

        hT = sb("hT", [P, KD, TOK])
        mix = sb("mix", [P, 8, TOK])
        wring = sb("wring", [P, WSLOTS, KD, WC])
        xreg = sb("xreg", [P, 2 * 4 * CMW])
        pad = sb("pad", [P, 2, ZPAD])
        ident = sb("ident", [P, P])
        ones = sb("ones", [P, P])
        masks = sb("masks", [P, 4 * P])
        vec1 = sb("vec1", [P, 99])
        vec2 = sb("vec2", [P, 108])
        modc_l = [sb(f"modc{n}", [P, 24, 2]) for n in range(2)]
        acol_l = [sb(f"acol{n}", [P, KD, 2]) for n in range(2)]
        gcol_l = [sb(f"gcol{n}", [P, KD, 2]) for n in range(2)]
        scond = sb("scond", [P, KD, 2])
        stat = sb("stat", [P, 2, 4 * NT])
        yst = sb("yst", [P, 2, NT])
        ostat = sb("ostat", [P, 2, NT, 8])
        smax = sb("smax", [P, 2, 2, 4])
        ssum = sb("ssum", [P, 2, 2, 4])
        nmax = sb("nmax", [P, 2, 4])
        rsum = sb("rsum", [P, 2, 4])
        abw = sb("abw", [P, KD, 16])
        dtb, alog = sb("dtb", [P, 8])[:, :], sb("alog", [P, 8])[:, :]
        ab = sb("ab", [P, NT, 16])
        eps = sb("eps", [P, 3])
        phase = sb("phase", [P, 28704])

        def view(at, *shape):
            n = int(np.prod(shape))
            v = phase[:, at:at + n]
            if len(shape) == 1:
                return v
            names = "abcd"[:len(shape)]
            return v.rearrange(f"p ({' '.join(names)}) -> p {' '.join(names)}",
                               **{k: s for k, s in zip(names, shape)})

        x = xreg[:, 0:NT * D].rearrange("p (t d) -> p t d", t=NT)
        cm = xreg[:, :].rearrange("p (s m c) -> p s m c", s=2, m=4)

        dft, idft = view(0, 4, 512), view(2048, 4, 512)
        dft_p, idft_p = view(4096, 256), view(4352, 2, 128)
        specP = [view(4608 + 7168 * o, NT, 512) for o in range(2)]
        specQ = [view(4608 + 7168 * o + 2560, NT, 512) for o in range(2)]
        specX = [view(4608 + 7168 * o + 5120, 3, 512) for o in range(2)]
        mid_sin = [view(4608 + 7168 * o + 6656, 512) for o in range(2)]
        Ydiff = view(18944, 4, 512)
        hy_v, hy_x1, hy_x2 = view(20992, NT, 512), view(23552, NT, 512), view(26112, 4, CMW)
        plus = [view(20992, NT, 512), hT[:, 0:4, :].rearrange("p k n -> p (k n)").rearrange("p (t n) -> p t n", t=NT)]
        minus = [view(23552, NT, 512), hT[:, 4:8, :].rearrange("p k n -> p (k n)").rearrange("p (t n) -> p t n", t=NT)]
        pflat = pad[:, :, :].rearrange("p s n -> p (s n)")
        mflat = mix[:, :, :].rearrange("p k n -> p (k n)")
        sqs = pflat[:, 0:D]
        sqs_l = [view(20992, D), sqs]
        mid_rows = mflat[:, 1280:2304].rearrange("p (s n) -> p s n", s=2)
        window = mflat[:, 0:NT * 512].rearrange("p (t n) -> p t n", t=NT)
        w3 = mflat[:, 2560:2560 + 2048].rearrange("p (o s c) -> p o s c", o=2, s=2)
        wflat = wring[:, WSLOTS - 1, :, :].rearrange("p k c -> p (k c)")
        rows = view(26120, 256)
        film_w = view(26376, 264)
        h2, turns, turns_f = view(26640, TOK), view(27280, TOK), view(27920, TOK)
        macc = [m[:, 0:4 * WC].rearrange("p (s c n) -> p s c n", s=2, c=2) for m in
                (pad[:, :, :].rearrange("p s n -> p (s n)"), mflat[:, 1280:2560])]
        YP = xreg[:, 0:NT * 512].rearrange("p (t n) -> p t n", t=NT)
        YQ = xreg[:, NT * 512:2 * NT * 512].rearrange("p (t n) -> p t n", t=NT)

        q_tm, k_tm, v_tm = view(0, NT, 512), view(2560, NT, 512), view(5120, NT, 512)
        qT, kT = view(7680, H, TOK), view(10240, H, TOK)
        v_cm = view(12800, 4, CMW)
        Uinv = view(12800, 2 * NT, 512)
        intraT = view(17920, 2 * NT, 512)
        o_acc = view(23040, NT, 512)
        levels = view(25600, 1024)
        gsm = view(26832, 11, NT, 8)
        kd = view(27408, 2, 512)
        xs = xreg[:, :]
        hflat = hT[:, :, :].rearrange("p k n -> p (k n)")
        dec = [xs[:, n:n + 1024].rearrange("p (d n) -> p d n", d=2) for n in (0, 1024)]
        gm = [xs[:, n:n + 1024].rearrange("p (d n) -> p d n", d=2) for n in (2048, 3072)]
        Tinv = [hflat[:, n:n + 1024].rearrange("p (d n) -> p d n", d=2) for n in (0, 1024)]
        Xl = [hflat[:, n:n + 512].rearrange("p (d n) -> p d n", d=2) for n in (2048, 2560)]
        LT = wring[:, :, :, :].rearrange("p s k c -> p (s k c)")[:, 0:NT * 1024]\
            .rearrange("p (t d n) -> p t d n", t=NT, d=2)
        rr, vn, S, Sp = dec[0], dec[1], gm[0], gm[1]
        diag0 = hflat[:, 0:2048].rearrange("p (n c) -> p n c", c=P)
        y = view(0, NT, D)
        gb_l = [view(12800, 2, D), view(17152, 2, D)]
        diag1 = view(5120, 8, P)

        xn = view(23040, NT, D)
        ztm, v_all = view(0, NT, 5, WC), view(6400, NT + 1, WC)
        rope, g_rows = view(7936, TS, 384), view(9472, 3, P)
        q_up, kv_up = view(9856, 2, 768), view(11392, 1024)
        c_k, c_ckv, c_kpe = view(12416, 2 * P), view(12672, P), view(12800, ROPE)
        oq, ok = view(13056, H, TOK), view(15616, 2, TOK + P)
        mqT, ckvT = view(17152, 2, TOK), view(18432, TOK + P)
        qnT, qpT = view(19200, H, TOK), view(21760, H, TOK)
        qpe, knT = view(24320, NT, WC), view(25600, H, TOK + P)
        vm, kpT = hflat[:, 0:3072].rearrange("p (t n) -> p t n", t=NT + 1), hflat[:, 3072:3072 + TOK + P]
        prob = [view(0, H, 640), view(2560, H, 640)]
        probT = [view(7936, NT, 512), view(10496, NT, 512)]
        GE, BE, CS, EG, NEG, TOT, KDF, GL, T0, T1, T3 = range(11)

        bank_full = [sem(f"bank_full{b}") for b in range(BANKS)]
        bank_free = [sem(f"bank_free{b}") for b in range(BANKS)]
        w_landed = [sem(f"w_landed{s}") for s in range(WSLOTS)]
        dve_step = sem("dve_step")
        act_step = sem("act_step")
        pool_step = sem("pool_step")
        rows_in = sem("rows_in")
        film_in = sem("film_in")
        tap_in = sem("tap_in")
        dft_in = sem("dft_in")
        idft_in = sem("idft_in")
        x_in = sem("x_in")
        xback_in = sem("xback_in")
        gdn_in = sem("gdn_in")
        ab_in = sem("ab_in")
        state_in = sem("state_in")
        odd_in = sem("odd_in")
        stored = sem("stored")
        y_stored = sem("y_stored")
        const_ok = sem("const_ok")
        arg_ready = sem("arg_ready")
        sin_ready = sem("sin_ready")
        h2_ready = sem("h2_ready")
        w3_ready = sem("w3_ready")
        taps_ready = sem("taps_ready")
        scond_ready = sem("scond_ready")
        macc_ready = sem("macc_ready")
        acol_ready = sem("acol_ready")
        sq_ready = sem("sq_ready")
        rstd_ready = sem("rstd_ready")
        xn_ready = sem("xn_ready")
        pad_zero = sem("pad_zero")
        conv_ready = sem("conv_ready")
        cm_ready = sem("cm_ready")
        Y_ready = sem("Y_ready")
        Ysum_ready = sem("Ysum_ready")
        YQ_ready = sem("YQ_ready")
        hy_done = sem("hy_done")
        g_chain = sem("g_chain")
        g_act = sem("g_act")
        g_ready = sem("g_ready")
        gmask_ready = sem("gmask_ready")
        scal_ready = sem("scal_ready")
        sq2_ready = sem("sq2_ready")
        ss_ready = sem("ss_ready")
        rinv_ready = sem("rinv_ready")
        normed = sem("normed")
        expd = sem("expd")
        masked = sem("masked")
        U1_ready = sem("U1_ready")
        kd_ready = sem("kd_ready")
        S_ready = sem("S_ready")
        osq_ready = sem("osq_ready")
        oss_ready = sem("oss_ready")
        orstd_ready = sem("orstd_ready")
        on_ready = sem("on_ready")
        diag_ready = sem("diag_ready")
        ysq_ready = sem("ysq_ready")
        yrstd_ready = sem("yrstd_ready")
        x_ready = sem("x_ready")
        z_ready = sem("z_ready")
        osum_ready = sem("osum_ready")
        oinv_ready = sem("oinv_ready")
        onorm_ready = sem("onorm_ready")
        qpe_ready = sem("qpe_ready")
        cache_out = sem("cache_out")
        max_ready = sem("max_ready")
        prob_ready = sem("prob_ready")

        hy_f = [project_fill(start["in_hy"], j) for j in range(8)]
        qkv_f = [project_fill(start["in_qkv"], j) for j in range(6)]
        spec_f, mod_f0 = spec_mod_fills(start["spec_mod"])
        mod_f = [mod_f0, [f + 3 for f in hy_f[1:] + qkv_f[1:]]]
        inv_groups, sum_f, key_f = inverse_fills(start["inv"], start["decays"])
        units = unit_fills(start["att"])
        last_tr = [g["levels"][-1] + 3 * len(g["chains"]) - 1 for g in inv_groups]

        def bank(f):
            return ps[:, f % BANKS, :]

        def wait_full(eng, f):
            eng.wait_ge(bank_full[f % BANKS], f // BANKS + 1)

        def wait_free(eng, f):
            if f >= BANKS:
                eng.wait_ge(bank_free[f % BANKS], f // BANKS)

        def wait_drained(eng, f):
            eng.wait_ge(bank_free[f % BANKS], f // BANKS + 1)

        def full(f):
            return bank_full[f % BANKS]

        def free(f):
            return bank_free[f % BANKS]

        def wchunk(i):
            return wring[:, i % WSLOTS, :, :]

        def wait_chunk(eng, i):
            eng.wait_ge(w_landed[i % WSLOTS], 16 * (i // WSLOTS + 1))

        def toks(t):
            return slice(t * P, t * P + P)

        def cols(t):
            return slice(t * P, t * P + P) if t < TS else slice(CMP, CMP + P)

        def halves(ap, b):
            return ap.rearrange("p (h n two b) -> p h n two b", h=H, two=2, b=b)

        def chunk_list():
            lst = []
            mod = a["mod_w"]
            even, odd = a["even_in_w"][0], a["odd_in_w"][0]
            for j in range(12):
                lst.append((mod[0], WC * j, WC, mod_f[0][j]))
            taken = 0
            for fills, columns in ((hy_f, (HG0, HV0, HX10, HX20)), (qkv_f, (Q0, K0, V0))):
                if fills is qkv_f:
                    lst.append((even, ZG0, WC, start["in_z0"] + 2))
                for j, f in enumerate(fills):
                    lst.append((even, columns[j // 2] + WC * (j % 2), WC, f + 2))
                    if j >= 1:
                        lst.append((mod[1], WC * taken, WC, mod_f[1][taken]))
                        taken += 1
            lst.append((even, ZG0 + WC, WC, start["in_z1"] + 2))
            for j in range(4):
                lst.append((a["even_out_w"][0], WC * j, WC, start["out0"] + NT * j + NT - 1))
            for n, c0 in enumerate((GQ0, GQ0 + WC, GK0, GK0 + WC, MQ0, MQ0 + WC)):
                lst.append((odd, c0, WC if n < 5 else RKV + ROPE, start["in_tm"] + NT * n + NT - 1))
            for j, c0 in enumerate((GG0, GG0 + WC, MG0, MG0 + WC)):
                lst.append((odd, c0, WC, start["in_g"] + 3 * j + 2))
            for j in range(4):
                lst.append((a["odd_out_w"][0], WC * j, WC, start["out1"] + NT * j + NT - 1))
            return lst

        chunks = chunk_list()
        chunk_of = {}
        for i, ch in enumerate(chunks):
            chunk_of[ch[3]] = i

        block = ctx.enter_context(nc.Block())

        @block.sync
        def _(sp):
            w1 = a["hyena_ffn_w1"][0]
            sp.dma_start(film_w[0:33, 0:128].rearrange("k (r c) -> k r c", r=2),
                         w1.unsqueeze(1).broadcast_to([33, 2, 64])).then_inc(film_in, 16)
            for half in range(2):
                at = slice(64 * half, 64 * half + 64)
                sp.dma_start(film_w[at, 256:257], a["hyena_ffn_b1"][0].rearrange("(c o) -> c o", o=1))\
                  .then_inc(film_in, 16)
                sp.dma_start(film_w[at, 257:258], a["hyena_ffn_b2"][0].rearrange("(c o) -> c o", o=1))\
                  .then_inc(film_in, 16)
                sp.dma_start(film_w[at, 258:260], a["hyena_sin_freq"][0].rearrange("l c -> c l")).then_inc(film_in, 16)
            sp.dma_start(ident[:, :], consts["k_ident"]).then_inc(rows_in, 16)
            mb = a["mod_b"].rearrange("l (r c) -> (l r) c", c=P)
            r1, r2 = rows[:, 0:128], rows[:, 128:256]
            sp.dma_start(r1[0:48, :], mb).then_inc(rows_in, 16)
            sp.dma_start(r1[48:64, :], a["pre_norm_g"].rearrange("l (r c) -> (l r) c", c=P)).then_inc(rows_in, 16)
            sp.dma_start(r1[64:80, :], a["post_norm_g"].rearrange("l (r c) -> (l r) c", c=P)).then_inc(rows_in, 16)
            sp.dma_start(r1[80:88, :], a["c"].rearrange("l (r c) -> (l r) c", c=P)).then_inc(rows_in, 16)
            sp.dma_start(r1[88:96, :], a["c_ctx"].rearrange("(r c) -> r c", c=P)).then_inc(rows_in, 16)
            sp.dma_start(r1[96:97, :], a["gdn_norm_g"]).then_inc(rows_in, 16)
            sp.dma_start(r1[97:99, :], a["mla_q_norm_g"].rearrange("l (r c) -> (l r) c", c=P)).then_inc(rows_in, 16)
            sp.dma_start(r2[0:60, :], a["gdn_conv_w"].rearrange("l j (r c) -> (l j r) c", c=P)).then_inc(rows_in, 16)
            sp.dma_start(r2[60:96, :], a["hyena_conv_w"].rearrange("l j (r c) -> (l j r) c", c=P))\
              .then_inc(rows_in, 16)
            sp.dma_start(r2[96:108, :], a["hyena_conv_b"].rearrange("l (r c) -> (l r) c", c=P)).then_inc(rows_in, 16)
            w3_in = a["hyena_ffn_w3"][0].rearrange("k (o s c) -> k o s c", o=2, s=2)
            for half in range(2):
                for sign in range(2):
                    sp.dma_start(w3[64 * half:64 * half + 64, :, sign, :], w3_in[:, :, half, :]).then_inc(tap_in, 16)
            sp.dma_start(window[:, 0:TS, :], consts["k_window"].rearrange("(t p) n -> p t n", p=P)).then_inc(tap_in, 16)
            sp.dma_start(window[:, TP, :], consts["k_window_p"]).then_inc(tap_in, 16)
            sp.dma_start(wflat[0:1, 1024:2048], a["hyena_bias"].rearrange("l o c -> l (o c)")).then_inc(tap_in, 16)
            sp.dma_start(dft, consts["k_dft"].rearrange("(t p) n -> p t n", p=P)).then_inc(dft_in, 16)
            sp.dma_start(dft_p, consts["k_dft_p"]).then_inc(dft_in, 16)
            sp.dma_start(x[:, 0:TS, :], a["x_sample"][0].rearrange("(t p) d -> p t d", p=P)).then_inc(x_in, 16)
            sp.dma_start(x[:, TP, :], a["x_prompt"][0]).then_inc(x_in, 16)
            for i, (w, c0, n, last) in enumerate(chunks):
                if i == WSLOTS - 1:
                    sp.wait_ge(taps_ready, 4)
                if chunks[i][3] == start["out0"] + NT - 1:
                    wait_full(sp, last_tr[-1])
                if i >= WSLOTS:
                    wait_full(sp, chunks[i - WSLOTS][3])
                sp.dma_start(wchunk(i)[:, :, 0:n], w[:, c0:c0 + n].rearrange("(k p) n -> p k n", p=P))\
                  .then_inc(w_landed[i % WSLOTS], 16)

            for t in range(NT):
                sp.wait_ge(x_ready, NT + t + 1)
                dst = out["y_sample"][0, toks(t), :] if t < TS else out["y_prompt"][0]
                sp.dma_start(dst, x[:, t, :]).then_inc(y_stored, 16)
            sp.wait_ge(y_stored, 16 * NT)

        @block.gpsimd
        def _(pool):
            steps = [0]

            def chained(ins):
                steps[0] += 1
                ins.then_inc(pool_step, 1)
                pool.wait_ge(pool_step, steps[0])

            nc.gpsimd.memset(ones[:, :], 1.0).then_inc(const_ok, 1)
            nc.gpsimd.memset(eps[:, 0:1], EPS).then_inc(const_ok, 1)
            nc.gpsimd.memset(eps[:, 1:2], EPS * P).then_inc(const_ok, 1)
            chained(nc.gpsimd.memset(eps[:, 2:3], -0.5))
            pool.dma_start(idft, consts["k_idft"].rearrange("(t p) n -> p t n", p=P)).then_inc(idft_in, 16)
            pool.dma_start(idft_p, consts["k_idft_p"].rearrange("(t p) n -> p t n", p=P)).then_inc(idft_in, 16)
            pool.dma_start(masks[:, :], consts["k_masks"]).then_inc(idft_in, 16)
            pool.dma_start(abw[:, :, :], a["even_in_w"][0][:, AB0:AB0 + 16].rearrange("(k p) n -> p k n", p=P))\
                .then_inc(ab_in, 16)
            pool.dma_start(dtb, a["gdn_dt_bias"].rearrange("l a b -> l (a b)").broadcast_to([P, 8])).then_inc(ab_in, 16)
            pool.dma_start(alog, a["gdn_a_log"].rearrange("l a b -> l (a b)").broadcast_to([P, 8])).then_inc(ab_in, 16)

            pool.wait_ge(tap_in, 16 * 7)
            nc.gpsimd.tensor_scalar(w3[64:128, :, 1, :], w3[64:128, :, 1, :], -1.0, None, ALU.mult)\
                .then_inc(w3_ready, 1)

            def inverse_roots(dst, src, n, ready):
                chained(nc.gpsimd.tensor_scalar(src, src, 1.0 / n, EPS, ALU.mult, ALU.add))
                nc.gpsimd.tensor_tensor(dst, src, eps[:, 2:3].broadcast_to([P, src.shape[1]]), ALU.pow)\
                    .then_inc(ready, 1)

            for t in range(NT):
                pool.wait_ge(sq_ready, t + 1)
                inverse_roots(stat[:, 1, t:t + 1], stat[:, 0, t:t + 1], D, rstd_ready)

            for o in range(2):
                for kt in range(2):
                    pool.wait_ge(Y_ready, 3 * o + kt + 1)
                    lo_, hi_ = YQ[:, kt, :], YQ[:, 2 + kt, :]
                    chained(nc.gpsimd.tensor_tensor(Ydiff[:, 2 + kt, :], lo_, hi_, ALU.subtract))
                    nc.gpsimd.tensor_tensor(lo_, lo_, hi_, ALU.add).then_inc(YQ_ready, 1)

            wait_full(pool, start["fft1_back"] + 4)
            pool.wait_ge(hy_done, 5)
            pool.dma_start(levels, consts["k_levels"]).then_inc(gdn_in, 16)
            nc.gpsimd.memset(o_acc, 0.0).then_inc(gmask_ready, 1)

            for n, src in enumerate((q_tm, k_tm)):
                for t in range(NT):
                    i = NT * n + t
                    wait_drained(pool, start["tr_q"] + i)
                    if i >= 2:
                        pool.wait_ge(ss_ready, i - 1)
                    nc.gpsimd.tensor_tensor(pflat[:, (i % 2) * 512:(i % 2) * 512 + 512], src[:, t, :], src[:, t, :],
                                            ALU.mult).then_inc(sq2_ready, 1)
            pool.wait_ge(g_ready, 1)
            pool.wait_ge(idft_in, 48)
            pool.wait_ge(gdn_in, 16)
            wait_full(pool, start["tr_k"] + NT - 1)
            for n in range(0, NT, 2):
                tiles = range(n, min(n + 2, NT))
                for t in tiles:
                    for d in range(2):
                        if t >= 2:
                            wait_full(pool, sum_f[t - 2] + d)
                        nc.gpsimd.tensor_tensor(
                            gm[t % 2][:, d, :].rearrange("p (h c) -> p h c", h=H),
                            masks[:, 2 * d * P:2 * d * P + P].unsqueeze(1).broadcast_to([P, H, P]),
                            gsm[:, GE, t, 4 * d:4 * d + 4].unsqueeze(2).broadcast_to([P, H, P]),
                            ALU.mult).then_inc(gmask_ready, 1)
                for t in tiles:
                    for d in range(2):
                        pool.wait_ge(expd, 2 * t + d + 1)
                        m_incl = masks[:, 2 * d * P:2 * d * P + P].unsqueeze(1).broadcast_to([P, H, P])
                        m_strict = masks[:, (2 * d + 1) * P:(2 * d + 2) * P].unsqueeze(1).broadcast_to([P, H, P])
                        dv = dec[t % 2][:, d, :].rearrange("p (h c) -> p h c", h=H)
                        nc.gpsimd.tensor_tensor(intraT[:, 2 * t + d, :].rearrange("p (h c) -> p h c", h=H), dv,
                                                m_incl, ALU.mult).then_inc(masked, 1)
                        nc.gpsimd.tensor_tensor(dv, dv, m_strict, ALU.mult).then_inc(masked, 1)
            pool.wait_ge(normed, 2 * NT)
            pool.wait_ge(g_act, 2)
            def root_heads(n):
                pool.wait_ge(oss_ready, n + 1)
                st = slice(4 * NORM_ORDER[n], 4 * NORM_ORDER[n] + 4)
                inverse_roots(stat[:, 1, st], stat[:, 0, st], P, orstd_ready)

            for i, s in enumerate(SCAN):
                for d in range(2):
                    t = s if d == 0 or s == TP else TS - 1 - s
                    if i >= 1:
                        wait_full(pool, start["scan"] + 10 * (i - 1) + 6 + d)
                    nc.gpsimd.tensor_tensor(kd[:, d, :].rearrange("p (h c) -> p h c", h=H),
                                            k_tm[:, t, :].rearrange("p (h c) -> p h c", h=H),
                                            gsm[:, KDF, t, 4 * d:4 * d + 4].unsqueeze(2).broadcast_to([P, H, P]),
                                            ALU.mult).then_inc(kd_ready, 1)
                if i == 0:
                    wait_full(pool, last_tr[-1])
                    for n in range(2 * KD):
                        nc.gpsimd.tensor_tensor(diag0[:, n, :], ident[:, :],
                                                gcol_l[0][:, n % KD, n // KD:n // KD + 1].broadcast_to([P, P]),
                                                ALU.mult).then_inc(diag_ready, 1)
                if i == 2:
                    root_heads(0)
                if i == 1:
                    wait_drained(pool, start["scan"] + 7)
                    for n, nm in enumerate(("new_gdn_fwd", "new_gdn_bwd")):
                        pool.dma_start(out[nm][0, 0].rearrange("h k v -> k h v"),
                                       Sp[:, n, :].rearrange("p (h v) -> p h v", h=H)).then_inc(stored, 16)
            wait_drained(pool, start["scan"] + 10 * NT - 3)
            wait_full(pool, start["scan"] + 10 * NT - 1)
            pool.wait_ge(stored, 32)
            pool.dma_start(x[:, 0:TS, :], a["x_sample"][0].rearrange("(t p) d -> p t d", p=P)).then_inc(xback_in, 16)
            pool.dma_start(x[:, TP, :], a["x_prompt"][0]).then_inc(xback_in, 16)
            for n in range(1, NT):
                root_heads(n)
            for t in range(NT + 1):
                if t < NT:
                    pool.wait_ge(ysq_ready, t + 1)
                    inverse_roots(yst[:, 1, t:t + 1], yst[:, 0, t:t + 1], D, yrstd_ready)
                if t >= 1:
                    pool.wait_ge(sq_ready, NT + t)
                    inverse_roots(stat[:, 1, t - 1:t], stat[:, 0, t - 1:t], D, rstd_ready)

            pool.wait_ge(x_ready, NT)
            pool.dma_start(v_all[:, NT, :], a["cache_gqa_v"][0, 0].rearrange("t h d -> t (h d)")).then_inc(odd_in, 16)
            pool.dma_start(rope, consts["k_rope"].rearrange("(t p) n -> p t n", p=P)).then_inc(odd_in, 16)
            for n, nm in enumerate(("gqa_q_norm_g", "gqa_k_norm_g", "mla_kv_norm_g")):
                pool.dma_start(g_rows[:, n, :], a[nm].broadcast_to([P, P])).then_inc(odd_in, 16)
            pool.dma_start(q_up, a["mla_q_up"][0].rearrange("(k p) n -> p k n", p=P)).then_inc(odd_in, 16)
            pool.dma_start(kv_up, a["mla_kv_up"][0]).then_inc(odd_in, 16)
            pool.dma_start(c_k, a["cache_gqa_k"][0, 0].rearrange("t h d -> t (h d)")).then_inc(odd_in, 16)
            pool.dma_start(c_ckv, a["cache_mla_ckv"][0, 0]).then_inc(odd_in, 16)
            pool.dma_start(c_kpe, a["cache_mla_kpe"][0, 0]).then_inc(odd_in, 16)
            pool.wait_ge(onorm_ready, NT)
            wait_drained(pool, start["in_tm"] + 6 * NT - 1)
            pool.dma_start(out["new_gqa_k"][0, 0].rearrange("t h d -> t (h d)"), ztm[:, TP, 2, :]).then_inc(stored, 16)
            pool.dma_start(out["new_gqa_v"][0, 0].rearrange("t h d -> t (h d)"), v_all[:, TP, :]).then_inc(stored, 16)
            pool.dma_start(out["new_mla_ckv"][0, 0], ztm[:, TP, 4, 0:RKV]).then_inc(stored, 16)
            pool.dma_start(out["new_mla_kpe"][0, 0], ztm[:, TP, 4, RKV:RKV + ROPE]).then_inc(stored, 16)
            pool.wait_ge(stored, 96)
            nc.gpsimd.memset(rsum[:, :, :], 0.0).then_inc(cache_out, 1)
            pool.wait_ge(acol_ready, 4)
            wait_full(pool, start["tr_att"] + 3 * NT - 1)
            for n in range(2 * KD):
                if n == KD:
                    wait_full(pool, units[GATE_UNITS[0]]["g"] + 1)
                nc.gpsimd.tensor_tensor(diag1[:, n % KD, :], ident[:, :],
                                        gcol_l[1][:, n % KD, n // KD:n // KD + 1].broadcast_to([P, P]),
                                        ALU.mult).then_inc(diag_ready, 1)
            for t in range(NT):
                pool.wait_ge(ysq_ready, NT + t + 1)
                inverse_roots(yst[:, 1, t:t + 1], yst[:, 0, t:t + 1], D, yrstd_ready)

        @block.scalar
        def _(act):
            steps = [0]

            def chained(ins):
                steps[0] += 1
                ins.then_inc(act_step, 1)
                act.wait_ge(act_step, steps[0])

            def square_x(layer, t):
                if layer == 0:
                    act.wait_ge(x_in, 32)
                else:
                    act.wait_ge(x_ready, t + 1)
                if t >= 1 or layer == 1:
                    act.wait_ge(sq_ready, NT * layer + t)
                nc.scalar.activation(sqs_l[layer], x[:, t, :], ACT.Square, accum_out=stat[:, 0, t:t + 1])\
                    .then_inc(sq_ready, 1)

            act.dma_start(wflat[0:33, 0:LS], consts["k_pos"]).then_inc(film_in, 16)
            act.dma_start(wflat[0:33, LS:TOK], consts["k_pos_p"]).then_inc(film_in, 16)
            w2 = a["hyena_ffn_w2"][0]
            act.dma_start(film_w[0:64, 128:256].rearrange("k (r c) -> k r c", r=2),
                          w2.unsqueeze(1).broadcast_to([64, 2, 64])).then_inc(film_in, 16)
            for layer in range(2):
                act.wait_ge(arg_ready, layer + 1)
                nc.scalar.activation(h2, h2, ACT.Sin).then_inc(sin_ready, 1)
            f = start["vectors"]
            wait_full(act, f)
            nc.scalar.activation(vec1[:, :], bank(f)[:, 0:99], ACT.Copy).then_inc(free(f), 1)
            wait_full(act, f + 1)
            nc.scalar.activation(vec2[:, :], bank(f + 1)[:, 0:108], ACT.Copy).then_inc(free(f + 1), 1)
            wait_drained(act, f + 1)
            nc.scalar.activation(scond[:, :, 0], vec1[:, 80:88], ACT.Silu).then_inc(scond_ready, 1)
            nc.scalar.activation(scond[:, :, 1], vec1[:, 88:96], ACT.Silu).then_inc(scond_ready, 1)
            def take_even(f, dst):
                wait_full(act, f)
                nc.scalar.activation(dst, bank(f), ACT.Copy).then_inc(free(f), 1)

            for o in range(2):
                for kt in range(2):
                    take_even(spec_f[o][4 * kt], specP[o][:, kt, :])
                    take_even(spec_f[o][4 * kt + 2], specQ[o][:, kt, :])
                for j in range(8, 10):
                    f = spec_f[o][j]
                    wait_full(act, f)
                    nc.scalar.activation((specP, specQ)[j - 8][o][:, TP, :], bank(f), ACT.Copy).then_inc(free(f), 1)
                for j in (1, 3, 8, 9):
                    wait_drained(act, spec_f[o][j])
                for n, t in enumerate((0, 2, TP)):
                    chained(nc.scalar.activation(specX[o][:, n, :], specP[o][:, t, :], ACT.Copy))
                    nc.scalar.mul(specQ[o][0:1, t, :], specQ[o][0:1, t, :], 0.0)
                for j, tiles, scale in ((10, (0, 1), 0.5), (11, (2,), 1.0)):
                    f = spec_f[o][j]
                    wait_full(act, f)
                    for t in tiles:
                        ins = nc.scalar.activation(specX[o][0:1, t, :], bank(f)[0:1, :], ACT.Copy, scale=scale)
                    ins.then_inc(free(f), 1)
                if o == 0:
                    for t in range(NT):
                        square_x(0, t)
                    for t in range(NT):
                        act.wait_ge(rstd_ready, t + 1)
                        nc.scalar.activation(x[:, t, :], x[:, t, :], ACT.Copy, scale=stat[:, 1, t:t + 1])\
                            .then_inc(xn_ready, 1)
            def modulate_x(base, layer, tiles):
                for t in tiles:
                    f = base + 2 * t
                    wait_full(act, f)
                    if t == 0:
                        act.wait_ge(acol_ready, 2 * layer + 2)
                    for k in range(4):
                        c = 0 if t < TS else 1
                        ins = nc.scalar.activation(hT[:, k, toks(t)], bank(f)[:, k * P:k * P + P],
                                                   ACT.Identity, bias=modc_l[layer][:, k, c:c + 1],
                                                   scale=acol_l[layer][:, k, c:c + 1])
                    ins.then_inc(free(f), 1)

            modulate_x(start["hT0"], 0, range(NT))

            def take_gates(f, m0):
                for m in range(2):
                    wait_full(act, f + m)
                    nc.scalar.activation(mix[:, m0 + m, 0:LS], bank(f + m), ACT.Silu).then_inc(free(f + m), 1)
                wait_full(act, f + 2)
                nc.scalar.activation(mix[:, m0:m0 + 2, LS:TOK],
                                     bank(f + 2)[:, 0:2 * P].rearrange("p (m n) -> p m n", m=2), ACT.Silu)\
                    .then_inc(free(f + 2), 1)

            def take_rows(f, n):
                if n == 6:
                    act.wait_ge(pad_zero, 2)
                if n >= 1:
                    act.wait_ge(conv_ready, 2 * n)
                else:
                    act.wait_ge(pad_zero, 1)
                for m in range(2):
                    wait_full(act, f + m)
                    nc.scalar.activation(pad[:, m, 2:2 + LS], bank(f + m), ACT.Copy).then_inc(free(f + m), 1)
                wait_full(act, f + 2)
                nc.scalar.activation(pad[:, :, LS + 6:LS + 6 + LP],
                                     bank(f + 2)[:, 0:2 * P].rearrange("p (m n) -> p m n", m=2), ACT.Copy)\
                    .then_inc(free(f + 2), 1)

            for j in range(2):
                take_gates(hy_f[j], 4 + 2 * j)
            for j in range(6):
                take_rows(hy_f[2 + j], j)
            for o in range(2):
                for kt in range(2):
                    take_even(start[f"fft{o}"] + 4 * kt, YP[:, kt, :])
                    take_even(start[f"fft{o}"] + 4 * kt + 2, YQ[:, kt, :])
                if o == 1:
                    take_gates(start["in_z0"], 0)
            act.wait_ge(g_chain, 1)
            act.wait_ge(ab_in, 48)
            chained(nc.scalar.activation(gsm[:, T1, :, :], gsm[:, T1, :, :], ACT.Exp))
            nc.scalar.activation(gsm[:, T1, :, :], gsm[:, T1, :, :], ACT.Ln, bias=1.0)
            nc.scalar.activation(alog, alog, ACT.Exp)
            nc.scalar.activation(gsm[:, BE, :, :], ab[:, :, 8:16], ACT.Exp, scale=-1.0).then_inc(g_act, 1)

            def silu_rows(dst, n):
                for m in range(4):
                    act.wait_ge(conv_ready, n + m + 1)
                    nc.scalar.activation(dst[:, m, :], dst[:, m, :], ACT.Silu).then_inc(cm_ready, 1)

            for n, dst in enumerate((cm[:, 0, :, :], cm[:, 1, :, :], v_cm)):
                for j in range(2):
                    take_rows(qkv_f[2 * n + j], 6 + 2 * n + j)
                if n < 2:
                    silu_rows(dst, 12 + 4 * n)
            act.wait_ge(scal_ready, 1)
            nc.scalar.activation(gsm[:, EG, :, :], gsm[:, CS, :, :], ACT.Exp)
            nc.scalar.activation(gsm[:, GL, :, :], gsm[:, TOT, :, :], ACT.Exp)
            nc.scalar.activation(gsm[:, KDF, :, :], gsm[:, KDF, :, :], ACT.Exp).then_inc(g_act, 1)
            for n, dst in enumerate((q_tm, k_tm)):
                for t in range(NT):
                    f = start["tr_q"] + NT * n + t
                    wait_full(act, f)
                    nc.scalar.activation(dst[:, t, :], bank(f), ACT.Copy).then_inc(free(f), 1)
            silu_rows(v_cm, 20)
            act.wait_ge(ss_ready, 2 * NT)
            act.wait_ge(const_ok, 3)
            chained(nc.scalar.activation(stat[:, 1, :], stat[:, 0, :], ACT.Ln, scale=float(P), bias=eps[:, 1:2]))
            chained(nc.scalar.activation(gsm[:, T3, :, 0:4], gsm[:, T3, :, 0:4], ACT.Ln, bias=eps[:, 0:1]))
            nc.scalar.activation(stat[:, 1, :], stat[:, 1, :], ACT.Exp, scale=-0.5)
            nc.scalar.activation(gsm[:, T3, :, 0:4], gsm[:, T3, :, 0:4], ACT.Exp, scale=-0.5).then_inc(rinv_ready, 1)
            take_gates(start["in_z1"], 2)

            def exponentiate(t):
                for d in range(2):
                    wait_drained(act, sum_f[t] + d)
                    nc.scalar.activation(dec[t % 2][:, d, :], dec[t % 2][:, d, :], ACT.Exp).then_inc(expd, 1)

            for t in GROUPS[0]:
                exponentiate(t)
            for t in range(NT):
                for n, dst in enumerate((qT, kT)):
                    f = start["back"] + 2 * t + n
                    wait_full(act, f)
                    nc.scalar.activation(dst[:, :, toks(t)], bank(f).rearrange("p (h c) -> p h c", h=H), ACT.Copy)\
                        .then_inc(free(f), 1)
            for g in inv_groups:
                chains, nch = g["chains"], len(g["chains"])
                for l in range(len(LEVELS)):
                    for n, (t, d) in enumerate(chains):
                        f = g["levels"][l] + 2 * nch + n
                        wait_full(act, f)
                        nc.scalar.activation(Uinv[:, 2 * t + d, :], bank(f), ACT.Copy).then_inc(free(f), 1)
                    for kind, t in g["prepare"][l]:
                        if kind == "sums":
                            exponentiate(t)
            wait_drained(act, last_tr[-1])
            for d, nm in enumerate(("state_gdn_fwd", "state_gdn_bwd")):
                act.dma_start(S[:, d, :].rearrange("p (h v) -> p h v", h=H),
                              a[nm][0, 0].rearrange("h k v -> k h v")).then_inc(state_in, 16)
            def square_heads(n):
                t = NORM_ORDER[n]
                step = {TP: 0, 1: 3, 2: 3, 0: 4, 3: 4}[t]
                wait_drained(act, start["scan"] + 10 * step + 9)
                if n >= 2:
                    act.wait_ge(oss_ready, n - 1)
                nc.scalar.activation(pflat[:, (n % 2) * 512:(n % 2) * 512 + 512], o_acc[:, t, :], ACT.Square)\
                    .then_inc(osq_ready, 1)

            for n in range(NT):
                square_heads(n)

            def take_gate_rows(f0, n, layer):
                for i in range(n, n + 2):
                    f = f0 + i - n
                    wait_full(act, f)
                    nc.scalar.activation(gb_l[layer][:, i // 2, (i % 2) * 512:(i % 2) * 512 + 512], bank(f), ACT.Copy)\
                        .then_inc(free(f), 1)

            take_gate_rows(start["gate0"], 0, 0)
            take_gate_rows(start["gate0"] + 2, 2, 0)

            def take_output(layer):
                for j in range(4):
                    for t in range(NT):
                        f = start[f"out{layer}"] + NT * j + t
                        wait_full(act, f)
                        nc.scalar.activation(y[:, t, WC * j:WC * j + WC], bank(f)[:, 0:WC], ACT.Copy)\
                            .then_inc(free(f), 1)
                        if j == 3:
                            wait_drained(act, f)
                            if t >= 1:
                                act.wait_ge(ysq_ready, NT * layer + t)
                            if t >= 2 and layer == 0:
                                act.wait_ge(sq_ready, NT + t - 1)
                            nc.scalar.activation(sqs, y[:, t, :], ACT.Square, accum_out=yst[:, 0, t:t + 1])\
                                .then_inc(ysq_ready, 1)
                            if t >= 1 and layer == 0:
                                act.wait_ge(ysq_ready, t + 1)
                                square_x(1, t - 1)

            take_output(0)

            modulate_x(start["hT1"], 1, range(0, 1))
            square_x(1, NT - 1)
            modulate_x(start["hT1"], 1, range(1, NT))
            for j in range(6):
                for t in range(NT):
                    f = start["in_tm"] + NT * j + t
                    n = WC if j < 5 else RKV + ROPE
                    dst = v_all[:, t, :] if j == 3 else ztm[:, t, j - (j > 3), 0:n]
                    wait_full(act, f)
                    nc.scalar.activation(dst, bank(f)[:, 0:n], ACT.Copy).then_inc(free(f), 1)
            wait_drained(act, start["in_tm"] + 6 * NT - 1)
            for t in range(NT):
                z = ztm[:, t, :, :].rearrange("p j c -> p (j c)")
                for n in range(8):
                    lo, w = ((n * P, P) if n < 6 else (8 * P, P) if n == 6 else (6 * P, 2 * P))
                    if n == 0 and t >= 1:
                        act.wait_ge(z_ready, 8 * t)
                    nc.scalar.activation(pflat[:, lo:lo + w], z[:, lo:lo + w], ACT.Square,
                                         accum_out=ostat[:, 0, t, n:n + 1]).then_inc(z_ready, 1)
            act.wait_ge(osum_ready, 1)
            chained(nc.scalar.activation(ostat[:, 1, :, :], ostat[:, 0, :, :], ACT.Ln))
            nc.scalar.activation(ostat[:, 1, :, :], ostat[:, 1, :, :], ACT.Exp, scale=-0.5).then_inc(oinv_ready, 1)
            for j in range(4):
                take_gates(start["in_g"] + 3 * j, 2 * j)
            for t in range(NT + 1):
                f = start["tr_att"] + 3 * t
                if t < NT:
                    f += 1
                    wait_full(act, f)
                    nc.scalar.activation(ok[:, :, toks(t)], bank(f)[:, 0:2 * P].rearrange("p (h c) -> p h c", h=2),
                                         ACT.Copy)
                    for k in range(2):
                        ins = nc.scalar.activation(mqT[:, k, toks(t)], bank(f)[:, (2 + k) * P:(3 + k) * P], ACT.Copy,
                                                   scale=vec1[:, 97 + k:98 + k])
                    ins.then_inc(free(f), 1)
                    f += 1
                    wait_full(act, f)
                    nc.scalar.activation(ckvT[:, toks(t)], bank(f)[:, 0:P], ACT.Copy)
                    nc.scalar.activation(kpT[0:ROPE, toks(t)], bank(f)[0:ROPE, P:2 * P], ACT.Copy).then_inc(free(f), 1)
                else:
                    wait_full(act, f)
                    nc.scalar.activation(ok[:, :, toks(t)], bank(f)[:, 0:2 * P].rearrange("p (h c) -> p h c", h=2),
                                         ACT.Copy)
                    nc.scalar.activation(ckvT[:, toks(t)], bank(f)[:, 2 * P:3 * P], ACT.Copy)
                    nc.scalar.activation(kpT[0:ROPE, toks(t)], bank(f)[0:ROPE, 3 * P:4 * P], ACT.Copy)\
                        .then_inc(free(f), 1)
            for n, dst in ((0, qnT),):
                for h in range(H):
                    f = start["q_nope"] + h
                    wait_full(act, f)
                    nc.scalar.activation(dst[:, h, 0:LS], bank(f), ACT.Copy).then_inc(free(f), 1)
                f = start["q_nope"] + H
                wait_full(act, f)
                nc.scalar.activation(dst[:, :, LS:TOK], bank(f).rearrange("p (h c) -> p h c", h=H), ACT.Copy)\
                    .then_inc(free(f), 1)
            for t in range(NT):
                f = start["q_pe"] + t
                wait_full(act, f)
                nc.scalar.activation(qpe[:, t, :], bank(f)[:, 0:WC], ACT.Copy).then_inc(free(f), 1)
            for h in range(H):
                f = start["k_nope"] + h
                wait_full(act, f)
                nc.scalar.activation(knT[:, h, 0:LS], bank(f), ACT.Copy).then_inc(free(f), 1)
            for g in range(2):
                f = start["k_nope"] + H + g
                wait_full(act, f)
                nc.scalar.activation(knT[:, 2 * g:2 * g + 2, LS:TOK + P],
                                     bank(f).rearrange("p (h c) -> p h c", h=2), ACT.Copy).then_inc(free(f), 1)
            for t in range(NT + 1):
                f = start["v_up"] + t
                wait_full(act, f)
                nc.scalar.activation(vm[:, t, :], bank(f), ACT.Copy).then_inc(free(f), 1)
            for t in range(NT):
                f = start["tr_qpe"] + t
                wait_full(act, f)
                nc.scalar.activation(qpT[0:ROPE, :, toks(t)], bank(f)[0:ROPE, :].rearrange("p (h c) -> p h c", h=H),
                                     ACT.Copy).then_inc(free(f), 1)
            def exponentials(u):
                kind, h = UNITS[u]
                scale = (P if h < 4 else P + ROPE) ** -0.5
                f = units[u]["s"]
                if u >= 2:
                    wait_full(act, units[u - 2]["t"] + (4 if UNITS[u - 2][0] == "sample" else 0))
                else:
                    act.wait_ge(cache_out, 1)
                for g in range(4):
                    act.wait_ge(max_ready, 4 * u + g + 1)
                    keys = slice(LS, 640) if kind == "sample" else slice(0, P)
                    if kind == "sample":
                        nc.scalar.activation(prob[u % 2][:, g, 0:LS], bank(f + 1 + g), ACT.Exp, scale=scale,
                                             bias=nmax[:, u % 2, g:g + 1], accum_out=ssum[:, u % 2, 0, g:g + 1])\
                            .then_inc(free(f + 1 + g), 1)
                    ins = nc.scalar.activation(prob[u % 2][:, g, keys], bank(f)[:, g * P:g * P + P], ACT.Exp,
                                               scale=scale, bias=nmax[:, u % 2, g:g + 1],
                                               accum_out=ssum[:, u % 2, 1, g:g + 1])
                ins.then_inc(free(f), 1)

            def take_probT(u):
                kind, h = UNITS[u]
                for k in range(5 if kind == "sample" else 1):
                    f = units[u]["t"] + k
                    wait_full(act, f)
                    nc.scalar.activation(probT[u % 2][:, k, :], bank(f), ACT.Copy).then_inc(free(f), 1)

            exponentials(0)
            exponentials(1)
            for u in range(len(UNITS)):
                take_probT(u)
                if u + 2 < len(UNITS):
                    exponentials(u + 2)
                if u in GATE_UNITS:
                    take_gate_rows(units[u]["g"], 2 * GATE_UNITS.index(u), 1)
            take_output(1)


        @block.tensor
        def _(pe):
            def mm(o, l, r, first=True, last=True):
                return nc.tensor.matmul(o, l, r, start=first, stop=last)

            idn = ident[:, :]

            def spread_gates(f0, ns, diag, ready):
                pe.wait_ge(diag_ready, ready)
                for i, n in enumerate(ns):
                    f = f0 + i
                    wait_free(pe, f)
                    for k in range(4):
                        ins = mm(bank(f)[:, k * P:k * P + P], ones[:, :], diag[:, 4 * (n % (diag.shape[1] // 4)) + k, :])
                    ins.then_inc(full(f), 1)

            pe.wait_ge(film_in, 16 * 10)
            f = start["film"]
            mm(bank(f)[:, 0:LS], film_w[0:33, 0:128], wflat[0:33, 0:LS]).then_inc(full(f), 1)
            mm(bank(f + 1)[:, 0:LP], film_w[0:33, 0:128], wflat[0:33, LS:TOK]).then_inc(full(f + 1), 1)
            pe.wait_ge(sin_ready, 1)
            mm(bank(f + 2)[:, 0:LS], film_w[0:64, 128:256], h2[0:64, 0:LS]).then_inc(full(f + 2), 1)
            mm(bank(f + 3)[:, 0:LP], film_w[0:64, 128:256], h2[0:64, LS:TOK]).then_inc(full(f + 3), 1)
            pe.wait_ge(rows_in, 16 * 11)
            f = start["vectors"]
            nc.tensor.transpose(bank(f)[:, 0:99], rows[0:99, 0:128], ident[0:99, 0:99]).then_inc(full(f), 1)
            nc.tensor.transpose(bank(f + 1)[:, 0:108], rows[0:108, 128:256], ident[0:108, 0:108])\
                .then_inc(full(f + 1), 1)
            pe.wait_ge(h2_ready, 1)
            pe.wait_ge(tap_in, 16 * 7)
            pe.wait_ge(w3_ready, 1)
            for o in range(2):
                for t in range(NT):
                    for s in range(2):
                        f = start[f"filt{o}"] + 2 * t + s
                        wait_free(pe, f)
                        mm(bank(f), h2[:, toks(t)], w3[:, o, s, :]).then_inc(full(f), 1)
            def modulation(layer, j):
                f = mod_f[layer][j]
                wait_free(pe, f)
                if j not in SUMMED[layer]:
                    pe.wait_ge(scond_ready, 2)
                    i = chunk_of[f]
                    wait_chunk(pe, i)
                    for m in range(2):
                        for k in range(KD):
                            ins = mm(bank(f)[:, 2 * m:2 * m + 2], wchunk(i)[:, k, m * P:m * P + P], scond[:, k, :],
                                     k == 0, k == KD - 1)
                    ins.then_inc(full(f), 1)
                    return
                nth = SUMMED[layer].index(j)
                pe.wait_ge(macc_ready, 2 * len(SUMMED[0]) * layer + 2 * nth + 2)
                for m in range(2):
                    for n in range(2):
                        ins = mm(bank(f)[:, 2 * m + n:2 * m + n + 1],
                                 macc[layer][:, nth % 2, n, m * P:m * P + P], ones[:, 0:1])
                ins.then_inc(full(f), 1)

            def spectrum(o, j):
                f = spec_f[o][j]
                wait_free(pe, f)
                if j < 8:
                    kt, part, odd = j // 4, (j % 4) // 2, j % 2
                    taps = (plus, minus)[part][o]
                    for k in range(2):
                        ins = mm(bank(f), dft[:, 2 * odd + k, part * 256 + kt * P:part * 256 + kt * P + P],
                                 taps[:, 2 * odd + k, :], k == 0, k == 1)
                elif j < 10:
                    ins = mm(bank(f), dft_p[:, (j % 2) * P:(j % 2) * P + P], (plus, minus)[j % 2][o][:, TP, :])
                elif j == 10:
                    for k in range(2):
                        ins = mm(bank(f)[0:1, :], dft[:, k, 256:257], plus[o][:, k, :], k == 0, k == 1)
                else:
                    ins = mm(bank(f)[0:1, :], dft_p[:, P:P + 1], plus[o][:, TP, :])
                ins.then_inc(full(f), 1)

            pe.wait_ge(dft_in, 32)
            pe.wait_ge(const_ok, 1)
            for n in range(12):
                pe.wait_ge(taps_ready, 2 * (2 * n // 12 + 1))
                spectrum(2 * n // 12, 2 * n % 12)
                spectrum(2 * n // 12, 2 * n % 12 + 1)
                if n >= 1:
                    modulation(0, n - 1)
            modulation(0, 11)

            def turn_x(base, before, src):
                for t in range(NT):
                    pe.wait_ge(xn_ready, before + t + 1)
                    for g in range(2):
                        f = base + 2 * t + g
                        wait_free(pe, f)
                        for k in range(4):
                            ins = nc.tensor.transpose(bank(f)[:, k * P:k * P + P],
                                                      src(t)[:, (4 * g + k) * P:(4 * g + k + 1) * P], idn)
                        ins.then_inc(full(f), 1)

            def project_cm(f, i):
                wait_chunk(pe, i)
                w = wchunk(i)
                for m in range(2):
                    wait_free(pe, f + m)
                    for k in range(KD):
                        ins = mm(bank(f + m), w[:, k, m * P:m * P + P], hT[:, k, 0:LS], k == 0, k == KD - 1)
                    ins.then_inc(full(f + m), 1)
                wait_free(pe, f + 2)
                for m in range(2):
                    for k in range(KD):
                        ins = mm(bank(f + 2)[:, m * P:m * P + P], w[:, k, m * P:m * P + P], hT[:, k, LS:TOK],
                                 k == 0, k == KD - 1)
                ins.then_inc(full(f + 2), 1)

            def turn4(f, src):
                wait_free(pe, f)
                for h in range(H):
                    ins = nc.tensor.transpose(bank(f)[:, h * P:h * P + P], src(h), idn)
                ins.then_inc(full(f), 1)

            turn_x(start["hT0"], 0, lambda t: x[:, t, :])
            for f in range(2 * NT - 2, 2 * NT):
                wait_drained(pe, start["hT0"] + f)
            for j in range(8):
                project_cm(hy_f[j], chunk_of[hy_f[j] + 2])
                if j >= 1:
                    modulation(1, j - 1)
            def parity_cols(t):
                at = 2 * P * (t % 2) + t // 2
                return slice(at, at + 2 * P - 1, 2) if t < TS else cols(t)

            for n in range(2):
                pe.wait_ge(conv_ready, 4 * n + 4)
                for t in range(NT):
                    turn4(start["tr_hy"] + NT * n + t, lambda m: cm[:, n, m, parity_cols(t)])
            for o in range(2):
                f = start[f"fft{o}"]
                if o == 0:
                    wait_drained(pe, start["tr_hy"] + NT - 1)
                else:
                    wait_drained(pe, f - 1)
                for j in range(8):
                    kt, part, odd = j // 4, (j % 4) // 2, j % 2
                    wait_free(pe, f)
                    for k in range(2):
                        ins = mm(bank(f), dft[:, 2 * odd + k, part * 256 + kt * P:part * 256 + kt * P + P],
                                 hy_v[:, 2 * odd + k, :], k == 0, k == 1)
                    ins.then_inc(full(f), 1)
                    f += 1
                for s in range(2):
                    wait_free(pe, f)
                    mm(bank(f), dft_p[:, s * P:s * P + P], hy_v[:, TP, :]).then_inc(full(f), 1)
                    f += 1
                if o == 0:
                    f = start["ab"]
                    pe.wait_ge(ab_in, 48)
                    wait_free(pe, f)
                    for t in range(NT):
                        for k in range(KD):
                            ins = mm(bank(f)[:, 16 * t:16 * t + 16], hT[:, k, toks(t)], abw[:, k, :], k == 0, k == KD - 1)
                    ins.then_inc(full(f), 1)
                else:
                    project_cm(start["in_z0"], chunk_of[start["in_z0"] + 2])
                f = start[f"fft{o}_back"]
                pe.wait_ge(idft_in, 48)
                pe.wait_ge(Ysum_ready, o + 1)
                pe.wait_ge(YQ_ready, 2 * (o + 1))
                Y = [[YP[:, 0, :], YP[:, 1, :], Ydiff[:, 2, :], Ydiff[:, 3, :]],
                     [Ydiff[:, 0, :], Ydiff[:, 1, :], YQ[:, 0, :], YQ[:, 1, :]]]
                Yp = [YP[:, TP, :], YQ[:, TP, :]]
                if o == 0:
                    for t in range(TS):
                        wait_free(pe, f)
                        for k in range(4):
                            ins = mm(bank(f), idft[:, k, toks(t)], Y[t // 2][k], k == 0, k == 3)
                        ins.then_inc(full(f), 1)
                        f += 1
                    pe.wait_ge(Y_ready, 3)
                    wait_free(pe, f)
                    for k in range(2):
                        ins = mm(bank(f), idft_p[:, k, :], Yp[k], k == 0, k == 1)
                    ins.then_inc(full(f), 1)
                else:
                    for m in range(4):
                        wait_free(pe, f)
                        for odd in range(2):
                            for k in range(4):
                                ins = mm(bank(f)[:, odd:LS:2], Y[odd][k][:, m * P:m * P + P],
                                         idft[:, k, odd * 256:odd * 256 + 256], k == 0, k == 3)
                        ins.then_inc(full(f), 1)
                        f += 1
                    pe.wait_ge(Y_ready, 6)
                    wait_free(pe, f)
                    for m in range(4):
                        for k in range(2):
                            ins = mm(bank(f)[:, m * P:m * P + P], Yp[k][:, m * P:m * P + P], idft_p[:, k, :],
                                     k == 0, k == 1)
                    ins.then_inc(full(f), 1)

            for j in range(6):
                project_cm(qkv_f[j], chunk_of[qkv_f[j] + 2])
                if j >= 1:
                    modulation(1, 6 + j)
            f = start["cumsum"]
            pe.wait_ge(g_ready, 1)
            pe.wait_ge(const_ok, 1)
            pe.wait_ge(idft_in, 48)
            wait_free(pe, f)
            for d in range(2):
                mm(bank(f)[:, 20 * d:20 * d + 20], masks[:, 2 * d * P:2 * d * P + P], gsm[:, GE, :, 4 * d:4 * d + 4])
            mm(bank(f)[:, 40:80], ones[:, :], gsm[:, GE, :, :]).then_inc(full(f), 1)
            def sum_decays(t):
                for d in range(2):
                    pe.wait_ge(gmask_ready, 2 * t + d + 2)
                    wait_free(pe, sum_f[t] + d)
                    mm(bank(sum_f[t] + d), ones[:, :], gm[t % 2][:, d, :]).then_inc(full(sum_f[t] + d), 1)

            def key_products(t):
                for m, other in enumerate((kT, qT)):
                    f = key_f[t] + m
                    wait_free(pe, f)
                    for h in range(H):
                        ins = mm(bank(f)[:, h * P:h * P + P], kT[:, h, toks(t)], other[:, h, toks(t)])
                    ins.then_inc(full(f), 1)

            for n, src in enumerate((cm[:, 0, :, :], cm[:, 1, :, :], v_cm)):
                if n == 2:
                    project_cm(start["in_z1"], chunk_of[start["in_z1"] + 2])
                    for t in GROUPS[0]:
                        sum_decays(t)
                pe.wait_ge(cm_ready, 4 * n + 4)
                for t in range(NT):
                    turn4(start[("tr_q", "tr_k", "tr_v")[n]] + t, lambda m: src[:, m, cols(t)])
            for t in range(NT):
                for n, src in enumerate((q_tm, k_tm)):
                    pe.wait_ge(normed, 2 * t + n + 1)
                    turn4(start["back"] + 2 * t + n, lambda h: src[:, t, h * P:h * P + P])
            wait_drained(pe, start["back"] + 2 * NT - 1)
            for t in GROUPS[0]:
                key_products(t)
            for g in inv_groups:
                chains, nch = g["chains"], len(g["chains"])
                for n, (t, d) in enumerate(chains):
                    pe.wait_ge(U1_ready, 2 * t + d + 1)
                    turn4(g["T1"] + n, lambda h: Uinv[:, 2 * t + d, h * P:h * P + P])
                for l, b in enumerate(LEVELS):
                    fl = g["levels"][l]
                    for n, (t, d) in enumerate(chains):
                        wait_drained(pe, g["T1"] + n if l == 0 else g["levels"][l - 1] + nch + n)
                        wait_free(pe, fl + n)
                        Tv = halves(Tinv[t % 2][:, d, :], b)
                        for h in range(H):
                            ins = mm(bank(fl + n)[:, h * 64:h * 64 + 64], LT[:, t, d, h * P:h * P + P],
                                     Tv[:, h, :, d, :])
                        ins.then_inc(full(fl + n), 1)
                    for n, (t, d) in enumerate(chains):
                        if l > 0:
                            wait_drained(pe, g["levels"][l - 1] + 2 * nch + n)
                        wait_drained(pe, fl + n)
                        wait_free(pe, fl + nch + n)
                        for h in range(H):
                            ins = mm(bank(fl + nch + n)[:, h * 64:h * 64 + 64],
                                     Uinv[:, 2 * t + d, h * P:h * P + P], Xl[t % 2][:, d, h * 64:h * 64 + 64])
                        ins.then_inc(full(fl + nch + n), 1)
                    for n, (t, d) in enumerate(chains):
                        wait_drained(pe, fl + nch + n)
                        turn4(fl + 2 * nch + n, lambda h: Tinv[t % 2][:, d, h * P:h * P + P])
                    for kind, t in g["prepare"][l]:
                        (sum_decays if kind == "sums" else key_products)(t)
            wait_drained(pe, last_tr[-1])
            for i, s in enumerate(SCAN):
                fs = start["scan"] + 10 * i
                St = Sp if s == TP else S
                tt = [s, s if s == TP else TS - 1 - s]
                for d in range(2):
                    if i > 1:
                        wait_drained(pe, fs - 4 + d)
                    elif d == 0:
                        pe.wait_ge(S_ready, 1)
                        if i == 1:
                            pe.wait_ge(state_in, 32)
                    wait_free(pe, fs + d)
                    for h in range(H):
                        ins = mm(bank(fs + d)[:, h * P:h * P + P], kT[:, h, toks(tt[d])], St[:, d, h * P:h * P + P])
                    ins.then_inc(full(fs + d), 1)
                for d in range(2):
                    wait_free(pe, fs + 2 + d)
                    for h in range(H):
                        ins = mm(bank(fs + 2 + d)[:, h * P:h * P + P], qT[:, h, toks(tt[d])],
                                 St[:, d, h * P:h * P + P])
                    ins.then_inc(full(fs + 2 + d), 1)
                for d in range(2):
                    wait_drained(pe, fs + d)
                    wait_free(pe, fs + 4 + d)
                    for h in range(H):
                        ins = mm(bank(fs + 4 + d)[:, h * P:h * P + P], Uinv[:, 2 * tt[d] + d, h * P:h * P + P],
                                 rr[:, d, h * P:h * P + P])
                    ins.then_inc(full(fs + 4 + d), 1)
                for d in range(2):
                    wait_drained(pe, fs + 4 + d)
                    pe.wait_ge(kd_ready, 2 * i + d + 1)
                    wait_free(pe, fs + 6 + d)
                    for h in range(H):
                        ins = mm(bank(fs + 6 + d)[:, h * P:h * P + P], kd[:, d, h * P:h * P + P],
                                 vn[:, d, h * P:h * P + P])
                    ins.then_inc(full(fs + 6 + d), 1)
                for d in range(2):
                    wait_free(pe, fs + 8 + d)
                    for h in range(H):
                        ins = mm(bank(fs + 8 + d)[:, h * P:h * P + P], intraT[:, 2 * tt[d] + d, h * P:h * P + P],
                                 vn[:, d, h * P:h * P + P])
                    ins.then_inc(full(fs + 8 + d), 1)
            spread_gates(start["gate0"], range(4), diag0, 16)
            for n, t in enumerate(NORM_ORDER):
                pe.wait_ge(on_ready, n + 1)
                turn4(start["tr_o"] + n, lambda h: o_acc[:, t, h * P:h * P + P])

            def project_out(base):
                for j in range(4):
                    i = chunk_of[base + NT * j + NT - 1]
                    wait_chunk(pe, i)
                    for t in range(NT):
                        f = base + NT * j + t
                        wait_free(pe, f)
                        for k in range(KD):
                            ins = mm(bank(f)[:, 0:WC], mix[:, k, toks(t)], wchunk(i)[:, k, :], k == 0, k == KD - 1)
                        ins.then_inc(full(f), 1)

            pe.wait_ge(hy_done, 5)
            wait_drained(pe, start["tr_o"] + NT - 1)
            project_out(start["out0"])

            turn_x(start["hT1"], NT, lambda t: xn[:, t, :])
            for j in range(6):
                n = WC if j < 5 else RKV + ROPE
                i = chunk_of[start["in_tm"] + NT * j + NT - 1]
                wait_chunk(pe, i)
                for t in range(NT):
                    if j == 0:
                        for g in range(2):
                            wait_drained(pe, start["hT1"] + 2 * t + g)
                    f = start["in_tm"] + NT * j + t
                    wait_free(pe, f)
                    for k in range(KD):
                        ins = mm(bank(f)[:, 0:n], hT[:, k, toks(t)], wchunk(i)[:, k, 0:n], k == 0, k == KD - 1)
                    ins.then_inc(full(f), 1)
            for j in range(4):
                f = start["in_g"] + 3 * j
                project_cm(f, chunk_of[f + 2])
            for t in range(NT + 1):
                f = start["tr_att"] + 3 * t
                if t < NT:
                    pe.wait_ge(onorm_ready, t + 1)
                    turn4(f, lambda h: ztm[:, t, h // 2, (h % 2) * P:(h % 2) * P + P])
                    turn4(f + 1, lambda h: ztm[:, t, 2 + h // 2, (h % 2) * P:(h % 2) * P + P])
                    wait_free(pe, f + 2)
                    nc.tensor.transpose(bank(f + 2)[:, 0:P], ztm[:, t, 4, 0:P], idn)
                    nc.tensor.transpose(bank(f + 2)[0:ROPE, P:2 * P], ztm[:, t, 4, P:P + ROPE], idn)\
                        .then_inc(full(f + 2), 1)
                else:
                    pe.wait_ge(odd_in, 160)
                    wait_free(pe, f)
                    for h in range(2):
                        nc.tensor.transpose(bank(f)[:, h * P:h * P + P], c_k[:, h * P:h * P + P], idn)
                    nc.tensor.transpose(bank(f)[:, 2 * P:3 * P], c_ckv, idn)
                    nc.tensor.transpose(bank(f)[0:ROPE, 3 * P:4 * P], c_kpe, idn).then_inc(full(f), 1)
            wait_drained(pe, start["tr_att"] + 3 * NT)
            qw = q_up.rearrange("p k (h c) -> p k h c", h=H)
            kw = kv_up.rearrange("p (h c) -> p h c", h=H)
            for h in range(H):
                f = start["q_nope"] + h
                wait_free(pe, f)
                for k in range(2):
                    ins = mm(bank(f), qw[:, k, h, 0:P], mqT[:, k, 0:LS], k == 0, k == 1)
                ins.then_inc(full(f), 1)
            f = start["q_nope"] + H
            wait_free(pe, f)
            for h in range(H):
                for k in range(2):
                    ins = mm(bank(f)[:, h * P:h * P + P], qw[:, k, h, 0:P], mqT[:, k, LS:TOK], k == 0, k == 1)
            ins.then_inc(full(f), 1)
            for t in range(NT):
                f = start["q_pe"] + t
                wait_free(pe, f)
                for k in range(2):
                    ins = mm(bank(f)[:, 0:WC], mqT[:, k, toks(t)], qw[:, k, :, P:P + ROPE], k == 0, k == 1)
                ins.then_inc(full(f), 1)
            for h in range(H):
                f = start["k_nope"] + h
                wait_free(pe, f)
                mm(bank(f), kw[:, h, 0:P], ckvT[:, 0:LS]).then_inc(full(f), 1)
            for g in range(2):
                f = start["k_nope"] + H + g
                wait_free(pe, f)
                for h in range(2):
                    ins = mm(bank(f)[:, h * WC:h * WC + WC], kw[:, 2 * g + h, 0:P], ckvT[:, LS:TOK + P])
                ins.then_inc(full(f), 1)
            for t in range(NT + 1):
                f = start["v_up"] + t
                wait_free(pe, f)
                mm(bank(f), ckvT[:, toks(t)], kw[:, :, P:2 * P]).then_inc(full(f), 1)
            for t in range(NT):
                f = start["tr_qpe"] + t
                if t < TS:
                    pe.wait_ge(qpe_ready, t + 1)
                else:
                    wait_drained(pe, start["q_pe"] + t)
                wait_free(pe, f)
                for h in range(H):
                    ins = nc.tensor.transpose(bank(f)[0:ROPE, h * P:h * P + P], qpe[:, t, h * ROPE:(h + 1) * ROPE], idn)
                ins.then_inc(full(f), 1)

            def scores(u):
                kind, h0 = UNITS[u]
                f = units[u]["s"]

                def product(o, h, q, keys):
                    if h < 4:
                        return mm(o, oq[:, h, q], ok[:, h // 2, keys])
                    mm(o, qnT[:, h - 4, q], knT[:, h - 4, keys], True, False)
                    return mm(o, qpT[0:ROPE, h - 4, q], kpT[0:ROPE, keys], False, True)

                if kind == "sample":
                    wait_free(pe, f)
                    for g in range(4):
                        ins = product(bank(f)[:, g * P:g * P + P], h0, toks(g), toks(NT))
                    ins.then_inc(full(f), 1)
                    for g in range(4):
                        wait_free(pe, f + 1 + g)
                        product(bank(f + 1 + g), h0, toks(g), slice(0, LS)).then_inc(full(f + 1 + g), 1)
                else:
                    wait_free(pe, f)
                    for g in range(4):
                        ins = product(bank(f)[:, g * P:g * P + P], h0 + g, toks(TP), toks(TP))
                    ins.then_inc(full(f), 1)

            def turn_probabilities(u):
                kind, h0 = UNITS[u]
                pe.wait_ge(prob_ready, 4 * u + 4)
                f = units[u]["t"]
                n = 5 if kind == "sample" else 1
                for k in range(n):
                    turn4(f + k, lambda g: prob[u % 2][:, g, k * P:k * P + P])

            def values(u):
                kind, h0 = UNITS[u]
                n = 5 if kind == "sample" else 1
                f = units[u]["p"]
                wait_free(pe, f)
                wait_drained(pe, units[u]["t"] + n - 1)

                def vals(h, t):
                    return v_all[:, t, (h // 2) * P:(h // 2) * P + P] if h < 4 else vm[:, t, (h - 4) * P:(h - 3) * P]

                if kind == "sample":
                    for k in range(5):
                        ins = mm(bank(f), vals(h0, k if k < TS else NT), probT[u % 2][:, k, :], k == 0, k == 4)
                else:
                    for g in range(4):
                        ins = mm(bank(f)[:, g * P:g * P + P], vals(h0 + g, TP), probT[u % 2][:, 0, g * P:g * P + P])
                ins.then_inc(full(f), 1)

            wait_drained(pe, start["tr_qpe"] + NT - 1)
            scores(0)
            scores(1)
            for u in range(len(UNITS)):
                turn_probabilities(u)
                if u + 2 < len(UNITS):
                    scores(u + 2)
                values(u)
                if u in GATE_UNITS:
                    n = GATE_UNITS.index(u)
                    spread_gates(units[u]["g"], (2 * n, 2 * n + 1), diag1, 16 + 8 * (n + 1))
            wait_drained(pe, units[-1]["p"])
            project_out(start["out1"])

        @block.vector
        def _(dve):
            steps = [0]

            def chained(ins):
                steps[0] += 1
                ins.then_inc(dve_step, 1)
                dve.wait_ge(dve_step, steps[0])

            tt, ts, stt = nc.vector.tensor_tensor, nc.vector.tensor_scalar, nc.vector.scalar_tensor_tensor

            def heads(ap):
                return ap.rearrange("p (h c) -> p h c", h=H)

            def mark(ins):
                steps[0] += 1
                ins.then_inc(dve_step, 1)
                return steps[0]

            two_pi = 2.0 * math.pi
            hi = float(np.float32(np.round(two_pi * 1024) / 1024))
            lo = two_pi - hi
            for layer in range(2):
                for n, (c0, c1) in enumerate(((0, LS), (LS, TOK))):
                    f = start["film"] + 2 * layer + n
                    wait_full(dve, f)
                    ts(h2[:, c0:c1], bank(f)[:, 0:c1 - c0], film_w[:, 256 + layer:257 + layer],
                       film_w[:, 258 + layer:259 + layer], ALU.add, ALU.mult).then_inc(free(f), 1)
                    wait_drained(dve, f)
                chained(ts(turns[:, :].bitcast(I32), h2[:, :], 1.0 / two_pi, None, ALU.mult))
                chained(nc.vector.tensor_copy(turns_f[:, :], turns[:, :].bitcast(I32)))
                chained(stt(h2[:, :], turns_f[:, :], -hi, h2[:, :], ALU.mult, ALU.add))
                chained(stt(h2[:, :], turns_f[:, :], -lo, h2[:, :], ALU.mult, ALU.add))
                ts(h2[:, :], h2[:, :], 3.1415925, -3.1415925, ALU.min, ALU.max).then_inc(arg_ready, 1)
            dve.wait_ge(sin_ready, 2)
            nc.vector.memset(h2[64:128, 0:1], 0.0)
            nc.vector.memset(h2[64:128, LS:LS + 1], 0.0).then_inc(h2_ready, 1)
            dve.wait_ge(tap_in, 16 * 7)
            for o in range(2):
                for t in range(NT):
                    f = start[f"filt{o}"] + 2 * t
                    pl = plus[o][:, t, :]
                    for s, taps in enumerate((plus, minus)):
                        wait_full(dve, f + s)
                        ins = tt(taps[o][:, t, :], bank(f + s), window[:, t, :], ALU.mult)
                        ins.then_inc(free(f + s), 1)
                    if t in (0, TP):
                        wait_drained(dve, f)
                        tt(pl[0:1, :], pl[0:1, :], wflat[0:1, 1024 + CH * o:1024 + CH * (o + 1)], ALU.add)\
                            .then_inc(taps_ready, 1)

            def sum_modulation(layer, j):
                i = chunk_of[mod_f[layer][j]]
                wait_chunk(dve, i)
                nth = SUMMED[layer].index(j)
                if nth >= 2:
                    wait_full(dve, mod_f[layer][SUMMED[layer][nth - 2]])
                done = [0, 0]
                for k in range(KD):
                    for n in range(2):
                        o, w, sc = macc[layer][:, nth % 2, n, :], wchunk(i)[:, k, :], scond[:, k, n:n + 1]
                        if k == 0:
                            ins = ts(o, w, sc, None, ALU.mult)
                        else:
                            dve.wait_ge(dve_step, done[n])
                            ins = stt(o, w, sc, o, ALU.mult, ALU.add)
                        if k < KD - 1:
                            steps[0] += 1
                            done[n] = steps[0]
                            ins.then_inc(dve_step, 1)
                        else:
                            ins.then_inc(macc_ready, 1)

            def take_modulation(layer, j):
                f = mod_f[layer][j]
                wait_full(dve, f)
                tt(modc_l[layer][:, 2 * j:2 * j + 2, :], bank(f)[:, 0:4].rearrange("p (m c) -> p m c", m=2),
                   vec1[:, 24 * layer + 2 * j:24 * layer + 2 * j + 2].unsqueeze(2).broadcast_to([P, 2, 2]),
                   ALU.add).then_inc(free(f), 1)

            def modulation_factors(layer, last):
                wait_drained(dve, last)
                stt(acol_l[layer][:, :, :], modc_l[layer][:, 8:16, :], 1.0,
                    vec1[:, 48 + 8 * layer:56 + 8 * layer].unsqueeze(2).broadcast_to([P, KD, 2]),
                    ALU.add, ALU.mult).then_inc(acol_ready, 1)
                tt(gcol_l[layer][:, :, :], modc_l[layer][:, 16:24, :],
                   vec1[:, 64 + 8 * layer:72 + 8 * layer].unsqueeze(2).broadcast_to([P, KD, 2]),
                   ALU.mult).then_inc(acol_ready, 1)

            def take_spectra(fs, p, q, mid=None):
                e_p, o_p, e_q, o_q = fs
                wait_drained(dve, e_p)
                wait_full(dve, o_p)
                p_high = mark(tt(p[:, 1, :], p[:, 0, :], bank(o_p), ALU.subtract))
                wait_drained(dve, e_q)
                wait_full(dve, o_q)
                q_high = mark(tt(q[:, 1, :], bank(o_q), q[:, 0, :], ALU.subtract))
                if mid is not None:
                    ts(mid[0:1, :], bank(o_q)[0:1, :], 0.5, None, ALU.mult)
                dve.wait_ge(dve_step, p_high)
                tt(p[:, 0, :], p[:, 0, :], bank(o_p), ALU.add).then_inc(free(o_p), 1)
                dve.wait_ge(dve_step, q_high)
                tt(q[:, 0, :], q[:, 0, :], bank(o_q), ALU.add).then_inc(free(o_q), 1)

            def pair(tiles, kt):
                return tiles[:, kt:kt + 3:2, :]

            dve.wait_ge(scond_ready, 2)
            for j in range(12):
                if j in SUMMED[0]:
                    sum_modulation(0, j)
                if j in (1, 3, 7, 9):
                    o, kt = j // 6, (j % 6) // 2
                    take_spectra(spec_f[o][4 * kt:4 * kt + 4], pair(specP[o], kt), pair(specQ[o], kt),
                                 mid_sin[o] if kt == 0 else None)
                if j >= 1:
                    take_modulation(0, j - 1)
            take_modulation(0, 11)
            modulation_factors(0, mod_f[0][11])
            nc.vector.memset(pad[:, :, :], 0.0).then_inc(pad_zero, 1)

            def modulate_x(base, layer):
                for t in range(NT):
                    f = base + 2 * t + 1
                    wait_full(dve, f)
                    for k in range(4, KD):
                        c = 0 if t < TS else 1
                        ins = ts(hT[:, k, toks(t)], bank(f)[:, (k - 4) * P:(k - 4) * P + P],
                                 acol_l[layer][:, k, c:c + 1], modc_l[layer][:, k, c:c + 1], ALU.mult, ALU.add)
                    ins.then_inc(free(f), 1)

            dve.wait_ge(acol_ready, 2)
            modulate_x(start["hT0"], 0)

            def convolve(f, width, w0, b0, dst, m0):
                wait_drained(dve, f + 2)
                for m in range(2):
                    o = dst[:, m0 + m, :]
                    for j in range(width):
                        src = pad[:, m, 2 - width // 2 + j:2 - width // 2 + j + CMW]
                        w = vec2[:, w0 + 12 * j + m0 + m:w0 + 12 * j + m0 + m + 1]
                        if j == 0 and b0 is None:
                            chained(ts(o, src, w, None, ALU.mult))
                        elif j == 0:
                            chained(ts(o, src, w, vec2[:, b0 + m0 + m:b0 + m0 + m + 1], ALU.mult, ALU.add))
                        elif j < width - 1:
                            chained(stt(o, src, w, o, ALU.mult, ALU.add))
                        else:
                            stt(o, src, w, o, ALU.mult, ALU.add).then_inc(conv_ready, 1)

            sum_modulation(1, 0)
            for j in range(6):
                if j == 0:
                    sum_modulation(1, 1)
                convolve(hy_f[2 + j], 3, 60 + 4 * (j // 2), 96 + 4 * (j // 2),
                         (cm[:, 0, :, :], cm[:, 1, :, :], hy_x2)[j // 2], 2 * (j % 2))
                take_modulation(1, j)
                if j < 5:
                    sum_modulation(1, j + 2)
            take_modulation(1, 6)
            for n, dst in enumerate((hy_v, hy_x1)):
                for t in range(NT):
                    f = start["tr_hy"] + NT * n + t
                    wait_full(dve, f)
                    nc.vector.tensor_copy(dst[:, t, :], bank(f)).then_inc(free(f), 1)
            wait_drained(dve, spec_f[1][11])
            s0, s1 = pflat[:, 0:512], pflat[:, 512:1024]
            for o in range(2):
                f = start[f"fft{o}"]
                if o == 0:
                    wait_full(dve, start["tr_hy"] + 2 * NT - 1)
                for kt in range(2):
                    p, q = pair(YP, kt), pair(YQ, kt)
                    sp_, sq_ = pair(specP[o], kt), pair(specQ[o], kt)
                    hx = specX[o][:, 0:2, :] if kt == 0 else sp_
                    p_sq = pflat[:, 0:1024].rearrange("p (s n) -> p s n", s=2)
                    q_sq = Ydiff[:, 0:2, :]
                    take_spectra([f, f + 1, f + 2, f + 3], p, q)
                    wait_drained(dve, f + 3)
                    tt(p_sq, p, sq_, ALU.mult)
                    if kt == 0:
                        for n in range(2):
                            tt(mid_rows[0:1, n, :], q[0:1, 1 - n, :], mid_sin[o][0:1, :], ALU.mult)
                    chained(tt(q_sq, q, sq_, ALU.mult))
                    tt(q, q, hx, ALU.mult)
                    chained(tt(p, p, sp_, ALU.mult))
                    tt(p, p, q_sq, ALU.subtract)
                    ins = tt(q, q, p_sq, ALU.add)
                    if kt == 0:
                        chained(ins)
                        tt(q[0:1, 0, :], q[0:1, 0, :], mid_rows[0:1, 0, :], ALU.subtract)
                        ins = tt(q[0:1, 1, :], q[0:1, 1, :], mid_rows[0:1, 1, :], ALU.add)
                    ins.then_inc(Y_ready, 1)
                    dve.wait_ge(Y_ready, 3 * o + kt + 1)
                    f += 4
                chained(tt(Ydiff[:, 0:2, :], YP[:, 0:2, :], YP[:, 2:4, :], ALU.subtract))
                tt(YP[:, 0:2, :], YP[:, 0:2, :], YP[:, 2:4, :], ALU.add).then_inc(Ysum_ready, 1)
                wait_full(dve, f)
                tt(YP[:, TP, :], bank(f), specP[o][:, TP, :], ALU.mult)
                tt(YQ[:, TP, :], bank(f), specQ[o][:, TP, :], ALU.mult).then_inc(free(f), 1)
                wait_full(dve, f + 1)
                tt(s0, bank(f + 1), specQ[o][:, TP, :], ALU.mult)
                tt(s1, bank(f + 1), specX[o][:, 2, :], ALU.mult).then_inc(free(f + 1), 1)
                wait_drained(dve, f + 1)
                tt(YP[:, TP, :], YP[:, TP, :], s0, ALU.subtract)
                tt(YQ[:, TP, :], YQ[:, TP, :], s1, ALU.add).then_inc(Y_ready, 1)
                dve.wait_ge(Y_ready, 3 * o + 3)
                if o == 0:
                    f = start["ab"]
                    wait_full(dve, f)
                    nc.vector.tensor_copy(ab[:, :, :], bank(f)[:, 0:16 * NT].rearrange("p (t c) -> p t c", t=NT))\
                        .then_inc(free(f), 1)
                f = start[f"fft{o}_back"]
                if o == 0:
                    for t in range(NT):
                        wait_full(dve, f)
                        tt(hy_v[:, t, :], bank(f), hy_x1[:, t, :], ALU.mult).then_inc(free(f), 1)
                        f += 1
                else:
                    for m in range(4):
                        wait_full(dve, f)
                        tt(hy_x2[:, m, 0:LS], bank(f), hy_x2[:, m, 0:LS], ALU.mult).then_inc(free(f), 1)
                        wait_drained(dve, f)
                        tt(mix[:, 4 + m, 0:LS], hy_x2[:, m, 0:LS], mix[:, 4 + m, 0:LS], ALU.mult).then_inc(hy_done, 1)
                        f += 1
                    wait_full(dve, f)
                    tt(hy_x2[:, :, CMP:CMP + LP], heads(bank(f)), hy_x2[:, :, CMP:CMP + LP], ALU.mult)\
                        .then_inc(free(f), 1)
                    wait_drained(dve, f)
                    tt(mix[:, 4:8, LS:TOK], hy_x2[:, :, CMP:CMP + LP], mix[:, 4:8, LS:TOK], ALU.mult)\
                        .then_inc(hy_done, 1)

            nc.vector.memset(pad[:, :, :], 0.0).then_inc(pad_zero, 1)
            dve.wait_ge(hy_done, 5)
            chained(tt(gsm[:, T0, :, :], ab[:, :, 0:8], dtb.unsqueeze(1).broadcast_to([P, NT, 8]), ALU.add))
            chained(ts(gsm[:, T1, :, :], gsm[:, T0, :, :], -1.0, None, ALU.mult))
            tt(gsm[:, T1, :, :], gsm[:, T0, :, :], gsm[:, T1, :, :], ALU.min).then_inc(g_chain, 1)
            dve.wait_ge(g_act, 1)
            chained(stt(gsm[:, GE, :, :], gsm[:, T0, :, :], 0.0, gsm[:, T1, :, :], ALU.max, ALU.add))
            stt(gsm[:, GE, :, :], gsm[:, GE, :, :], -1.0, alog.unsqueeze(1).broadcast_to([P, NT, 8]),
                ALU.mult, ALU.mult).then_inc(g_ready, 1)
            chained(ts(gsm[:, BE, :, :], gsm[:, BE, :, :], 1.0, None, ALU.add))
            chained(nc.vector.reciprocal(gsm[:, BE, :, :], gsm[:, BE, :, :]))
            for j in range(6):
                convolve(qkv_f[j], 5, 4 * (j // 2), None,
                         (cm[:, 0, :, :], cm[:, 1, :, :], v_cm)[j // 2], 2 * (j % 2))
                if j >= 1:
                    take_modulation(1, 6 + j)
                if j < 5:
                    sum_modulation(1, 7 + j)
            modulation_factors(1, mod_f[1][11])
            f = start["cumsum"]
            wait_full(dve, f)
            for d in range(2):
                nc.vector.tensor_copy(gsm[:, CS, :, 4 * d:4 * d + 4],
                                      bank(f)[:, 20 * d:20 * d + 20].rearrange("p (t h) -> p t h", t=NT))
            nc.vector.tensor_copy(gsm[:, TOT, :, :], bank(f)[:, 40:80].rearrange("p (t h) -> p t h", t=NT))\
                .then_inc(free(f), 1)
            wait_drained(dve, f)
            tt(gsm[:, KDF, :, :], gsm[:, TOT, :, :], gsm[:, CS, :, :], ALU.subtract).then_inc(scal_ready, 1)
            dve.wait_ge(g_act, 2)
            chained(ts(gsm[:, NEG, :, :], gsm[:, EG, :, :], -1.0, None, ALU.mult))
            for n in range(2):
                for t in range(NT):
                    i = NT * n + t
                    dve.wait_ge(sq2_ready, i + 1)
                    dst = stat[:, 0, 4 * t:4 * t + 4] if n == 0 else gsm[:, T3, t, 0:4]
                    nc.vector.tensor_reduce(dst, heads(pflat[:, (i % 2) * 512:(i % 2) * 512 + 512]), AXX, ALU.add)\
                        .then_inc(ss_ready, 1)
            dve.wait_ge(rinv_ready, 1)
            for t in range(NT):
                tt(heads(q_tm[:, t, :]), heads(q_tm[:, t, :]),
                   stat[:, 1, 4 * t:4 * t + 4].unsqueeze(2).broadcast_to([P, H, P]), ALU.mult).then_inc(normed, 1)
                tt(heads(k_tm[:, t, :]), heads(k_tm[:, t, :]),
                   gsm[:, T3, t, 0:4].unsqueeze(2).broadcast_to([P, H, P]), ALU.mult).then_inc(normed, 1)
            def take_decays(t):
                for d in range(2):
                    f = sum_f[t] + d
                    wait_full(dve, f)
                    if t >= 2:
                        wait_drained(dve, key_f[t - 2])
                    for h in range(H):
                        ins = ts(dec[t % 2][:, d, h * P:h * P + P], bank(f)[:, h * P:h * P + P],
                                 gsm[:, CS, t, 4 * d + h:4 * d + h + 1], 0.0, ALU.subtract, ALU.min)
                    ins.then_inc(free(f), 1)

            def take_keys(t):
                f, made = key_f[t], []
                wait_full(dve, f)
                for d in range(2):
                    dve.wait_ge(masked, 2 * (2 * t + d) + 2)
                    for h in range(H):
                        ins = stt(LT[:, t, d, h * P:h * P + P], bank(f)[:, h * P:h * P + P],
                                  gsm[:, BE, t, 4 * d + h:4 * d + h + 1], dec[t % 2][:, d, h * P:h * P + P],
                                  ALU.mult, ALU.mult)
                    if d == 0:
                        made.append(mark(ins))
                ins.then_inc(free(f), 1)
                wait_full(dve, f + 1)
                for d in range(2):
                    iv = intraT[:, 2 * t + d, :]
                    ins = tt(iv, bank(f + 1), iv, ALU.mult)
                ins.then_inc(free(f + 1), 1)
                for d in range(2):
                    if d == 0:
                        dve.wait_ge(dve_step, made[0])
                    else:
                        wait_drained(dve, f)
                    m0 = levels[:, d * P:d * P + P].unsqueeze(1).broadcast_to([P, H, P])
                    made.append(mark(tt(heads(Uinv[:, 2 * t + d, :]), heads(LT[:, t, d, :]), m0, ALU.mult)))
                for d in range(2):
                    dve.wait_ge(dve_step, made[1 + d])
                    tt(heads(Uinv[:, 2 * t + d, :]), ident[:, :].unsqueeze(1).broadcast_to([P, H, P]),
                       heads(Uinv[:, 2 * t + d, :]), ALU.subtract).then_inc(U1_ready, 1)

            dve.wait_ge(gdn_in, 16)
            for t in GROUPS[0]:
                take_decays(t)
            for t in range(NT):
                f = start["tr_v"] + t
                wait_full(dve, f)
                nc.vector.tensor_copy(v_tm[:, t, :], bank(f)).then_inc(free(f), 1)
            for t in GROUPS[0]:
                take_keys(t)
            for g in inv_groups:
                chains, nch = g["chains"], len(g["chains"])
                for n, (t, d) in enumerate(chains):
                    f = g["T1"] + n
                    wait_full(dve, f)
                    nc.vector.tensor_copy(Tinv[t % 2][:, d, :], bank(f)).then_inc(free(f), 1)
                for l, b in enumerate(LEVELS):
                    fl = g["levels"][l]
                    for n, (t, d) in enumerate(chains):
                        wait_full(dve, fl + n)
                        at = 2 * P + 64 * (len(LEVELS) * d + l)
                        stt(Xl[t % 2][:, d, :].rearrange("p (h c) -> p h c", h=H),
                            bank(fl + n)[:, 0:256].rearrange("p (h c) -> p h c", h=H), -1.0,
                            levels[:, at:at + 64].unsqueeze(1).broadcast_to([P, H, 64]), ALU.mult, ALU.mult)\
                            .then_inc(free(fl + n), 1)
                    for n, (t, d) in enumerate(chains):
                        f = fl + nch + n
                        wait_full(dve, f)
                        Tv = halves(Tinv[t % 2][:, d, :], b)[:, :, :, d, :]
                        tt(Tv, Tv, bank(f)[:, 0:256].rearrange("p (h n b) -> p h n b", h=H, b=b), ALU.add)\
                            .then_inc(free(f), 1)
                    for kind, t in g["prepare"][l]:
                        (take_decays if kind == "sums" else take_keys)(t)
            wait_full(dve, last_tr[-1])
            nc.vector.memset(Sp[:, :, :], 0.0).then_inc(S_ready, 1)
            dve.wait_ge(S_ready, 1)
            dve.wait_ge(gmask_ready, 1)
            def sum_squares(n):
                dve.wait_ge(osq_ready, n + 1)
                st = slice(4 * NORM_ORDER[n], 4 * NORM_ORDER[n] + 4)
                nc.vector.tensor_reduce(stat[:, 0, st], heads(pflat[:, (n % 2) * 512:(n % 2) * 512 + 512]), AXX,
                                        ALU.add).then_inc(oss_ready, 1)

            def norm_heads(n):
                t = NORM_ORDER[n]
                dve.wait_ge(orstd_ready, n + 1)
                tt(heads(o_acc[:, t, :]), heads(o_acc[:, t, :]),
                   stat[:, 1, 4 * t:4 * t + 4].unsqueeze(2).broadcast_to([P, H, P]), ALU.mult).then_inc(on_ready, 1)

            for i, s in enumerate(SCAN):
                if i == 1:
                    dve.wait_ge(state_in, 32)
                fs = start["scan"] + 10 * i
                St = Sp if s == TP else S
                tl = [s, s if s == TP else TS - 1 - s]

                def sc(which, d, h):
                    return gsm[:, which, tl[d], 4 * d + h:4 * d + h + 1]

                for d in range(2):
                    f = fs + d
                    wait_full(dve, f)
                    for h in range(H):
                        ins = stt(rr[:, d, h * P:h * P + P], bank(f)[:, h * P:h * P + P], sc(NEG, d, h),
                                  v_tm[:, tl[d], h * P:h * P + P], ALU.mult, ALU.add)
                    ins.then_inc(free(f), 1)
                for d in range(2):
                    f = fs + 2 + d
                    wait_full(dve, f)
                    for h in range(H):
                        oh = o_acc[:, tl[d], h * P:h * P + P]
                        ins = stt(oh, bank(f)[:, h * P:h * P + P], sc(EG, d, h), oh, ALU.mult, ALU.add)
                    ins.then_inc(free(f), 1)
                    wait_drained(dve, f)
                for d in range(2):
                    f = fs + 4 + d
                    wait_full(dve, f)
                    tt(heads(vn[:, d, :]), heads(bank(f)),
                       gsm[:, BE, tl[d], 4 * d:4 * d + 4].unsqueeze(2).broadcast_to([P, H, P]), ALU.mult)\
                        .then_inc(free(f), 1)
                for d in range(2):
                    f = fs + 6 + d
                    wait_full(dve, f)
                    for h in range(H):
                        Sh = St[:, d, h * P:h * P + P]
                        ins = stt(Sh, Sh, sc(GL, d, h), bank(f)[:, h * P:h * P + P], ALU.mult, ALU.add)
                    ins.then_inc(free(f), 1)
                for d in range(2):
                    f = fs + 8 + d
                    wait_full(dve, f)
                    tt(o_acc[:, tl[d], :], bank(f), o_acc[:, tl[d], :], ALU.add).then_inc(free(f), 1)
                    wait_drained(dve, f)
                if i == 1:
                    sum_squares(0)
                if i == 2:
                    norm_heads(0)
            sum_squares(1)
            for n in range(1, NT):
                if n > 1:
                    norm_heads(n - 1)
                if n + 1 < NT:
                    sum_squares(n + 1)
            norm_heads(NT - 1)
            for n, t in enumerate(NORM_ORDER):
                f = start["tr_o"] + n
                wait_full(dve, f)
                mv = mix[:, 0:4, toks(t)]
                stt(mv, heads(bank(f)), vec1[:, 96:97], mv, ALU.mult, ALU.mult).then_inc(free(f), 1)
            def post_norm(layer, t):
                dve.wait_ge(yrstd_ready, NT * layer + t + 1)
                chained(stt(y[:, t, :], y[:, t, :], yst[:, 1, t:t + 1], gb_l[layer][:, 0 if t < TS else 1, :],
                            ALU.mult, ALU.mult))
                tt(x[:, t, :], x[:, t, :], y[:, t, :], ALU.add).then_inc(x_ready, 1)

            dve.wait_ge(xback_in, 32)
            for t in range(NT + 1):
                if t < NT:
                    post_norm(0, t)
                if t >= 1:
                    dve.wait_ge(rstd_ready, NT + t)
                    ts(xn[:, t - 1, :], x[:, t - 1, :], stat[:, 1, t - 1:t], None, ALU.mult).then_inc(xn_ready, 1)
            dve.wait_ge(acol_ready, 4)
            modulate_x(start["hT1"], 1)
            dve.wait_ge(z_ready, 8 * NT)
            ts(ostat[:, 0, :, 0:7], ostat[:, 0, :, 0:7], 1.0 / P, EPS, ALU.mult, ALU.add)
            ts(ostat[:, 0, :, 7:8], ostat[:, 0, :, 7:8], 1.0 / RQ, EPS, ALU.mult, ALU.add).then_inc(osum_ready, 1)
            dve.wait_ge(oinv_ready, 1)
            dve.wait_ge(odd_in, 160)

            def rotate(v, n, width, cos, sin):
                b = width // 4
                scratch = pflat[:, 0:n * width]

                def split(ap, heads_):
                    return ap.rearrange("p (h a two b) -> p h a two b", h=heads_, a=2, two=2, b=b)

                def table(ap, i):
                    return ap.rearrange("p (a two b) -> p a two b", a=2, two=2, b=b)[:, :, i, :]\
                        .unsqueeze(1).broadcast_to([P, n, 2, b])

                for i in range(2):
                    ins = tt(split(scratch, n)[:, :, :, i, :], split(v, n)[:, :, :, 1 - i, :], table(sin, i), ALU.mult)
                chained(ins)
                vh = v.rearrange("p (h c) -> p h c", h=n)
                chained(tt(vh, vh, cos.unsqueeze(1).broadcast_to([P, n, width]), ALU.mult))
                return tt(v, v, scratch, ALU.add)

            for t in range(NT):
                z = ztm[:, t, :, :].rearrange("p j c -> p (j c)")
                for lo, n, w, i, g in ((0, 4, P, 0, 0), (4 * P, 2, P, 4, 1), (8 * P, 1, P, 6, 2), (6 * P, 1, 2 * P, 7, None)):
                    v = z[:, lo:lo + n * w].rearrange("p (h c) -> p h c", h=n)
                    ins = tt(v, v, ostat[:, 1, t, i:i + n].unsqueeze(2).broadcast_to([P, n, w]), ALU.mult)
                    if g is not None:
                        chained(ins)
                        chained(tt(v, v, g_rows[:, g, :].unsqueeze(1).broadcast_to([P, n, w]), ALU.mult))
                if t < TS:
                    chained(ins)
                    chained(rotate(z[:, 0:4 * P], 4, P, rope[:, t, 0:P], rope[:, t, P:2 * P]))
                    chained(rotate(z[:, 4 * P:6 * P], 2, P, rope[:, t, 0:P], rope[:, t, P:2 * P]))
                    ins = rotate(z[:, 9 * P:9 * P + ROPE], 1, ROPE, rope[:, t, 2 * P:2 * P + ROPE],
                                 rope[:, t, 2 * P + ROPE:2 * P + 2 * ROPE])
                ins.then_inc(onorm_ready, 1)
                dve.wait_ge(onorm_ready, t + 1)
            for t in range(NT):
                f = start["tr_att"] + 3 * t
                wait_full(dve, f)
                nc.vector.tensor_copy(oq[:, :, toks(t)], heads(bank(f))).then_inc(free(f), 1)
            for t in range(TS):
                wait_drained(dve, start["q_pe"] + t)
                rotate(qpe[:, t, :], 4, ROPE, rope[:, t, 2 * P:2 * P + ROPE],
                       rope[:, t, 2 * P + ROPE:2 * P + 2 * ROPE]).then_inc(qpe_ready, 1)
                dve.wait_ge(qpe_ready, t + 1)

            def maxima(u):
                kind, h = UNITS[u]
                scale = (P if h < 4 else P + ROPE) ** -0.5
                f = units[u]["s"]
                if kind == "sample":
                    wait_full(dve, f)
                    chained(nc.vector.tensor_reduce(smax[:, u % 2, 1, :], heads(bank(f)), AXX, ALU.max))
                    for g in range(4):
                        wait_full(dve, f + 1 + g)
                        chained(nc.vector.tensor_reduce(smax[:, u % 2, 0, g:g + 1], bank(f + 1 + g), AXX, ALU.max))
                        ts(nmax[:, u % 2, g:g + 1], smax[:, u % 2, 0, g:g + 1], smax[:, u % 2, 1, g:g + 1], -scale,
                           ALU.max, ALU.mult).then_inc(max_ready, 1)
                else:
                    wait_full(dve, f)
                    chained(nc.vector.tensor_reduce(smax[:, u % 2, 0, :], heads(bank(f)), AXX, ALU.max))
                    ts(nmax[:, u % 2, :], smax[:, u % 2, 0, :], -scale, None, ALU.mult).then_inc(max_ready, 4)

            def normalise(u):
                kind, h = UNITS[u]
                f = units[u]["s"]
                if kind == "sample":
                    wait_drained(dve, f)
                    chained(tt(ssum[:, u % 2, 1, :], ssum[:, u % 2, 0, :], ssum[:, u % 2, 1, :], ALU.add))
                else:
                    wait_drained(dve, f)
                chained(nc.vector.reciprocal(rsum[:, u % 2, :], ssum[:, u % 2, 1, :]))
                width = 640 if kind == "sample" else P
                for g in range(4):
                    ts(prob[u % 2][:, g, 0:width], prob[u % 2][:, g, 0:width], rsum[:, u % 2, g:g + 1], None,
                       ALU.mult).then_inc(prob_ready, 1)

            def gate_output(u):
                kind, h = UNITS[u]
                f = units[u]["p"]
                wait_full(dve, f)
                if kind == "sample":
                    tt(mix[:, h, 0:LS], bank(f), mix[:, h, 0:LS], ALU.mult).then_inc(free(f), 1)
                else:
                    tt(mix[:, h:h + 4, LS:TOK], heads(bank(f)), mix[:, h:h + 4, LS:TOK], ALU.mult).then_inc(free(f), 1)

            dve.wait_ge(cache_out, 1)
            for u in range(2):
                maxima(u)
                normalise(u)
            for u in range(len(UNITS)):
                if u + 2 < len(UNITS):
                    maxima(u + 2)
                    normalise(u + 2)
                gate_output(u)
            for t in range(NT):
                post_norm(1, t)


_INS = ['x_prompt', 'x_sample', 'state_gdn_fwd', 'state_gdn_bwd', 'cache_gqa_k', 'cache_gqa_v', 'cache_mla_ckv',
        'cache_mla_kpe', 'c', 'c_ctx', 'mod_w', 'mod_b', 'pre_norm_g', 'post_norm_g', 'even_in_w', 'gdn_conv_w',
        'gdn_a_log', 'gdn_dt_bias', 'gdn_norm_g', 'hyena_conv_w', 'hyena_conv_b', 'hyena_ffn_w1', 'hyena_ffn_b1',
        'hyena_ffn_w2', 'hyena_ffn_b2', 'hyena_ffn_w3', 'hyena_sin_freq', 'hyena_bias', 'even_out_w', 'odd_in_w',
        'gqa_q_norm_g', 'gqa_k_norm_g', 'mla_q_norm_g', 'mla_q_up', 'mla_kv_norm_g', 'mla_kv_up', 'odd_out_w']
_OUTS = [('y_prompt', (1, LP, D)), ('y_sample', (1, LS, D)), ('new_gdn_fwd', (1, 1, H, P, P)),
         ('new_gdn_bwd', (1, 1, H, P, P)), ('new_gqa_k', (1, 1, LP, 2, P)), ('new_gqa_v', (1, 1, LP, 2, P)),
         ('new_mla_ckv', (1, 1, LP, RKV)), ('new_mla_kpe', (1, 1, LP, ROPE))]


def kernel(**inputs):
    import concourse.bacc as bacc
    from concourse.bass_utils import run_bass_kernel_spmd as run

    nc = bacc.Bacc("TRN2", target_bir_lowering=False, num_devices=1)
    arrays, ins, outs, tables = {}, {}, {}, {}
    for name in _INS:
        v = np.ascontiguousarray(inputs[name])
        arrays[f"in_{name}"] = v
        ins[name] = nc.dram_tensor(f"in_{name}", v.shape, mybir.dt.from_np(v.dtype), kind="ExternalInput").ap()
    for name, v in constants().items():
        arrays[name] = v
        tables[name] = nc.dram_tensor(name, v.shape, F32, kind="ExternalInput").ap()
    for name, shape in _OUTS:
        outs[name] = nc.dram_tensor(f"out_{name}", shape, F32, kind="ExternalOutput").ap()
    program(nc, ins, outs, tables)
    r = run(nc, [arrays], core_ids=[0])
    return tuple(r.results[0][f"out_{name}"] for name, _ in _OUTS)
```
